# Optimizing a Trainium2 kernel written in Bass

```python
import math, functools
import jax, jax.numpy as jnp
from jax import lax
import numpy as np

D_MODEL = 1024
BATCH = 1
SEQ = 1024
DEPTH = 1
DEC_BATCH = 8
DEC_SEQ = 1
PAST_LEN = 256
PAGE_SIZE = 128

N_HEADS = 8
HEAD_DIM = 64
N_KV_HEADS = 2
GROUP = N_HEADS // N_KV_HEADS
BLOCK = 64
N_SELECT = 16
WINDOW = 512
Q_BLOCK = 128
NSA_WIDTH = N_HEADS * HEAD_DIM
KV_WIDTH = 2 * N_KV_HEADS * HEAD_DIM
FORCE_SCORE = 16.0
POOL_WINDOWS = (2, 4, 8, 16)
N_POOL_GROUPS = 4
POOL_WIDTH = 512
POOL_GROUP_DIM = POOL_WIDTH // N_POOL_GROUPS
POOL_HIST = 15
N_BRANCHES = 2
D_FF = 4 * D_MODEL
IN_WIDTH = NSA_WIDTH + 3 * KV_WIDTH + 3 * N_HEADS + POOL_WIDTH + N_BRANCHES * D_MODEL
EPS = 1e-6

kernel_name = "nsa_pool_gated_hybrid_step"

def rms_norm(x, g):
    x32 = x.astype(jnp.float32)
    y = x32 * lax.rsqrt(jnp.mean(x32 * x32, axis=-1, keepdims=True) + EPS)
    return (y * g.astype(jnp.float32)).astype(x.dtype)

def masked_softmax(s, mask):
    s = jnp.where(mask, s.astype(jnp.float32), -jnp.inf)
    m = jnp.max(s, axis=-1, keepdims=True)
    m = jnp.where(jnp.isfinite(m), m, 0.0)
    e = jnp.where(mask, jnp.exp(s - m), 0.0)
    return e / jnp.maximum(jnp.sum(e, axis=-1, keepdims=True), 1e-30)

def adaln(c, w_ada, b_ada):
    m = jnp.einsum('nd,de->ne', jax.nn.silu(c), w_ada) + b_ada
    return tuple(jnp.split(m[:, None, :], 6, axis=-1))

def project_in(h, w_in):
    n, t = h.shape[:2]
    z = jnp.einsum('ntd,de->nte', h, w_in)
    sizes = (NSA_WIDTH, KV_WIDTH, KV_WIDTH, KV_WIDTH, 3 * N_HEADS, POOL_WIDTH, N_BRANCHES * D_MODEL)
    cuts = [sum(sizes[:i + 1]) for i in range(len(sizes) - 1)]
    q, kv_c, kv_s, kv_w, g_nsa, u, g_merge = jnp.split(z, cuts, axis=-1)
    kv_shape = (n, t, 2, N_KV_HEADS, HEAD_DIM)
    return (q.reshape(n, t, N_KV_HEADS, GROUP, HEAD_DIM), kv_c.reshape(kv_shape), kv_s.reshape(kv_shape),
            kv_w.reshape(kv_shape), jax.nn.sigmoid(g_nsa).reshape(n, t, N_KV_HEADS, GROUP, 3), u,
            jax.nn.sigmoid(g_merge))

def compress_blocks(rows, w_cmp, pos_cmp):
    n, l = rows.shape[:2]
    blk = rows.reshape(n, l // BLOCK, BLOCK, 2, N_KV_HEADS, HEAD_DIM) + pos_cmp[:, :, None, :]
    return jnp.einsum('nbjshd,sjde->nbshe', blk, w_cmp)

def nsa_attend(q, q_pos, kv_cmp, kv_sel, kv_win, win_pos, gates):
    scale = HEAD_DIM ** -0.5
    n, t = q.shape[:2]
    nb = kv_cmp.shape[1]
    blk_ids = jnp.arange(nb)
    cur = q_pos // BLOCK
    s_c = jnp.einsum('nthgd,nbhd->nthgb', q, kv_cmp[:, :, 0]) * scale
    c_mask = (blk_ids[None, :] + 1) * BLOCK - 1 <= q_pos[:, None]
    p_c = masked_softmax(s_c, c_mask[None, :, None, None, :])
    o_c = jnp.einsum('nthgb,nbhd->nthgd', p_c.astype(q.dtype), kv_cmp[:, :, 1])
    imp = jnp.sum(p_c, axis=3)
    valid = blk_ids[None, :] <= cur[:, None]
    forced = (blk_ids[None, :] == 0) | (blk_ids[None, :] == cur[:, None]) | (blk_ids[None, :] == cur[:, None] - 1)
    score = jnp.where(valid[None, :, None, :], imp + FORCE_SCORE * forced[None, :, None, :].astype(jnp.float32), -1.0)
    top_val, top_idx = lax.top_k(score, min(N_SELECT, nb))
    n_sel = top_idx.shape[-1]
    n_idx = jnp.arange(n)[:, None, None, None]
    h_idx = jnp.arange(N_KV_HEADS)[None, None, :, None]
    kv_g = kv_sel[n_idx, h_idx, top_idx].reshape(n, t, N_KV_HEADS, n_sel * BLOCK, 2, HEAD_DIM)
    key_pos = (top_idx[..., None] * BLOCK + jnp.arange(BLOCK)).reshape(n, t, N_KV_HEADS, n_sel * BLOCK)
    ok = jnp.broadcast_to((top_val >= 0.0)[..., None], top_idx.shape + (BLOCK,)).reshape(n, t, N_KV_HEADS, n_sel * BLOCK)
    s_mask = ok & (key_pos <= q_pos[None, :, None, None])
    s_s = jnp.einsum('nthgd,nthkd->nthgk', q, kv_g[..., 0, :]) * scale
    p_s = masked_softmax(s_s, s_mask[:, :, :, None, :])
    o_s = jnp.einsum('nthgk,nthkd->nthgd', p_s.astype(q.dtype), kv_g[..., 1, :])
    delta = q_pos[:, None] - win_pos[None, :]
    w_mask = (delta >= 0) & (delta < WINDOW) & (win_pos[None, :] >= 0)
    s_w = jnp.einsum('nthgd,nshd->nthgs', q, kv_win[:, :, 0]) * scale
    p_w = masked_softmax(s_w, w_mask[None, :, None, None, :])
    o_w = jnp.einsum('nthgs,nshd->nthgd', p_w.astype(q.dtype), kv_win[:, :, 1])
    return gates[..., 0:1] * o_c + gates[..., 1:2] * o_s + gates[..., 2:3] * o_w

def nsa_prompt(q, kv_c_rows, kv_s_rows, kv_w_rows, gates, w_cmp, pos_cmp):
    n, s = q.shape[:2]
    kv_c = compress_blocks(kv_c_rows, w_cmp, pos_cmp)
    kv_s = kv_s_rows.reshape(n, s // BLOCK, BLOCK, 2, N_KV_HEADS, HEAD_DIM).transpose(0, 4, 1, 2, 3, 5)
    kv_w_pad = jnp.pad(kv_w_rows, ((0, 0), (WINDOW, 0), (0, 0), (0, 0), (0, 0)))

    def one_block(i):
        q0 = i * Q_BLOCK
        qb = lax.dynamic_slice_in_dim(q, q0, Q_BLOCK, axis=1)
        gb = lax.dynamic_slice_in_dim(gates, q0, Q_BLOCK, axis=1)
        kw = lax.dynamic_slice_in_dim(kv_w_pad, q0, WINDOW + Q_BLOCK, axis=1)
        q_pos = q0 + jnp.arange(Q_BLOCK)
        w_pos = q0 - WINDOW + jnp.arange(WINDOW + Q_BLOCK)
        return nsa_attend(qb, q_pos, kv_c, kv_s, kw, w_pos, gb)

    o = lax.map(one_block, jnp.arange(s // Q_BLOCK))
    o = o.transpose(1, 0, 2, 3, 4, 5).reshape(n, s, NSA_WIDTH)
    return o, (kv_c_rows, kv_s_rows, kv_w_rows[:, -min(WINDOW, s):])

def nsa_sample(q, kv_c_new, kv_s_new, kv_w_new, gates, cache_cmp_kv, cache_sel_kv, page_table, state_win_kv, w_cmp, pos_cmp):
    n, t = q.shape[:2]
    total = PAST_LEN + t
    nb = -(-total // BLOCK)
    pad = nb * BLOCK - total

    def full_rows(cache, new):
        past = cache[page_table].reshape(n, PAST_LEN, 2, N_KV_HEADS, HEAD_DIM)
        rows = jnp.concatenate([past, new], axis=1)
        return jnp.pad(rows, ((0, 0), (0, pad), (0, 0), (0, 0), (0, 0)))

    kv_c = compress_blocks(full_rows(cache_cmp_kv, kv_c_new), w_cmp, pos_cmp)
    kv_s = full_rows(cache_sel_kv, kv_s_new).reshape(n, nb, BLOCK, 2, N_KV_HEADS, HEAD_DIM).transpose(0, 4, 1, 2, 3, 5)
    win_buf = state_win_kv.shape[1]
    kw = jnp.concatenate([state_win_kv, kv_w_new], axis=1)
    q_pos = PAST_LEN + jnp.arange(t)
    w_pos = PAST_LEN - win_buf + jnp.arange(win_buf + t)
    o = nsa_attend(q, q_pos, kv_c, kv_s, kw, w_pos, gates)
    return o.reshape(n, t, NSA_WIDTH), (kv_c_new, kv_s_new, kw[:, t:])

def pool_mix(u, hist, first_pos, w_pool, pool_scale):
    n, t = u.shape[:2]
    ext = jnp.concatenate([hist, u], axis=1).astype(jnp.float32)
    cs = jnp.pad(jnp.cumsum(ext, axis=1), ((0, 0), (1, 0), (0, 0)))
    pos = first_pos + jnp.arange(t)
    end = cs[:, POOL_HIST + 1:]
    groups = []
    for gi, w in enumerate(POOL_WINDOWS):
        sl = slice(gi * POOL_GROUP_DIM, (gi + 1) * POOL_GROUP_DIM)
        start = cs[:, POOL_HIST + 1 - w: POOL_HIST + 1 - w + t, sl]
        cnt = jnp.minimum(pos + 1, w).astype(jnp.float32)[None, :, None]
        groups.append((end[..., sl] - start) / cnt)
    pooled = jnp.concatenate(groups, axis=-1).astype(u.dtype) - u
    pg = pooled.reshape(n, t, N_POOL_GROUPS, POOL_GROUP_DIM)
    mixed = jnp.einsum('ntgc,gcd->ntgd', pg, w_pool).reshape(n, t, POOL_WIDTH)
    return mixed * pool_scale

def run_layer(x, ada, layer_w, nsa_fn, pool_hist, first_pos):
    (g_pre_mix, g_post_mix, g_pre_mlp, g_post_mlp, w_in, w_pool, pool_scale,
     w_up_nsa, w_up_pool, w_o, w_ff1, w_ff2) = layer_w
    shift1, scale1, gate1, shift2, scale2, gate2 = ada
    h = rms_norm(x, g_pre_mix) * (1.0 + scale1) + shift1
    q, kv_c, kv_s, kv_w, g_nsa, u, g_merge = project_in(h, w_in)
    o_nsa, nsa_state = nsa_fn(q, kv_c, kv_s, kv_w, g_nsa)
    o_pool = pool_mix(u, pool_hist, first_pos, w_pool, pool_scale)
    new_pool = jnp.concatenate([pool_hist, u], axis=1)[:, -POOL_HIST:]
    g_a, g_b = jnp.split(g_merge, 2, axis=-1)
    m = g_a * jnp.einsum('ntc,cd->ntd', o_nsa, w_up_nsa) + g_b * jnp.einsum('ntc,cd->ntd', o_pool, w_up_pool)
    m = jnp.einsum('ntd,de->nte', m, w_o)
    x = x + gate1 * rms_norm(m, g_post_mix)
    h = rms_norm(x, g_pre_mlp) * (1.0 + scale2) + shift2
    f = jnp.einsum('ntf,fd->ntd', jnp.square(jax.nn.relu(jnp.einsum('ntd,df->ntf', h, w_ff1))), w_ff2)
    x = x + gate2 * rms_norm(f, g_post_mlp)
    return x, nsa_state + (new_pool,)

def setup_inputs(seed: int = 0) -> dict:
    key = jax.random.key(seed)
    ks = jax.random.split(key, 32)
    n_pages = PAST_LEN // PAGE_SIZE
    n_used = DEC_BATCH * n_pages
    n_phys = n_used + (n_used + 3) // 4
    win_buf = min(WINDOW, PAST_LEN)

    def nrm(k, shape, s):
        return jax.random.normal(k, shape, jnp.float32) * s

    page_table = jax.random.permutation(ks[0], n_phys)[:n_used].reshape(DEC_BATCH, n_pages).astype(jnp.int32)
    kv_page_shape = (DEPTH, n_phys, PAGE_SIZE, 2, N_KV_HEADS, HEAD_DIM)
    return {
        "x_prompt": nrm(ks[1], (BATCH, SEQ, D_MODEL), 1.0),
        "x_sample": nrm(ks[2], (DEC_BATCH, DEC_SEQ, D_MODEL), 1.0),
        "cache_cmp_kv": nrm(ks[3], kv_page_shape, 1.0),
        "cache_sel_kv": nrm(ks[4], kv_page_shape, 1.0),
        "state_win_kv": nrm(ks[5], (DEPTH, DEC_BATCH, win_buf, 2, N_KV_HEADS, HEAD_DIM), 1.0),
        "state_pool": nrm(ks[6], (DEPTH, DEC_BATCH, POOL_HIST, POOL_WIDTH), 1.0),
        "page_table": page_table,
        "c_prompt": nrm(ks[7], (BATCH, D_MODEL), 1.0),
        "c_sample": nrm(ks[8], (DEC_BATCH, D_MODEL), 1.0),
        "w_ada": nrm(ks[9], (DEPTH, D_MODEL, 6 * D_MODEL), D_MODEL ** -0.5),
        "b_ada": nrm(ks[10], (DEPTH, 6 * D_MODEL), 0.02),
        "g_pre_mix": 1.0 + nrm(ks[11], (DEPTH, D_MODEL), 0.05),
        "g_post_mix": 1.0 + nrm(ks[12], (DEPTH, D_MODEL), 0.05),
        "g_pre_mlp": 1.0 + nrm(ks[13], (DEPTH, D_MODEL), 0.05),
        "g_post_mlp": 1.0 + nrm(ks[14], (DEPTH, D_MODEL), 0.05),
        "w_in": nrm(ks[15], (DEPTH, D_MODEL, IN_WIDTH), D_MODEL ** -0.5),
        "w_cmp": nrm(ks[16], (DEPTH, 2, BLOCK, HEAD_DIM, HEAD_DIM), (BLOCK * HEAD_DIM) ** -0.5),
        "pos_cmp": nrm(ks[17], (DEPTH, BLOCK, 2, HEAD_DIM), 0.1),
        "w_pool": nrm(ks[18], (DEPTH, N_POOL_GROUPS, POOL_GROUP_DIM, POOL_GROUP_DIM), POOL_GROUP_DIM ** -0.5),
        "pool_scale": 1.0 + nrm(ks[19], (DEPTH, POOL_WIDTH), 0.1),
        "w_up_nsa": nrm(ks[20], (DEPTH, NSA_WIDTH, D_MODEL), NSA_WIDTH ** -0.5),
        "w_up_pool": nrm(ks[21], (DEPTH, POOL_WIDTH, D_MODEL), POOL_WIDTH ** -0.5),
        "w_o": nrm(ks[22], (DEPTH, D_MODEL, D_MODEL), D_MODEL ** -0.5),
        "w_ff1": nrm(ks[23], (DEPTH, D_MODEL, D_FF), D_MODEL ** -0.5),
        "w_ff2": nrm(ks[24], (DEPTH, D_FF, D_MODEL), D_FF ** -0.5),
    }

def reference(x_prompt, x_sample, cache_cmp_kv, cache_sel_kv, state_win_kv, state_pool, page_table,
              c_prompt, c_sample, w_ada, b_ada, g_pre_mix, g_post_mix, g_pre_mlp, g_post_mlp, w_in,
              w_cmp, pos_cmp, w_pool, pool_scale, w_up_nsa, w_up_pool, w_o, w_ff1, w_ff2):
    yp, ys = x_prompt, x_sample
    outs = [[] for _ in range(8)]
    for l in range(DEPTH):
        layer_w = (g_pre_mix[l], g_post_mix[l], g_pre_mlp[l], g_post_mlp[l], w_in[l], w_pool[l], pool_scale[l],
                   w_up_nsa[l], w_up_pool[l], w_o[l], w_ff1[l], w_ff2[l])
        ada_p = adaln(c_prompt, w_ada[l], b_ada[l])
        ada_s = adaln(c_sample, w_ada[l], b_ada[l])
        nsa_p = functools.partial(nsa_prompt, w_cmp=w_cmp[l], pos_cmp=pos_cmp[l])
        nsa_s = functools.partial(nsa_sample, cache_cmp_kv=cache_cmp_kv[l], cache_sel_kv=cache_sel_kv[l],
                                  page_table=page_table, state_win_kv=state_win_kv[l],
                                  w_cmp=w_cmp[l], pos_cmp=pos_cmp[l])
        hist_p = jnp.zeros((yp.shape[0], POOL_HIST, POOL_WIDTH), yp.dtype)
        yp, st_p = run_layer(yp, ada_p, layer_w, nsa_p, hist_p, 0)
        ys, st_s = run_layer(ys, ada_s, layer_w, nsa_s, state_pool[l], PAST_LEN)
        for i, a in enumerate(st_p + st_s):
            outs[i].append(a)
    new_cmp_kv_prompt = jnp.stack(outs[0], 0)
    new_sel_kv_prompt = jnp.stack(outs[1], 0)
    new_win_kv_prompt = jnp.stack(outs[2], 0)
    new_pool_prompt = jnp.stack(outs[3], 0)
    new_cmp_kv_sample = jnp.stack(outs[4], 0)
    new_sel_kv_sample = jnp.stack(outs[5], 0)
    new_win_kv_sample = jnp.stack(outs[6], 0)
    new_pool_sample = jnp.stack(outs[7], 0)
    return (yp, ys, new_cmp_kv_prompt, new_sel_kv_prompt, new_win_kv_prompt, new_pool_prompt,
            new_cmp_kv_sample, new_sel_kv_sample, new_win_kv_sample, new_pool_sample)


_drawn_inputs = setup_inputs


def setup_inputs(seed=0):
    import zlib

    import numpy as np

    out = dict(_drawn_inputs(seed))
    spreads = {}
    factors = {}
    for name, (base, spread) in spreads.items():
        noise = np.random.default_rng([zlib.crc32(name.encode()), seed]).standard_normal(out[name].shape)
        drawn = base * np.exp(spread * noise) if base else spread * noise
        out[name] = __import__('jax').numpy.asarray(drawn.astype(out[name].dtype))
    for name, factor in factors.items():
        out[name] = (out[name] * factor).astype(out[name].dtype)
    return out
```

```python
from contextlib import ExitStack

import concourse.bass as bass
from concourse import mybir

F32 = mybir.dt.float32
F32R = mybir.dt.float32r
BF16 = mybir.dt.bfloat16
I32 = mybir.dt.int32
ACT = mybir.ActivationFunctionType
ALU = mybir.AluOpType
AX = mybir.AxisListType

P = 128
D = 1024
KD = D // P
TP = 1024
NS = 8
T = TP + NS
NB = TP // P
NCH = 3
CH = T // NCH
HEADS, KVH, GRP, HD = 8, 2, 4, 64
BLOCK = 64
WINDOW = 512
WB = WINDOW // P
PAST = 256
PAGE = 128
NPG = PAST // PAGE
NPHYS = 20
NCB = TP // BLOCK
NDB = PAST // BLOCK
NCAT = NCB + NS * NDB + 1
Q_COL, KV_COL, G_COL, U_COL, M_COL = 0, 512, 1280, 1304, 1816
PW = 512
HIST = 15
FF = 4096
NFG = FF // D
EPS = 1e-6
SCALE = HD ** -0.5
MASKED = -1e30
MAX_FLOOR = -1e20
R = NS * HEADS
VB_ADA, VG_PRE_MIX, VG_POST_MIX, VG_PRE_MLP, VG_POST_MLP, V_POOL, NVEC = 0, 48, 56, 64, 72, 80, 84


def newton(dve, chain, y, v, t):
    chain.then_wait(dve.scalar_tensor_tensor(t, y, -0.5, y, ALU.mult, ALU.mult))
    chain.then_wait(dve.tensor_tensor(t, t, v, ALU.mult))
    chain.then_wait(dve.scalar_tensor_tensor(y, t, 1.5, y, ALU.add, ALU.mult))


class Chain:

    def __init__(self, eng, sem):
        self.eng, self.sem, self.n = eng, sem, 0

    def then_wait(self, ins):
        self.n += 1
        ins.then_inc(self.sem, 1)
        self.eng.wait_ge(self.sem, self.n)


class Buffers:

    SLAB = KD * T * 4
    CONSTS = 7424

    def __init__(self, nc):
        self.nc = nc
        self.base = (nc.sbuf_base + 31) // 32 * 32
        self.end = nc.sbuf_usable_end
        self.consts = 0
        self.tail = self.CONSTS + 6 * self.SLAB

    def at(self, name, shape, dt, offset):
        size = 2 if dt == BF16 else 4
        for n in shape[1:]:
            size *= n
        assert self.base + offset + size <= self.end, (name, self.base + offset + size - self.end)
        return self.nc.alloc_sbuf_tensor_at(name, shape, dt, offset=self.base + offset), offset + (size + 31) // 32 * 32

    def const(self, name, shape, dt=F32):
        t, self.consts = self.at(name, shape, dt, self.consts)
        assert self.consts <= self.CONSTS, self.consts
        return t

    def small(self, name, shape, dt=F32):
        t, self.tail = self.at(name, shape, dt, self.tail)
        return t

    def slabs(self, first, start=0):
        at = [self.CONSTS + first * self.SLAB + start]

        def place(name, shape, dt=F32):
            t, at[0] = self.at(name, shape, dt, at[0])
            return t

        place.at = at
        return place


class Semaphores:

    def __init__(self, nc):
        self.nc, self.used = nc, []

    def __call__(self, name):
        self.used.append(self.nc.alloc_semaphore(name=name))
        return self.used[-1]

    def recycle(self):
        self.nc.clear_and_free_semaphores(self.used)
        self.nc.all_engine_barrier()
        self.used = []


class Weights:

    def __init__(self, place):
        self.raw = place("w_raw", [P, 2, KD, P])
        self.hi = place("w_hi", [P, 2, KD, P], F32R)
        self.lo = place("w_lo", [P, 2, KD, P], F32R)


class Gemm:

    def __init__(self, w, accs, sem, name, parts=1):
        self.w, self.accs, self.parts = w, accs, parts
        self.loaded = [sem(f"{name}_w_loaded{s}") for s in range(2)]
        self.hi_ready = sem(f"{name}_w_hi_ready")
        self.lo_ready = sem(f"{name}_w_lo_ready")
        self.done = sem(f"{name}_products_done")
        self.freed = [sem(f"{name}_acc_freed{s}") for s in range(2)]

    def load(self, sp, src, j, s, first=False):
        if not first:
            sp.wait_ge(self.lo_ready, j * 2 + (s - 1))
        if self.parts == 1:
            sp.dma_start(self.w.raw[:, s, 0:src.shape[1]], src).then_inc(self.loaded[s], 16)
        else:
            for h in range(2):
                sp.dma_start(self.w.raw[:, s, :, h * HD:(h + 1) * HD], src[h]).then_inc(self.loaded[s], 16)

    def cut_hi(self, act, j, s, first=False, k=KD):
        act.wait_ge(self.loaded[s], (j * 16 + 16) * self.parts)
        if not first:
            act.wait_ge(self.done, j * 2 + (s - 1))
        act.activation(self.w.hi[:, s, 0:k], self.w.raw[:, s, 0:k], ACT.Copy).then_inc(self.hi_ready, 1)

    def cut_lo(self, pool, j, s, k=KD):
        pool.wait_ge(self.hi_ready, j * 2 + (s + 1))
        pool.tensor_tensor(self.w.lo[:, s, 0:k], self.w.raw[:, s, 0:k], self.w.hi[:, s, 0:k].bitcast(F32),
                           ALU.subtract).then_inc(self.lo_ready, 1)

    def multiply(self, pe, j, s, x_hi, x_lo, first=False, k=KD, before_last=None):
        pe.wait_ge(self.lo_ready, j * 2 + (s + 1))
        if not first:
            pe.wait_ge(self.freed[s], j * 1)
        for kk in range(k):
            if before_last is not None and kk == k - 1:
                before_last()
            for n, (w, x) in enumerate(((self.w.hi, x_hi), (self.w.hi, x_lo), (self.w.lo, x_hi))):
                for c in range(NCH):
                    last = pe.matmul(self.accs[s][:, c, 0:CH], w[:, s, kk], x[:, kk, c * CH:(c + 1) * CH],
                                     start=(kk == 0 and n == 0), stop=(kk == k - 1 and n == 2))
        last.then_inc(self.done, 1)

    def out(self, s):
        return self.accs[s][:, :, 0:CH]


def by_chunk(x):
    return x.rearrange("p (c t) -> p c t", c=NCH)


def columns(w, n):
    return w.rearrange("(k p) n -> p k n", p=P)[:, :, bass.ds(n, P)]



def cut_plain(nc, sem, name, tiles):
    hi_ready, lo_ready = sem(f"{name}_cut_hi"), sem(f"{name}_cut_lo")
    with nc.Block() as block:

        @block.scalar
        def _(act):
            for x, hi, _ in tiles:
                act.activation(hi, x, ACT.Copy).then_inc(hi_ready, 1)

        def lows(eng, mine):
            for n, (x, hi, lo) in enumerate(tiles):
                if n % 3 in mine:
                    eng.wait_ge(hi_ready, n + 1)
                    eng.tensor_tensor(lo, x, hi.bitcast(F32), ALU.subtract).then_inc(lo_ready, 1)

        @block.vector
        def _(dve):
            lows(dve, (0, 1))

        @block.gpsimd
        def _(pool):
            lows(pool, (2,))


def cut_in_place(nc, sem, name, tiles, tmp):
    tmp_ready, lo_ready = sem(f"{name}_tmp_ready"), sem(f"{name}_lo_ready")
    ring = tmp.shape[1]
    with nc.Block() as block:

        @block.scalar
        def _(act):
            for n, (x, _, _) in enumerate(tiles):
                if n >= ring:
                    act.wait_ge(lo_ready, n - ring + 1)
                act.activation(tmp[:, n % ring], x, ACT.Copy).then_inc(tmp_ready, 1)
            for n, (x, hi, _) in enumerate(tiles):
                act.wait_ge(lo_ready, n + 1)
                act.activation(hi, x, ACT.Copy)

        @block.vector
        def _(dve):
            for n, (x, _, lo) in enumerate(tiles):
                dve.wait_ge(tmp_ready, n + 1)
                dve.tensor_tensor(lo, x, tmp[:, n % ring].bitcast(F32), ALU.subtract).then_inc(lo_ready, 1)


def dense(nc, psum, sem, w, name, weights, x_hi, x_lo, out):
    with ExitStack() as st:
        accs = [psum(st, f"{name}_acc{s}", [P, NCH, 512]) for s in range(2)]
        g = Gemm(w, accs, sem, name)
        pairs = KD // 2
        with nc.Block() as block:

            @block.sync
            def _(sp):
                for s in range(2):
                    g.load(sp, columns(weights, s * P), 0, s, first=True)
                with sp.Fori(1, pairs) as j:
                    for s in range(2):
                        g.load(sp, columns(weights, (2 * j + s) * P), j, s)

            @block.scalar
            def _(act):
                for s in range(2):
                    g.cut_hi(act, 0, s, first=True)
                with act.Fori(1, pairs) as j:
                    for s in range(2):
                        g.cut_hi(act, j, s)

            @block.gpsimd
            def _(pool):
                with pool.Fori(0, pairs) as j:
                    for s in range(2):
                        g.cut_lo(pool, j, s)

            @block.tensor
            def _(pe):
                for s in range(2):
                    g.multiply(pe, 0, s, x_hi, x_lo, first=True)
                with pe.Fori(1, pairs) as j:
                    for s in range(2):
                        g.multiply(pe, j, s, x_hi, x_lo)

            @block.vector
            def _(dve):
                with dve.Fori(0, pairs) as j:
                    for s in range(2):
                        dve.wait_ge(g.done, j * 2 + (s + 1))
                        o = out[:, bass.ds(j * 2 + s, 1)].rearrange("p o t -> p (o t)")
                        dve.tensor_copy(by_chunk(o), g.out(s)).then_inc(g.freed[s], 1)


def feature_norm(nc, psum, sem, name, x, sqr, ones, rstd, mean, tmp):
    squared, summed, mean_ready, root_ready, nchain = (sem(f"{name}_{n}") for n in ("squared", "summed", "mean", "root", "chain"))
    with ExitStack() as st:
        acc = psum(st, f"{name}_ps", [P, NCH, 512])
        with nc.Block() as block:

            @block.scalar
            def _(act):
                for k in range(KD):
                    if k >= 2:
                        act.wait_ge(summed, k - 1)
                    act.activation(sqr[:, k % 2], x[:, k], ACT.Square).then_inc(squared, 1)
                act.wait_ge(mean_ready, 1)
                act.activation(rstd[:], mean[:], ACT.Sqrt).then_inc(root_ready, 1)

            @block.tensor
            def _(pe):
                for k in range(KD):
                    pe.wait_ge(squared, k + 1)
                    for c in range(NCH):
                        last = pe.matmul(acc[:, c, 0:CH], ones[:], sqr[:, k % 2, c * CH:(c + 1) * CH], start=(k == 0), stop=(k == KD - 1))
                    last.then_inc(summed, 1)

            @block.vector
            def _(dve):
                chain = Chain(dve, nchain)
                dve.wait_ge(summed, KD)
                dve.tensor_scalar(by_chunk(mean[:]), acc[:, :, 0:CH], 1.0 / D, EPS, ALU.mult, ALU.add).then_inc(mean_ready, 1)
                dve.wait_ge(root_ready, 1)
                chain.then_wait(dve.reciprocal(rstd[:], rstd[:]))
                newton(dve, chain, rstd[:], mean[:], tmp[:])


def add_gated(nc, sem, name, x, y, rstd, gate, term):
    scaled, used, chain0 = sem(f"{name}_scaled"), sem(f"{name}_used"), sem(f"{name}_chain")
    with nc.Block() as block:

        @block.gpsimd
        def _(pool):
            for k in range(KD):
                if k >= 2:
                    pool.wait_ge(used, k - 1)
                pool.tensor_tensor(term[:, k % 2], y[:, k], rstd[:], ALU.mult).then_inc(scaled, 1)

        @block.vector
        def _(dve):
            chain = Chain(dve, chain0)
            for k in range(KD):
                dve.wait_ge(scaled, k + 1)
                t = term[:, k % 2]
                chain.then_wait(dve.tensor_tensor(t[:, TP:T], t[:, TP:T], gate[:, k, 1:], ALU.mult))
                dve.tensor_tensor(x[:, k, TP:T], x[:, k, TP:T], t[:, TP:T], ALU.add)
                dve.scalar_tensor_tensor(x[:, k, 0:TP], t[:, 0:TP], gate[:, k, 0:1], x[:, k, 0:TP], ALU.mult, ALU.add).then_inc(used, 1)


def hybrid_step(nc, x_prompt, x_sample, cache_cmp_kv, cache_sel_kv, state_win_kv, state_pool, page_table,
                c_prompt, c_sample, w_ada, b_ada, g_pre_mix, g_post_mix, g_pre_mlp, g_post_mlp, w_in,
                w_cmp, pos_cmp, w_pool, pool_scale, w_up_nsa, w_up_pool, w_o, w_ff1, w_ff2,
                y_prompt, y_sample, n_cmp_p, n_sel_p, n_win_p, n_pool_p, n_cmp_s, n_sel_s, n_win_s, n_pool_s):
    with ExitStack() as root:
        sem = Semaphores(nc)
        buf = Buffers(nc)

        def psum(st, name, shape):
            return st.enter_context(nc.psum_tensor(name, shape, F32))

        ident = buf.const("ident", [P, P])
        identb = buf.const("identb", [P, P], BF16)
        ones = buf.const("ones", [P, P])
        causal = buf.const("causal", [P, P], BF16)
        behind = buf.const("behind", [P, P], BF16)
        cmask = buf.const("cmask", [P, NB, NCB], BF16)
        dmask = buf.const("dmask", [R, NS], BF16)
        dcmask = buf.const("dcmask", [R, NS, NDB], BF16)
        invcnt = buf.const("invcnt", [P, 4, 16])
        vecs = buf.const("vecs", [P, NVEC])
        sc1, gt1, sc2, gt2 = (buf.const(n, [P, KD, 1 + NS]) for n in ("sc1", "gt1", "sc2", "gt2"))
        ada = buf.const("ada", [P, 6 * KD, 1 + NS])
        gtok = buf.const("gtok", [P, NB, 24])
        gdec8 = buf.const("gdec8", [NS, 24])
        gdec = buf.const("gdec", [R, 3])
        x1_spill = nc.dram_tensor("x1_spill", [P, KD, T], F32, kind="Internal").ap()
        w = Weights(buf.slabs(5))

        h_hi = buf.slabs(0)("h_hi", [P, KD, T], F32R)
        h_lo = buf.slabs(1)("h_lo", [P, KD, T], F32R)

        with ExitStack() as st:
            at = buf.slabs(2)
            xt = at("xt", [P, NB + 1, D])
            NR = 3
            wa = at("wa", [P, NR, KD, 512])
            NA = 6 * D // 512
            htmp = at("htmp", [P, 2, 512])
            sq = at("sq", [P, D])
            vrow = at("vrow", [NVEC, P])
            crow = at("crow", [1 + NS, D])
            csig = at("csig", [1 + NS, D])
            cT = at("cT", [P, KD, 1 + NS])
            ss, ms, rs, rt = (at(n, [P, NB + 1]) for n in ("ss", "ms", "rs", "rt"))
            iot = at("iot", [P, 16])
            tp = [psum(st, f"tp{i}", [P, 512]) for i in range(3)]
            adaP = psum(st, "adaP", [P, 6 * KD, 1 + NS])
            vec_loaded, c_loaded, x_loaded, xs_loaded = sem("vec_loaded"), sem("c_loaded"), sem("x_loaded"), sem("xs_loaded")
            wa_loaded = [sem(f"wa_loaded{r}") for r in range(NR)]
            zeroed, consts_ready, pool_chain = sem("zeroed"), sem("consts_ready"), sem("pool_chain0")
            csig_ready, silu_ready, cT_done, cT_ready = sem("csig_ready"), sem("silu_ready"), sem("cT_done"), sem("cT_ready")
            vT_done, ada_done, ada_ready = sem("vT_done"), sem("ada_done"), sem("ada_ready")
            squares_ready, ms_ready, root_ready, x_scaled = sem("squares_ready"), sem("ms_ready"), sem("root_ready"), sem("x_scaled")
            xT_done, h_ready, hhi_ready, hlo_ready = sem("xT_done0"), sem("h_ready"), sem("hhi_ready"), sem("hlo_ready")
            dve_chain, act_chain = sem("dve_chain0"), sem("act_chain0")
            with nc.Block() as block:

                @block.sync
                def _(sp):
                    sp.dma_start(crow[0:1, :], c_prompt).then_inc(c_loaded, 16)
                    sp.dma_start(crow[1:1 + NS, :], c_sample).then_inc(c_loaded, 16)
                    for at_row, v in ((VB_ADA, b_ada), (VG_PRE_MIX, g_pre_mix), (VG_POST_MIX, g_post_mix),
                                      (VG_PRE_MLP, g_pre_mlp), (VG_POST_MLP, g_post_mlp), (V_POOL, pool_scale)):
                        v = v[0].rearrange("(r p) -> r p", p=P)
                        sp.dma_start(vrow[at_row:at_row + v.shape[0], :], v).then_inc(vec_loaded, 16)
                    for c in range(NA):
                        if c >= NR:
                            sp.wait_ge(ada_done, c - NR + 1)
                        sp.dma_start(wa[:, c % NR], w_ada[0].rearrange("(k p) n -> p k n", p=P)[:, :, c * 512:(c + 1) * 512])\
                            .then_inc(wa_loaded[c % NR], 16)

                @block.scalar
                def _(act):
                    act.dma_start(xt[:, 0:NB], x_prompt[0].rearrange("(b p) d -> p b d", p=P)).then_inc(x_loaded, 16)
                    act.dma_start(xt[0:NS, NB], x_sample[:, 0, :]).then_inc(xs_loaded, 16)
                    act.wait_ge(c_loaded, 32)
                    act.activation(csig[:], crow[:], ACT.Sigmoid).then_inc(csig_ready, 1)
                    act.wait_ge(zeroed, 1)
                    act.wait_ge(x_loaded, 16)
                    chain = Chain(act, act_chain)
                    for b in range(NB):
                        chain.then_wait(act.activation(sq[:], xt[:, b], ACT.Square, accum_out=ss[:, b:b + 1]))
                    act.wait_ge(xs_loaded, 16)
                    act.activation(sq[0:NS], xt[0:NS, NB], ACT.Square, accum_out=ss[0:NS, NB:NB + 1]).then_inc(squares_ready, 1)
                    act.wait_ge(ms_ready, 1)
                    act.activation(rt[:], ms[:], ACT.Sqrt).then_inc(root_ready, 1)
                    for e in range(2 * KD):
                        act.wait_ge(h_ready, e + 1)
                        hf, k = divmod(e, KD)
                        act.activation(h_hi[:, k, hf * 512:(hf + 1) * 512], htmp[:, e % 2], ACT.Copy).then_inc(hhi_ready, 1)
                    act.wait_ge(h_ready, 2 * KD + 1)
                    act.activation(h_hi[:, :, TP:T], htmp[:, 0, 0:KD * NS].rearrange("p (k n) -> p k n", k=KD),
                                   ACT.Copy).then_inc(hhi_ready, 1)

                @block.gpsimd
                def _(pool):
                    chain = Chain(pool, pool_chain)
                    pool.memset(ss[:], 1.0).then_inc(zeroed, 1)
                    pool.memset(ident[:], 0.0)
                    pool.memset(ones[:], 1.0)
                    for m in (causal, behind, cmask, dmask):
                        pool.memset(m[:], 0.0)
                    chain.then_wait(pool.memset(dcmask[:], 0.0))
                    pool.affine_select(out=ident[:], in_=ident[:], compare_op=ALU.not_equal, fill=1.0, base=0,
                                       pattern=[[-1, P]], channel_multiplier=1)
                    pool.affine_select(out=causal[:], in_=causal[:], compare_op=ALU.is_ge, fill=MASKED, base=0,
                                       pattern=[[-1, P]], channel_multiplier=1)
                    pool.affine_select(out=behind[:], in_=behind[:], compare_op=ALU.is_gt, fill=MASKED, base=0,
                                       pattern=[[1, P]], channel_multiplier=-1)
                    pool.affine_select(out=cmask[:], in_=cmask[:], compare_op=ALU.is_ge, fill=MASKED, base=-(BLOCK - 1),
                                       pattern=[[P, NB], [-BLOCK, NCB]], channel_multiplier=1)
                    pool.affine_select(out=dmask[:], in_=dmask[:], compare_op=ALU.is_ge, fill=MASKED, base=0,
                                       pattern=[[-HEADS, NS]], channel_multiplier=1)
                    chain.then_wait(pool.affine_select(out=dcmask[:], in_=dcmask[:], compare_op=ALU.is_ge, fill=MASKED,
                                    base=0, pattern=[[-HEADS, NS], [0, NDB]], channel_multiplier=1))
                    pool.affine_select(out=dmask[:], in_=dmask[:], compare_op=ALU.is_ge, fill=MASKED, base=HEADS - 1,
                                       pattern=[[HEADS, NS]], channel_multiplier=-1)
                    pool.affine_select(out=dcmask[:], in_=dcmask[:], compare_op=ALU.is_ge, fill=MASKED, base=HEADS - 1,
                                       pattern=[[HEADS, NS], [0, NDB]], channel_multiplier=-1)
                    pool.iota(iot[:], pattern=[[1, 16]], base=1, channel_multiplier=0, allow_small_or_imprecise_dtypes=True)
                    chain.then_wait(pool.tensor_copy(identb[:], ident[:]))
                    for g in range(4):
                        last = pool.tensor_scalar(invcnt[:, g], iot[:], float(2 << g), None, ALU.min)
                    last.then_inc(consts_ready, 1)
                    for e in range(2 * KD):
                        pool.wait_ge(hhi_ready, e + 1)
                        hf, k = divmod(e, KD)
                        c = slice(hf * 512, (hf + 1) * 512)
                        pool.tensor_tensor(h_lo[:, k, c], htmp[:, e % 2], h_hi[:, k, c].bitcast(F32), ALU.subtract)\
                            .then_inc(hlo_ready, 1)
                    pool.wait_ge(hhi_ready, 2 * KD + 1)
                    pool.tensor_tensor(h_lo[:, :, TP:T], htmp[:, 0, 0:KD * NS].rearrange("p (k n) -> p k n", k=KD),
                                       h_hi[:, :, TP:T].bitcast(F32), ALU.subtract).then_inc(hlo_ready, 1)

                @block.tensor
                def _(pe):
                    pe.wait_ge(consts_ready, 1)
                    pe.wait_ge(vec_loaded, 96)
                    pe.transpose(tp[1][:, 0:NVEC], vrow[:], ident[0:NVEC, 0:NVEC]).then_inc(vT_done, 1)
                    pe.wait_ge(silu_ready, 1)
                    for k in range(KD):
                        last = pe.transpose(tp[0][:, k * 16:k * 16 + 1 + NS], crow[:, k * P:(k + 1) * P], ident[0:1 + NS, 0:1 + NS])
                    last.then_inc(cT_done, 1)
                    pe.wait_ge(cT_ready, 1)

                    def condition(c):
                        pe.wait_ge(wa_loaded[c % NR], 16 * (c // NR + 1))
                        for n in range(4):
                            for k in range(KD):
                                last = pe.matmul(adaP[:, 4 * c + n], wa[:, c % NR, k, n * P:(n + 1) * P], cT[:, k],
                                                 start=(k == 0), stop=(k == KD - 1))
                        last.then_inc(ada_done, 1)

                    for c in range(NA):
                        condition(c)
                    pe.wait_ge(x_scaled, 1)
                    for e in range(2 * KD):
                        hf, k = divmod(e, KD)
                        if e >= 2:
                            pe.wait_ge(h_ready, e - 1)
                        for b in range(4):
                            last = pe.transpose(tp[1 + e % 2][:, b * P:(b + 1) * P], xt[:, 4 * hf + b, k * P:(k + 1) * P], ident[:])
                        last.then_inc(xT_done, 1)
                    for k in range(KD):
                        last = pe.transpose(tp[0][:, k * NS:(k + 1) * NS], xt[0:NS, NB, k * P:(k + 1) * P], ident[0:NS, 0:NS])
                    last.then_inc(xT_done, 1)

                @block.vector
                def _(dve):
                    chain = Chain(dve, dve_chain)
                    dve.wait_ge(csig_ready, 1)
                    dve.tensor_tensor(crow[:], crow[:], csig[:], ALU.mult).then_inc(silu_ready, 1)
                    dve.wait_ge(vT_done, 1)
                    dve.tensor_copy(vecs[:], tp[1][:, 0:NVEC])
                    dve.wait_ge(cT_done, 1)
                    dve.tensor_copy(cT[:], tp[0][:, 0:KD * 16].rearrange("p (k n) -> p k n", k=KD)[:, :, 0:1 + NS]).then_inc(cT_ready, 1)
                    dve.wait_ge(consts_ready, 1)
                    dve.reciprocal(invcnt[:], invcnt[:])
                    dve.wait_ge(squares_ready, 1)
                    dve.tensor_scalar(ms[:], ss[:], 1.0 / D, EPS, ALU.mult, ALU.add).then_inc(ms_ready, 1)
                    dve.wait_ge(root_ready, 1)
                    chain.then_wait(dve.reciprocal(rs[:], rt[:]))
                    newton(dve, chain, rs[:], ms[:], rt[:])
                    for b in range(NB):
                        dve.tensor_scalar(xt[:, b], xt[:, b], rs[:, b:b + 1], None, ALU.mult)
                    dve.tensor_scalar(xt[0:NS, NB], xt[0:NS, NB], rs[0:NS, NB:NB + 1], None, ALU.mult).then_inc(x_scaled, 1)
                    dve.wait_ge(ada_done, NA)
                    chain.then_wait(dve.tensor_tensor(ada[:], adaP[:], vecs[:, 0:6 * KD].unsqueeze(2).broadcast_to([P, 6 * KD, 1 + NS]), ALU.add))

                    def vec(at_row):
                        return vecs[:, at_row:at_row + KD].unsqueeze(2).broadcast_to([P, KD, 1 + NS])

                    dve.scalar_tensor_tensor(sc1[:], ada[:, KD:2 * KD], 1.0, vec(VG_PRE_MIX), ALU.add, ALU.mult)
                    dve.tensor_tensor(gt1[:], ada[:, 2 * KD:3 * KD], vec(VG_POST_MIX), ALU.mult)
                    dve.scalar_tensor_tensor(sc2[:], ada[:, 4 * KD:5 * KD], 1.0, vec(VG_PRE_MLP), ALU.add, ALU.mult)
                    chain.then_wait(dve.tensor_tensor(gt2[:], ada[:, 5 * KD:6 * KD], vec(VG_POST_MLP), ALU.mult))
                    for e in range(2 * KD):
                        k = e % KD
                        dve.wait_ge(xT_done, e + 1)
                        if e >= 2:
                            dve.wait_ge(hlo_ready, e - 1)
                        dve.tensor_scalar(htmp[:, e % 2], tp[1 + e % 2][:], sc1[:, k, 0:1], ada[:, k, 0:1],
                                          ALU.mult, ALU.add).then_inc(h_ready, 1)
                    dve.wait_ge(xT_done, 2 * KD + 1)
                    dve.wait_ge(hlo_ready, 2 * KD - 1)
                    hd = htmp[:, 0, 0:KD * NS].rearrange("p (k n) -> p k n", k=KD)
                    chain.then_wait(dve.tensor_tensor(hd, tp[0][:, 0:KD * NS].rearrange("p (k n) -> p k n", k=KD),
                                                      sc1[:, :, 1:], ALU.mult))
                    dve.tensor_tensor(hd, hd, ada[:, 0:KD, 1:], ALU.add).then_inc(h_ready, 1)

        at = buf.slabs(2)
        qT = at("qT", [P, GRP, T])
        uT = at("uT", [P, 4, T])
        catT = at("catT", [P, 2, NCAT * BLOCK])
        kvT = at("kvT", [P, 4, T])
        gT = at("gT", [24, T])
        cnewT = at("cnewT", [P, 2, NS])
        scratch3 = at.at[0] - buf.CONSTS - 3 * buf.SLAB
        with ExitStack() as st:
            accs = [psum(st, f"in_acc{s}", [P, NCH, 512]) for s in range(2)]
            g = Gemm(w, accs, sem, "in", parts=2)
            NU = 15
            with nc.Block() as block:

                @block.sync
                def _(sp):
                    wq = w_in[0, :, Q_COL:KV_COL].rearrange("(k p) (h c) -> p k h c", p=P, h=KVH)
                    for u in range(NU):
                        j, s = divmod(u, 2)
                        if u < GRP:
                            src = [wq[:, :, h, u * HD:(u + 1) * HD] for h in range(KVH)]
                        else:
                            c = KV_COL + (u - 4) * P if u < 10 else G_COL if u == 10 else U_COL + (u - 11) * P
                            src = [columns(w_in[0], c)[:, :, h * HD:(h + 1) * HD] for h in range(2)]
                        g.load(sp, src, j, s, first=(j == 0))

                @block.scalar
                def _(act):
                    g.cut_hi(act, 0, 0, first=True)
                    g.cut_hi(act, 0, 1, first=True)
                    with act.Fori(1, NU // 2) as j:
                        g.cut_hi(act, j, 0)
                        g.cut_hi(act, j, 1)
                    g.cut_hi(act, NU // 2, 0)

                @block.gpsimd
                def _(pool):
                    with pool.Fori(0, NU // 2) as j:
                        g.cut_lo(pool, j, 0)
                        g.cut_lo(pool, j, 1)
                    g.cut_lo(pool, NU // 2, 0)

                @block.tensor
                def _(pe):
                    g.multiply(pe, 0, 0, h_hi, h_lo, first=True)
                    g.multiply(pe, 0, 1, h_hi, h_lo, first=True)
                    with pe.Fori(1, NU // 2) as j:
                        g.multiply(pe, j, 0, h_hi, h_lo)
                        g.multiply(pe, j, 1, h_hi, h_lo)
                    g.multiply(pe, NU // 2, 0, h_hi, h_lo)

                @block.vector
                def _(dve):
                    for u in range(NU):
                        j, s = divmod(u, 2)
                        dve.wait_ge(g.done, u + 1)
                        if u in (4, 5):
                            k = u - 4
                            dve.tensor_copy(catT[:, k, 0:2 * CH].rearrange("p (c t) -> p c t", c=2), accs[s][:, 0:2, 0:CH])
                            dve.tensor_copy(catT[:, k, 2 * CH:TP], accs[s][:, 2, 0:TP - 2 * CH])
                            last = dve.tensor_copy(cnewT[:, k], accs[s][:, 2, TP - 2 * CH:CH])
                        elif u == 10:
                            last = dve.tensor_copy(by_chunk(gT[:]), accs[s][0:24, :, 0:CH])
                        else:
                            dst = qT[:, u] if u < 4 else kvT[:, u - 6] if u < 10 else uT[:, u - 11]
                            last = dve.tensor_copy(by_chunk(dst), g.out(s))
                        last.then_inc(g.freed[s], 1)

        at = buf.slabs(5)
        kT_hi = at("kT_hi", [P, 2, T], F32R)
        kT_lo = at("kT_lo", [P, 2, T], F32R)
        v_hi = at("v_hi", [P, 2, NB, P], F32R)
        v_lo = at("v_lo", [P, 2, NB, P], F32R)
        kcT = buf.small("kcT", [P, 2, NCAT])
        kc_hi = buf.small("kc_hi", [P, NCB], F32R)
        kc_lo = buf.small("kc_lo", [P, NCB], F32R)
        vc_hi = buf.small("vc_hi", [NCB, P], F32R)
        vc_lo = buf.small("vc_lo", [NCB, P], F32R)
        vc_dec = buf.small("vc_dec", [NS * NDB, P])
        v_new = buf.small("v_new", [NS, 2, P])
        knew = buf.const("knew", [P, 2, NS])
        with ExitStack() as st:
            at = buf.slabs(3, scratch3)
            JC = 8
            NWC = BLOCK // JC
            wc = at("wc", [P, 2, JC, P])
            ck = at("ck", [P, 2, NPG, 2 * P])
            tok = at("tok", [P, 2, 6 * P])
            behind_all = buf.tail
            posd = buf.small("posd", [BLOCK, 2, KVH, HD])
            tp = [psum(st, f"sh_tp{i}", [P, 1024]) for i in range(2)]
            cps = psum(st, "cps", [P, 2, 64])
            pos_loaded, ck_loaded = sem("pos_loaded"), [sem(f"ck_loaded{i}") for i in range(2)]
            wc_zeroed, wc_loaded = sem("wc_zeroed"), [sem(f"wc_loaded{i}") for i in range(2)]
            tp_done, tp_taken, wc_used = sem("tp_done"), sem("tp_taken"), sem("wc_used")
            gates_ready, rows_out, small_out = sem("gates_ready"), [sem(f"rows_out{i}") for i in range(2)], sem("small_out")
            vhi_ready, vlo_ready, khi_ready, klo_ready = sem("vhi_ready"), sem("vlo_ready"), sem("khi_ready"), sem("klo_ready")
            kc_done, kc_ready, kchi_ready, kclo_ready, vchi_ready = (sem(n) for n in ("kc_done", "kc_ready", "kchi_ready", "kclo_ready", "vchi_ready"))
            page_read, dchain, page_loaded = sem("page_read"), sem("dve_chain1"), sem("page_loaded")
            pt_sb = buf.const("pt_sb", [1, NS * NPG], I32)
            E_POS, E_GATE, E_TOK, E_NEW, E_U, E_UNEW, E_CK, E_VC = 0, 1, 2, 10, 11, 12, 13, 13 + NS
            utok = buf.small("utok", [HIST, PW])
            with nc.Block() as block:

                @block.sync
                def _(sp):
                    sp.dma_start(pt_sb[:], page_table.rearrange("n (o g) -> o (n g)", o=1)).then_inc(page_loaded, 16)
                    for h in range(KVH):
                        sp.dma_start(posd[:, :, h], pos_cmp[0]).then_inc(pos_loaded, 16)
                    sp.wait_ge(page_loaded, 16)
                    for n in range(NS):
                        if n >= 2:
                            sp.wait_ge(tp_done, E_CK + n - 1)
                        for g in range(NPG):
                            page = sp.value_load(pt_sb[0:1, n * NPG + g:n * NPG + g + 1], min_val=0, max_val=NPHYS - 1)
                            sp.dma_start(ck[:, n % 2, g], cache_cmp_kv[0].rearrange("n s a h d -> n s (a h d)")[bass.ds(page, 1)]
                                         .rearrange("n s c -> (n s) c")).then_inc(ck_loaded[n % 2], 16)
                    sp.wait_ge(small_out, 16 * 7)

                @block.gpsimd
                def _(pool):
                    pool.memset(wc[:], 0.0).then_inc(wc_zeroed, 1)
                    pool.wait_ge(khi_ready, 1)
                    for s in range(2):
                        last = pool.tensor_tensor(kT_lo[:, s], kvT[:, 2 * s], kT_hi[:, s].bitcast(F32), ALU.subtract)
                    last.then_inc(klo_ready, 1)
                    for b in range(NB):
                        pool.wait_ge(vhi_ready, b + 1)
                        t = tok[:, b % 2].rearrange("p (a s c) -> p a s c", a=3, s=2)[:, 1:3, 1]
                        pool.tensor_tensor(v_lo[:, :, b], t, v_hi[:, :, b].bitcast(F32), ALU.subtract).then_inc(vlo_ready, 1)

                @block.scalar
                def _(act):
                    act.activation(gT[:], gT[:], ACT.Sigmoid).then_inc(gates_ready, 1)
                    for s in range(2):
                        last = act.activation(kT_hi[:, s], kvT[:, 2 * s], ACT.Copy)
                    last.then_inc(khi_ready, 1)
                    act.activation(knew[:], kvT[:].rearrange("p (b s) t -> p b s t", b=2)[:, :, 0, TP:T], ACT.Copy)
                    for b in range(NB):
                        act.wait_ge(tp_taken, E_TOK + b + 1)
                        t = tok[:, b % 2]
                        for c, dst in ((0, n_cmp_p), (1, n_sel_p)):
                            act.dma_start(dst[0, 0, b * P:(b + 1) * P].rearrange("t a h d -> t (a h d)"),
                                          t[:, c * 256:(c + 1) * 256]).then_inc(rows_out[b % 2], 16)
                        if b >= NB - WB:
                            w0 = (b - (NB - WB)) * P
                            act.dma_start(n_win_p[0, 0, w0:w0 + P].rearrange("t a h d -> t (a h d)"),
                                          t[:, 512:768]).then_inc(rows_out[b % 2], 16)
                        act.activation(v_hi[:, :, b], t.rearrange("p (a s c) -> p a s c", a=3, s=2)[:, 1:3, 1],
                                       ACT.Copy).then_inc(vhi_ready, 1)
                    act.wait_ge(tp_taken, E_NEW + 1)
                    for c, dst in ((0, n_cmp_s), (1, n_sel_s)):
                        act.dma_start(dst[0, :, 0].rearrange("n a h d -> n (a h d)"), tok[0:NS, 0, c * 256:(c + 1) * 256]).then_inc(small_out, 16)
                    act.dma_start(n_win_s[0, :, PAST - 1].rearrange("n a h d -> n (a h d)"), tok[0:NS, 0, 512:768]).then_inc(small_out, 16)
                    act.dma_start(n_win_s[0, :, 0:PAST - 1].rearrange("n t a h d -> n (t a h d)"),
                                  state_win_kv[0, :, 1:PAST].rearrange("n t a h d -> n (t a h d)")).then_inc(small_out, 16)
                    act.dma_start(n_pool_s[0, :, 0:HIST - 1], state_pool[0, :, 1:HIST]).then_inc(small_out, 16)
                    act.wait_ge(tp_taken, E_U + 1)
                    act.dma_start(n_pool_p[0, 0], utok[:]).then_inc(small_out, 16)
                    act.wait_ge(tp_taken, E_UNEW + 1)
                    act.dma_start(n_pool_s[0, :, HIST - 1], tok[0:NS, 1, 0:PW]).then_inc(small_out, 16)
                    act.wait_ge(wc_zeroed, 1)
                    for q in range(2 * NWC):
                        s, c = divmod(q, NWC)
                        if q >= 2:
                            act.wait_ge(wc_used, q - 1)
                        for h in range(KVH):
                            act.dma_start(wc[h * HD:(h + 1) * HD, q % 2, :, h * HD:(h + 1) * HD],
                                          w_cmp[0, s, c * JC:(c + 1) * JC].rearrange("j d e -> d j e")).then_inc(wc_loaded[q % 2], 16)
                    act.wait_ge(kc_ready, 1)
                    act.activation(kc_hi[:], kcT[:, 0, 0:NCB], ACT.Copy).then_inc(kchi_ready, 1)
                    act.wait_ge(tp_done, E_VC + 1)
                    act.activation(vc_hi[:], tp[E_VC % 2][0:NCB, 0:P], ACT.Copy).then_inc(vchi_ready, 1)
                    act.wait_ge(rows_out[0], 16 * (2 * 4 + 2))
                    act.wait_ge(rows_out[1], 16 * (2 * 4 + 2))

                @block.tensor
                def _(pe):
                    def slot(e):
                        if e >= 2:
                            pe.wait_ge(tp_taken, e - 1)
                        return tp[e % 2]

                    t = slot(E_POS)
                    pe.wait_ge(pos_loaded, 32)
                    for s in range(2):
                        last = pe.transpose(t[:, s * BLOCK:(s + 1) * BLOCK], posd[:, s].rearrange("j h d -> j (h d)"), ident[0:BLOCK, 0:BLOCK])
                    last.then_inc(tp_done, 1)
                    t = slot(E_GATE)
                    pe.wait_ge(gates_ready, 1)
                    for b in range(NB):
                        pe.transpose(t[:, b * 24:(b + 1) * 24], gT[:, b * P:(b + 1) * P], ident[0:24, 0:24])
                    pe.transpose(t[0:NS, NB * 24:(NB + 1) * 24], gT[:, TP:T], ident[0:24, 0:24]).then_inc(tp_done, 1)
                    sources = [catT[:, 0], catT[:, 1], kvT[:, 0], kvT[:, 1], kvT[:, 2], kvT[:, 3]]
                    for b in range(NB):
                        t = slot(E_TOK + b)
                        for n, x in enumerate(sources):
                            last = pe.transpose(t[:, n * P:(n + 1) * P], x[:, b * P:(b + 1) * P], ident[:])
                        last.then_inc(tp_done, 1)
                    t = slot(E_NEW)
                    for n in range(6):
                        x = cnewT[:, n] if n < 2 else kvT[:, n - 2, TP:T]
                        last = pe.transpose(t[0:NS, n * P:(n + 1) * P], x, ident[:])
                    last.then_inc(tp_done, 1)
                    t = slot(E_U)
                    for n in range(4):
                        last = pe.transpose(t[0:HIST, n * P:(n + 1) * P], uT[:, n, TP - HIST:TP], ident[:])
                    last.then_inc(tp_done, 1)
                    t = slot(E_UNEW)
                    for n in range(4):
                        last = pe.transpose(t[0:NS, n * P:(n + 1) * P], uT[:, n, TP:T], ident[:])
                    last.then_inc(tp_done, 1)
                    for n in range(NS):
                        t = slot(E_CK + n)
                        pe.wait_ge(ck_loaded[n % 2], 16 * NPG * (n // 2 + 1))
                        for s in range(2):
                            for g in range(NPG):
                                last = pe.transpose(t[:, (s * NPG + g) * P:(s * NPG + g + 1) * P], ck[:, n % 2, g, s * P:(s + 1) * P], ident[:])
                        last.then_inc(tp_done, 1)
                    pe.wait_ge(tp_taken, E_VC)
                    for q in range(2 * NWC):
                        s, c = divmod(q, NWC)
                        pe.wait_ge(wc_loaded[q % 2], 32 * (q // 2 + 1))
                        rows = catT[:, s].rearrange("p (b j) -> p j b", j=BLOCK)
                        for jj in range(JC):
                            j = c * JC + jj
                            last = pe.matmul(cps[:, s, 0:NCAT], wc[:, q % 2, jj], rows[:, j], start=(j == 0), stop=(j == BLOCK - 1))
                        last.then_inc(wc_used, 1)
                    t = slot(E_VC)
                    pe.wait_ge(kc_ready, 1)
                    pe.transpose(t[0:NCB, 0:P], kcT[:, 1, 0:NCB], ident[:])
                    pe.transpose(t[0:NS * NDB, P:2 * P], kcT[:, 1, NCB:NCAT - 1], ident[:]).then_inc(tp_done, 1)

                @block.vector
                def _(dve):
                    chain = Chain(dve, dchain)
                    for e in range(E_VC):
                        dve.wait_ge(tp_done, e + 1)
                        t = tp[e % 2]
                        if e == E_POS:
                            last = dve.tensor_copy(catT[:, :, (NCAT - 1) * BLOCK:], t[:, 0:2 * BLOCK].rearrange("p (s j) -> p s j", s=2))
                        elif e == E_GATE:
                            dve.tensor_copy(gtok[:], t[:, 0:NB * 24].rearrange("p (b c) -> p b c", b=NB))
                            last = dve.tensor_copy(gdec8[:], t[0:NS, NB * 24:(NB + 1) * 24])
                        elif e < E_NEW:
                            b = e - E_TOK
                            if b >= 2:
                                dve.wait_ge(vlo_ready, b - 1)
                                dve.wait_ge(rows_out[b % 2], 16 * (2 * (b // 2) + max(0, b // 2 - 2)))
                            last = dve.tensor_copy(tok[:, b % 2], t[:, 0:6 * P])
                        elif e == E_NEW:
                            dve.wait_ge(vlo_ready, NB)
                            dve.wait_ge(rows_out[0], 16 * 10)
                            chain.then_wait(dve.tensor_copy(tok[0:NS, 0], t[0:NS, 0:6 * P]))
                            last = dve.tensor_copy(v_new[:], tok[0:NS, 0].rearrange("p (a s c) -> p a s c", a=3, s=2)[:, 1:3, 1])
                        elif e == E_U:
                            last = dve.tensor_copy(utok[:], t[0:HIST, 0:PW])
                        elif e == E_UNEW:
                            dve.wait_ge(rows_out[1], 16 * 10)
                            last = dve.tensor_copy(tok[0:NS, 1, 0:PW], t[0:NS, 0:PW])
                        else:
                            c = TP + (e - E_CK) * PAST
                            last = dve.tensor_copy(catT[:, :, c:c + PAST], t[:, 0:2 * PAST].rearrange("p (s c) -> p s c", s=2))
                        last.then_inc(tp_taken, 1)
                    dve.wait_ge(wc_used, 2 * NWC)
                    chain.then_wait(dve.tensor_copy(kcT[:], cps[:, :, 0:NCAT]))
                    for s in range(2):
                        last = dve.tensor_scalar(kcT[:, s, 0:NCAT - 1], kcT[:, s, 0:NCAT - 1], kcT[:, s, NCAT - 1:NCAT], None, ALU.add)
                    last.then_inc(kc_ready, 1)
                    dve.wait_ge(kchi_ready, 1)
                    dve.tensor_tensor(kc_lo[:], kcT[:, 0, 0:NCB], kc_hi[:].bitcast(F32), ALU.subtract)
                    dve.wait_ge(vchi_ready, 1)
                    dve.tensor_tensor(vc_lo[:], tp[E_VC % 2][0:NCB, 0:P], vc_hi[:].bitcast(F32), ALU.subtract)
                    dve.tensor_copy(vc_dec[:], tp[E_VC % 2][0:NS * NDB, P:2 * P]).then_inc(kclo_ready, 1)

        with ExitStack() as st:
            at = buf.slabs(3)
            wsum = at("wsum", [P, 2, TP])
            hist = at("hist", [NS * HIST, PW])
            ext = at("ext", [P, 4, NS, 16])
            dsum = at("dsum", [P, 4, NS])
            pooled = at("pooled", [P, 4, T])
            wp = at("wp", [P, 4, P])
            ph = psum(st, "ph", [P, 512])
            pp = [psum(st, f"pp{i}", [P, NCH, 512]) for i in range(2)]
            hist_loaded, wp_loaded, hT_done, pooled_ready, mixed_done = (sem(n) for n in ("hist_loaded", "wp_loaded", "hT_done", "pooled_ready", "mixed_done"))
            pchain, gd_loaded, mix_taken = sem("dve_chain2"), sem("gd_loaded"), sem("mix_taken")
            with nc.Block() as block:

                @block.sync
                def _(sp):
                    sp.dma_start(hist[:], state_pool[0].rearrange("n t c -> (n t) c")).then_inc(hist_loaded, 16)
                    sp.dma_start(wp[:], w_pool[0].rearrange("g c d -> c g d")).then_inc(wp_loaded, 16)
                    for n in range(NS):
                        sp.dma_start(gdec[n * HEADS:(n + 1) * HEADS, :], gdec8[n:n + 1, :]).then_inc(gd_loaded, 16)
                    sp.wait_ge(gd_loaded, 16 * NS)

                @block.tensor
                def _(pe):
                    pe.wait_ge(hist_loaded, 16)
                    n = NS * HIST
                    for g in range(4):
                        last = pe.transpose(ph[:, g * n:(g + 1) * n], hist[:, g * P:(g + 1) * P], ident[0:n, 0:n])
                    last.then_inc(hT_done, 1)
                    pe.wait_ge(wp_loaded, 16)
                    for g in range(4):
                        pe.wait_ge(pooled_ready, g + 1)
                        if g >= 2:
                            pe.wait_ge(mix_taken, g - 1)
                        for c in range(NCH):
                            last = pe.matmul(pp[g % 2][:, c, 0:CH], wp[:, g], pooled[:, g, c * CH:(c + 1) * CH], start=True, stop=True)
                        last.then_inc(mixed_done, 1)

                @block.scalar
                def _(act):
                    for g in range(4):
                        act.wait_ge(mixed_done, g + 1)
                        act.activation(by_chunk(uT[:, g]), pp[g % 2][:, :, 0:CH], ACT.Copy, scale=vecs[:, V_POOL + g:V_POOL + g + 1])\
                           .then_inc(mix_taken, 1)

                @block.vector
                def _(dve):
                    chain = Chain(dve, pchain)
                    dve.wait_ge(hT_done, 1)
                    dve.tensor_copy(ext[:, :, :, 0:HIST], ph[:, 0:4 * NS * HIST].rearrange("p (g n t) -> p g n t", g=4, n=NS))
                    chain.then_wait(dve.tensor_copy(ext[:, :, :, HIST], uT[:, :, TP:T]))
                    for g in range(4):
                        win = 2 << g
                        src, n = uT[:, g, 0:TP], 1
                        for r in range(g + 1):
                            dst = wsum[:, r % 2]
                            dve.tensor_copy(dst[:, 0:n], src[:, 0:n])
                            chain.then_wait(dve.tensor_tensor(dst[:, n:TP], src[:, n:TP], src[:, 0:TP - n], ALU.add))
                            src, n = dst, 2 * n
                        chain.then_wait(dve.tensor_tensor(src[:, 0:16], src[:, 0:16], invcnt[:, g], ALU.mult))
                        dve.scalar_tensor_tensor(pooled[:, g, 0:16], uT[:, g, 0:16], -1.0, src[:, 0:16], ALU.mult, ALU.add)
                        dve.scalar_tensor_tensor(pooled[:, g, 16:TP], src[:, 16:TP], 1.0 / win, uT[:, g, 16:TP], ALU.mult, ALU.subtract)
                        chain.then_wait(dve.tensor_reduce(dsum[:, g], ext[:, g, :, 16 - win:16], AX.X, ALU.add))
                        dve.scalar_tensor_tensor(pooled[:, g, TP:T], dsum[:, g], 1.0 / win, uT[:, g, TP:T],
                                                 ALU.mult, ALU.subtract).then_inc(pooled_ready, 1)

        SEL, WIN, CMP = 0, TP, TP + WINDOW + P
        NKP = CMP + NCB
        NG = NB * KVH
        JOBS = 2 * GRP
        PAIRS = JOBS // 2
        LAG = 2
        RING = LAG + 1
        groups = [divmod(n, KVH) for n in range(NG)]

        def key_blocks(i):
            first = max(0, i - WB)
            win = [(1, b, WIN + (b - first) * P, P) for b in range(first, i + 1)]
            sel = [(0, b, SEL + b * P, P) for b in range(i + 1)]
            return win + [(2, 0, CMP, NCB)] + sel

        blocks_before = [sum(len(key_blocks(i)) for i, _ in groups[:n]) for n in range(NG + 1)]
        blocks = [(n, z) for n, (i, _) in enumerate(groups) for z in range(len(key_blocks(i)))]
        NBL = len(blocks)
        ends = [b - 1 for b in blocks_before[1:]]

        def jobs_at(t):
            n, z = blocks[t]
            size = len(key_blocks(groups[n][0]))
            return [(n + 1, k) for k in range(JOBS) if k * size // JOBS == z and n + 1 < NG]

        with ExitStack() as st:
            at = buf.slabs(3)
            prob = at("prob", [P, 2, GRP, NKP])
            q_hi = at("q_hi", [P, GRP, P], F32R)
            q_lo = at("q_lo", [P, GRP, P], F32R)
            p_hi = at("p_hi", [P, RING, GRP * P], F32R)
            buf.tail = behind_all
            p_lo = [at("p_lo0", [P, GRP * P], F32R)] + [buf.small(f"p_lo{r}", [P, GRP * P], F32R) for r in range(1, RING)]
            top = buf.const("top", [P, 2, GRP, 3])
            bias = buf.const("bias", [P, 2, GRP, 3])
            total = buf.const("total", [P, 2, GRP, 3])
            share = buf.const("share", [P, 2, GRP, 3])
            sps = [psum(st, f"scores{i}", [P, 1024]) for i in range(2)]
            pT = [psum(st, f"pT{i}", [P, 512]) for i in range(RING)]
            out = psum(st, "attn_out", [P, 512])
            qhi_ready, qlo_ready, scores_done, bias_ready, exp_done = (sem(n) for n in ("qhi_ready", "qlo_ready", "scores_done", "bias_ready", "exp_done"))
            share_ready, prob_ready, pT_done, phi_ready, plo_ready, pv_done, out_taken = (
                sem(n) for n in ("share_ready", "prob_ready", "pT_done", "phi_ready", "plo_ready", "pv_done", "out_taken"))
            achain = sem("dve_chain3")

            def rows_of(kv):
                return slice(kv * HD, (kv + 1) * HD)

            with nc.Block() as block:

                @block.tensor
                def _(pe):
                    def product(dst, rows, g, keys_hi, keys_lo, start, more):
                        for m, (a, b) in enumerate(((q_hi, keys_hi), (q_hi, keys_lo), (q_lo, keys_hi))):
                            last = pe.matmul(dst, a[rows, g], b, start=start and m == 0, stop=(m == 2 and not more),
                                             skip_group_check=True)
                        return last

                    def branch(ps, s, rows, g, k0, k1, masks):
                        for c in range(k0, k1, 512):
                            e = min(c + 512, k1)
                            inside = [(at, m) for at, m in masks if c <= at < e]
                            last = product(ps[:, c - k0:e - k0], rows, g, kT_hi[rows, s, c:e], kT_lo[rows, s, c:e], True, bool(inside))
                            for z, (at_key, m) in enumerate(inside):
                                last = pe.matmul(ps[:, at_key - k0:at_key - k0 + P], identb[:], m[:], start=False,
                                                 stop=(z == len(inside) - 1), skip_group_check=True)
                        return last

                    def scores(n, k):
                        i, kv = groups[n]
                        rows, g, job = rows_of(kv), k % GRP, n * JOBS + k
                        ps = sps[job % 2]
                        if k == 0 and kv == 0:
                            pe.wait_ge(qlo_ready, i + 1)
                        if job >= 2:
                            pe.wait_ge(exp_done, job - 1)
                        if k >= GRP:
                            last = branch(ps, 0, rows, g, 0, (i + 1) * P, [(i * P, causal)])
                        else:
                            first = max(0, i - WB) * P
                            branch(ps, 1, rows, g, first, (i + 1) * P, [(i * P, causal)] + ([(first, behind)] if i >= WB else []))
                            whole = i < WB
                            c0 = WINDOW + P
                            product(ps[:, c0:c0 + NCB], rows, g, kc_hi[rows, :], kc_lo[rows, :], whole, True)
                            last = pe.matmul(ps[:, c0:c0 + NCB], identb[:], cmask[:, i], start=False, stop=True,
                                             skip_group_check=True)
                        last.then_inc(scores_done, 1)

                    def turn(t):
                        n, z = blocks[t]
                        br, _, c, m = key_blocks(groups[n][0])[z]
                        if z == 0:
                            pe.wait_ge(prob_ready, n * PAIRS + PAIRS // 2)
                        elif br == 0:
                            pe.wait_ge(prob_ready, (n + 1) * PAIRS)
                        if t >= RING:
                            pe.wait_ge(plo_ready, t - RING + 1)
                        for g in range(GRP):
                            last = pe.transpose(pT[t % RING][0:m, g * P:(g + 1) * P], prob[:, n % 2, g, c:c + m], ident[:])
                        last.then_inc(pT_done, 1)

                    def values(t):
                        n, z = blocks[t]
                        br, b, _, m = key_blocks(groups[n][0])[z]
                        if z == 0 and n:
                            pe.wait_ge(out_taken, n)
                        pe.wait_ge(plo_ready, t + 1)
                        a_hi, a_lo = (vc_hi[:], vc_lo[:]) if br == 2 else (v_hi[:, br, b], v_lo[:, br, b])
                        hi, lo = p_hi[0:m, t % RING], p_lo[t % RING][0:m]
                        for x, (a, p) in enumerate(((a_hi, hi), (a_hi, lo), (a_lo, hi))):
                            last = pe.matmul(out[:], a, p, start=(z == 0 and x == 0),
                                             stop=(t + 1 == blocks_before[n + 1] and x == 2), skip_group_check=True)
                        last.then_inc(pv_done, 1)

                    for k in range(JOBS):
                        scores(0, k)
                    for t in range(NBL):
                        for n, k in jobs_at(t):
                            scores(n, k)
                        turn(t)
                        if t >= LAG:
                            values(t - LAG)
                    for t in range(NBL - LAG, NBL):
                        values(t)

                @block.scalar
                def _(act):
                    def exps(n, k):
                        i, _ = groups[n]
                        g, job = k % GRP, n * JOBS + k
                        ps = sps[job % 2]
                        if k == 0 and n >= 2:
                            act.wait_ge(pT_done, blocks_before[n - 1])
                        act.wait_ge(bias_ready, job + 1)
                        nw = (min(i, WB) + 1) * P
                        todo = [(2, 0, nw, WIN), (0, WINDOW + P, NCB, CMP)] if k < GRP else [(1, 0, (i + 1) * P, SEL)]
                        for which, c0, m, to in todo:
                            last = act.activation(prob[:, n % 2, g, to:to + m], ps[:, c0:c0 + m], ACT.Exp, scale=SCALE,
                                                  bias=bias[:, n % 2, g, which:which + 1],
                                                  accum_out=total[:, n % 2, g, which:which + 1])
                        last.then_inc(exp_done, 1)

                    def cut(t):
                        n, z = blocks[t]
                        m = key_blocks(groups[n][0])[z][3]
                        act.wait_ge(pT_done, t + 1)
                        if t >= RING:
                            act.wait_ge(pv_done, t - RING + 1)
                        act.activation(p_hi[0:m, t % RING], pT[t % RING][0:m, :], ACT.Copy).then_inc(phi_ready, 1)

                    def cut_q(i):
                        if i:
                            act.wait_ge(scores_done, JOBS * KVH * i)
                        act.activation(q_hi[:], qT[:, :, i * P:(i + 1) * P], ACT.Copy).then_inc(qhi_ready, 1)

                    cut_q(0)
                    for k in range(JOBS):
                        exps(0, k)
                    for t in range(NBL):
                        jobs = jobs_at(t)
                        for n, k in jobs[:-1]:
                            exps(n, k)
                        cut(t)
                        for n, k in jobs[-1:]:
                            exps(n, k)
                            if k == JOBS - 1 and n % KVH == KVH - 1 and n + 1 < NG:
                                cut_q((n + 1) // KVH)

                @block.gpsimd
                def _(pool):
                    for n in range(NG):
                        i, _ = groups[n]
                        nw = (min(i, WB) + 1) * P
                        for pair in range(PAIRS):
                            pool.wait_ge(share_ready, n * PAIRS + pair + 1)
                            todo = [(2, WIN, nw), (0, CMP, NCB)] if pair < PAIRS // 2 else [(1, SEL, (i + 1) * P)]
                            for g in range(2 * pair % GRP, 2 * pair % GRP + 2):
                                for which, c, m in todo:
                                    y = prob[:, n % 2, g, c:c + m]
                                    last = pool.tensor_scalar(y, y, share[:, n % 2, g, which:which + 1], None, ALU.mult)
                            last.then_inc(prob_ready, 1)

                @block.vector
                def _(dve):
                    chain = Chain(dve, achain)

                    def maxima(n, k):
                        i, _ = groups[n]
                        g, job = k % GRP, n * JOBS + k
                        ps, tp_, bs = sps[job % 2], top[:, n % 2, g], bias[:, n % 2, g]
                        dve.wait_ge(scores_done, job + 1)
                        if k >= GRP:
                            chain.then_wait(dve.tensor_reduce(tp_[:, 1:2], ps[:, 0:(i + 1) * P], AX.X, ALU.max))
                            dve.tensor_scalar(bs[:, 1:2], tp_[:, 1:2], -SCALE, None, ALU.mult).then_inc(bias_ready, 1)
                        else:
                            dve.tensor_reduce(tp_[:, 2:3], ps[:, 0:(min(i, WB) + 1) * P], AX.X, ALU.max)
                            chain.then_wait(dve.tensor_reduce(tp_[:, 0:1], ps[:, WINDOW + P:WINDOW + P + NCB], AX.X, ALU.max))
                            dve.tensor_scalar(bs[:, 0:3:2], tp_[:, 0:3:2], MAX_FLOOR, -SCALE, ALU.max, ALU.mult).then_inc(bias_ready, 1)

                    def shares(n, pair):
                        i, kv = groups[n]
                        dve.wait_ge(exp_done, n * JOBS + 2 * pair + 2)
                        g = slice(2 * pair % GRP, 2 * pair % GRP + 2)
                        which = slice(0, 3, 2) if pair < PAIRS // 2 else slice(1, 2)
                        x = share[:, n % 2, g, which]
                        gates = gtok[:, i].rearrange("p (k g b) -> p k g b", k=KVH, g=GRP)[:, kv, g, which]
                        chain.then_wait(dve.tensor_scalar(x, total[:, n % 2, g, which], 1e-30, None, ALU.max))
                        chain.then_wait(dve.reciprocal(x, x))
                        dve.tensor_tensor(x, x, gates, ALU.mult).then_inc(share_ready, 1)

                    def cut(t):
                        n, z = blocks[t]
                        m = key_blocks(groups[n][0])[z][3]
                        dve.wait_ge(phi_ready, t + 1)
                        dve.tensor_tensor(p_lo[t % RING][0:m], pT[t % RING][0:m, :], p_hi[0:m, t % RING].bitcast(F32), ALU.subtract)\
                           .then_inc(plo_ready, 1)

                    def cut_q(i):
                        dve.wait_ge(qhi_ready, i + 1)
                        dve.tensor_tensor(q_lo[:], qT[:, :, i * P:(i + 1) * P], q_hi[:].bitcast(F32), ALU.subtract).then_inc(qlo_ready, 1)

                    def take(n):
                        i, kv = groups[n]
                        rows = rows_of(kv)
                        dve.wait_ge(pv_done, blocks_before[n + 1])
                        dve.tensor_copy(qT[rows, :, i * P:(i + 1) * P],
                                        out[rows].rearrange("p (g t) -> p g t", g=GRP)).then_inc(out_taken, 1)

                    cut_q(0)
                    for k in range(JOBS):
                        maxima(0, k)
                        if k >= 3 and k % 2:
                            shares(0, k // 2 - 1)
                    shares(0, PAIRS - 1)
                    for t in range(NBL):
                        if t > LAG and t - LAG - 1 in ends:
                            take(ends.index(t - LAG - 1))
                        for n, k in jobs_at(t):
                            maxima(n, k)
                        cut(t)
                        for n, k in jobs_at(t - 1) if t else []:
                            if k % 2:
                                shares(n, k // 2)
                        for n, k in jobs_at(t):
                            if k == JOBS - 1 and n % KVH == KVH - 1 and n + 1 < NG:
                                cut_q((n + 1) // KVH)
                    take(NG - 1)

        GATE = (1, 2, 0)
        with ExitStack() as st:
            at = buf.slabs(3)
            cs = at("cs", [P, NS, NPG, 2 * P])
            cw = at("cw", [P, NS, NPG, 2 * P])
            keysT = at("keysT", [P, 2, NS, PAST])
            qz = at("qz", [P, NS * (R + HEADS)])
            qall = at("qall", [P, NS, HEADS])
            NKD = 2 * (PAST + NS) + NS * NDB
            NKS, NKW, NKC = 0, PAST + NS, 2 * (PAST + NS)
            pd = at("pd", [R, NKD])
            chunks = [(NKS, P), (NKS + P, P), (NKS + PAST, NS), (NKW, P), (NKW + P, P), (NKW + PAST, NS), (NKC, NS * NDB)]
            pdT = at("pdT", [P, len(chunks), R])
            dtop, dbias, dtotal, dshare = (at(n, [R, 3]) for n in ("dtop", "dbias", "dtotal", "dshare"))
            dps = psum(st, "dps", [P, 3, 512])
            tpd = [psum(st, f"tpd{i}", [P, 512]) for i in range(2)]
            ptp = psum(st, "ptp", [P, len(chunks), R])
            dout = psum(st, "dout", [P, R])
            cs_loaded, cw_loaded, qz_zeroed, qz_ready = (sem(n) for n in ("cs_loaded", "cw_loaded", "qz_zeroed", "qz_ready"))
            kt_done, kt_taken, dsc_done, dbias_ready, dexp_done = (sem(n) for n in ("kt_done", "kt_taken", "dsc_done", "dbias_ready", "dexp_done"))
            pd_ready, pdT_done, pdT_ready, dout_done, ddchain = (sem(n) for n in ("pd_ready", "pdT_done", "pdT_ready", "dout_done", "dve_chain4"))
            with nc.Block() as block:

                @block.sync
                def _(sp):
                    for n in range(NS):
                        sp.dma_start(cw[:, n], state_win_kv[0, n].rearrange("(g s) a h d -> s g (a h d)", g=NPG)).then_inc(cw_loaded, 16)
                        for g in range(NPG):
                            page = sp.value_load(pt_sb[0:1, n * NPG + g:n * NPG + g + 1], min_val=0, max_val=NPHYS - 1)
                            sp.dma_start(cs[:, n, g], cache_sel_kv[0].rearrange("n s a h d -> n s (a h d)")[bass.ds(page, 1)]
                                         .rearrange("n s c -> (n s) c")).then_inc(cs_loaded, 16)

                @block.gpsimd
                def _(pool):
                    pool.memset(qz[:], 0.0).then_inc(qz_zeroed, 1)

                @block.tensor
                def _(pe):
                    for br, (c, loaded) in enumerate(((cs, cs_loaded), (cw, cw_loaded))):
                        pe.wait_ge(loaded, 16 * NS * (NPG if br == 0 else 1))
                        for m in range(NS // 2):
                            e = br * (NS // 2) + m
                            if e >= 2:
                                pe.wait_ge(kt_taken, e - 1)
                            for x in range(2 * NPG):
                                last = pe.transpose(tpd[e % 2][:, x * P:(x + 1) * P], c[:, 2 * m + x // NPG, x % NPG, 0:P], ident[:])
                            last.then_inc(kt_done, 1)
                    pe.wait_ge(kt_taken, NS)
                    pe.wait_ge(qz_ready, 1)
                    qa = qall[:].rearrange("p n h -> p (n h)")
                    for br in range(2):
                        ps = dps[0:R, br]
                        pe.matmul(ps[:, PAST:PAST + NS], qa, knew[:, br], start=True, stop=False, skip_group_check=True)
                        pe.matmul(ps[:, PAST:PAST + NS], identb[0:R, 0:R], dmask[:], start=False, stop=True, skip_group_check=True)
                        for n in range(NS):
                            pe.matmul(ps[:, 0:PAST], qz[:, n * R:(n + 1) * R], keysT[:, br, n], start=False, stop=(n == NS - 1),
                                      skip_group_check=True)
                    pe.matmul(dps[0:R, 2, 0:NS * NDB], qa, kcT[:, 0, NCB:NCAT - 1], start=True, stop=False)
                    pe.matmul(dps[0:R, 2, 0:NS * NDB], identb[0:R, 0:R], dcmask[:].rearrange("p n b -> p (n b)"),
                              start=False, stop=True).then_inc(dsc_done, 1)
                    pe.wait_ge(pd_ready, 1)
                    for x, (c, m) in enumerate(chunks):
                        last = pe.transpose(ptp[0:m, x], pd[:, c:c + m], ident[0:R, 0:R])
                    last.then_inc(pdT_done, 1)
                    pe.wait_ge(pdT_ready, 1)
                    pe.matmul(dout[:], vc_dec[:], pdT[0:NS * NDB, 6], start=True, stop=False, skip_group_check=True)
                    for br, (c, x) in enumerate(((cs, 0), (cw, 3))):
                        pe.matmul(dout[:], v_new[:, br], pdT[0:NS, x + 2], start=False, stop=False, skip_group_check=True)
                        for n in range(NS):
                            own = slice(n * HEADS, (n + 1) * HEADS)
                            for g in range(NPG):
                                last = pe.matmul(dout[:, own], c[:, n, g, P:2 * P], pdT[:, x + g, own], start=False,
                                                 stop=(br == 1 and g == NPG - 1), skip_group_check=True)
                    last.then_inc(dout_done, 1)

                @block.scalar
                def _(act):
                    act.wait_ge(dbias_ready, 1)
                    for br, (c, m) in enumerate(((NKS, PAST + NS), (NKW, PAST + NS), (NKC, NS * NDB))):
                        last = act.activation(pd[:, c:c + m], dps[0:R, br, 0:m], ACT.Exp, scale=SCALE, bias=dbias[:, br:br + 1],
                                              accum_out=dtotal[:, GATE[br]:GATE[br] + 1])
                    last.then_inc(dexp_done, 1)

                @block.vector
                def _(dve):
                    chain = Chain(dve, ddchain)
                    dve.wait_ge(qz_zeroed, 1)
                    qzn = qz[:].rearrange("p (n c) -> p n c", c=R + HEADS)
                    for kv in range(KVH):
                        rows = slice(kv * HD, (kv + 1) * HD)
                        heads = slice(kv * GRP, (kv + 1) * GRP)
                        chain.then_wait(dve.tensor_copy(qzn[rows, :, heads], qT[rows, :, TP:T].rearrange("p g n -> p n g")))
                    dve.tensor_copy(qall[:], qzn[:, :, 0:HEADS]).then_inc(qz_ready, 1)
                    for e in range(NS):
                        dve.wait_ge(kt_done, e + 1)
                        br, m = divmod(e, NS // 2)
                        dve.tensor_copy(keysT[:, br, 2 * m:2 * m + 2], tpd[e % 2][:].rearrange("p (n k) -> p n k", n=2)).then_inc(kt_taken, 1)
                    dve.wait_ge(dsc_done, 1)
                    dve.tensor_reduce(dtop[:, 0:2], dps[0:R, 0:2, 0:PAST + NS], AX.X, ALU.max)
                    chain.then_wait(dve.tensor_reduce(dtop[:, 2:3], dps[0:R, 2, 0:NS * NDB], AX.X, ALU.max))
                    dve.tensor_scalar(dbias[:], dtop[:], -SCALE, None, ALU.mult).then_inc(dbias_ready, 1)
                    dve.wait_ge(dexp_done, 1)
                    chain.then_wait(dve.reciprocal(dshare[:], dtotal[:]))
                    chain.then_wait(dve.tensor_tensor(dshare[:], dshare[:], gdec[:], ALU.mult))
                    for br, (c, m) in enumerate(((NKS, PAST + NS), (NKW, PAST + NS), (NKC, NS * NDB))):
                        last = dve.tensor_scalar(pd[:, c:c + m], pd[:, c:c + m], dshare[:, GATE[br]:GATE[br] + 1], None, ALU.mult)
                    last.then_inc(pd_ready, 1)
                    dve.wait_ge(pdT_done, 1)
                    for x, (c, m) in enumerate(chunks):
                        last = dve.tensor_copy(pdT[0:m, x], ptp[0:m, x])
                    last.then_inc(pdT_ready, 1)
                    dve.wait_ge(dout_done, 1)
                    for kv in range(KVH):
                        rows = slice(kv * HD, (kv + 1) * HD)
                        dve.tensor_copy(qT[rows, :, TP:T].rearrange("p g n -> p n g"),
                                        dout[rows].rearrange("p (n h) -> p n h", n=NS)[:, :, kv * GRP:(kv + 1) * GRP])

        sem.recycle()
        at = buf.slabs(2)
        b_hi = [at("o_hi", [P, 4, T], F32R), at("pool_hi", [P, 4, T], F32R)]
        at = buf.slabs(3)
        b_lo = [at("o_lo", [P, 4, T], F32R), at("pool_lo", [P, 4, T], F32R)]
        cut_in_place(nc, sem, "mix", [(x[:, k], a[:, k], b[:, k]) for x, a, b in zip((qT, uT), b_hi, b_lo) for k in range(4)],
                     buf.slabs(5)("cut_tmp", [P, 4, T], F32R))

        mT = buf.slabs(4)("mT", [P, KD, T])
        with ExitStack() as st:
            accs = [psum(st, f"merge_acc{s}", [P, NCH, 512]) for s in range(2)]
            g = Gemm(w, accs, sem, "merge")
            sig = buf.slabs(5, 3 * 8192)("sig", [P, T])
            prod = buf.slabs(6)("prod", [P, T])
            m_chain, up_loaded = sem("m_chain"), sem("up_loaded")
            up_nsa = w_up_nsa[0].rearrange("(h g d) n -> h d g n", h=KVH, g=GRP)
            with nc.Block() as block:

                @block.sync
                def _(sp):
                    def tile(t, first=False):
                        at_a, at_b, at_up = ((sp.snap(t * P + c) if not first else c) for c in (M_COL, M_COL + D, 0))
                        g.load(sp, columns(w_in[0], at_a), t * 2, 0, first=first)
                        if not first:
                            sp.wait_ge(g.lo_ready, t * 4)
                        for h in reversed(range(KVH)):
                            sp.dma_start(w.raw[h * HD:(h + 1) * HD, 1, 0:4], up_nsa[h, :, :, bass.ds(at_up, P)]).then_inc(up_loaded, 16)
                        g.load(sp, columns(w_in[0], at_b), t * 2 + 1, 0)
                        sp.wait_ge(g.lo_ready, t * 4 + 2)
                        sp.dma_start(w.raw[:, 1, 0:4], columns(w_up_pool[0], at_up)).then_inc(g.loaded[1], 16)

                    tile(0, first=True)
                    with sp.Fori(1, KD) as t:
                        tile(t)

                @block.scalar
                def _(act):
                    def gate(t, s):
                        act.wait_ge(g.done, t * 4 + (2 * s + 1))
                        act.wait_ge(g.freed[1], t * 2 + s) if not isinstance(t, int) or 2 * t + s > 0 else None
                        act.activation(by_chunk(sig[:]), g.out(0), ACT.Sigmoid).then_inc(g.freed[0], 1)

                    def cut(t, x, first=False):
                        if x == 1:
                            act.wait_ge(up_loaded, t * 32 + 32)
                            if not first:
                                act.wait_ge(g.done, t * 4)
                            act.activation(w.hi[:, 1, 0:4], w.raw[:, 1, 0:4], ACT.Copy).then_inc(g.hi_ready, 1)
                        elif x == 3:
                            act.wait_ge(g.loaded[1], t * 16 + 16)
                            act.wait_ge(g.done, t * 4 + 2)
                            act.activation(w.hi[:, 1, 0:4], w.raw[:, 1, 0:4], ACT.Copy).then_inc(g.hi_ready, 1)
                        else:
                            g.cut_hi(act, t * 2 + x // 2, 0, first=first)

                    cut(0, 0, first=True)
                    cut(0, 1, first=True)

                    def tile(t, more=True):
                        gate(t, 0)
                        cut(t, 2)
                        cut(t, 3)
                        gate(t, 1)
                        if more:
                            cut(t + 1, 0)
                            cut(t + 1, 1)

                    tile(0)
                    with act.Fori(1, KD - 1) as t:
                        tile(t)
                    tile(KD - 1, more=False)

                @block.gpsimd
                def _(pool):
                    with pool.Fori(0, KD) as t:
                        for j in range(2):
                            g.cut_lo(pool, t * 2 + j, 0)
                            g.cut_lo(pool, t * 2 + j, 1, k=4)

                @block.tensor
                def _(pe):
                    def tile(t, first=False):
                        g.multiply(pe, t * 2, 0, h_hi, h_lo, first=first)
                        g.multiply(pe, t * 2, 1, b_hi[0], b_lo[0], first=first, k=4)
                        g.multiply(pe, t * 2 + 1, 0, h_hi, h_lo)
                        g.multiply(pe, t * 2 + 1, 1, b_hi[1], b_lo[1], k=4)

                    tile(0, first=True)
                    with pe.Fori(1, KD) as t:
                        tile(t)

                @block.vector
                def _(dve):
                    with dve.Fori(0, KD) as t:
                        m = mT[:, bass.ds(t, 1)].rearrange("p o t -> p (o t)")
                        dve.wait_ge(g.done, t * 4 + 2)
                        dve.wait_ge(g.freed[0], t * 2 + 1)
                        dve.tensor_tensor(by_chunk(m), g.out(1), by_chunk(sig[:]), ALU.mult).then_inc(g.freed[1], 1)
                        dve.wait_ge(g.done, t * 4 + 4)
                        dve.wait_ge(g.freed[0], t * 2 + 2)
                        dve.tensor_tensor(by_chunk(prod[:]), g.out(1), by_chunk(sig[:]), ALU.mult).then_inc(g.freed[1], 1)
                        dve.wait_ge(g.freed[1], t * 2 + 2)
                        dve.tensor_tensor(m, m, prod[:], ALU.add).then_inc(m_chain, 1)
                        dve.wait_ge(m_chain, t + 1)

        m_hi = buf.slabs(0)("m_hi", [P, KD, T], F32R)
        m_lo = buf.slabs(1)("m_lo", [P, KD, T], F32R)
        cut_plain(nc, sem, "m", [(mT[:, k], m_hi[:, k], m_lo[:, k]) for k in range(KD)])

        moT = buf.slabs(2)("moT", [P, KD, T])
        dense(nc, psum, sem, w, "wo", w_o[0], m_hi, m_lo, moT)

        xT = buf.slabs(3)("xT", [P, KD, T])
        with ExitStack() as st:
            xt2 = buf.slabs(4)("xt2", [P, NB + 1, D])
            tp = [psum(st, f"x_tp{i}", [P, 512]) for i in range(2)]
            x2_loaded, xT_done, xT_taken = sem("x2_loaded"), sem("xT_done1"), sem("xT_taken1")
            with nc.Block() as block:

                @block.sync
                def _(sp):
                    sp.dma_start(xt2[:, 0:NB], x_prompt[0].rearrange("(b p) d -> p b d", p=P)).then_inc(x2_loaded, 16)
                    sp.dma_start(xt2[0:NS, NB], x_sample[:, 0, :]).then_inc(x2_loaded, 16)

                @block.tensor
                def _(pe):
                    pe.wait_ge(x2_loaded, 32)
                    for e in range(2 * KD + 1):
                        hf, k = divmod(e, KD)
                        if e >= 2:
                            pe.wait_ge(xT_taken, e - 1)
                        for b in range(4 if hf < 2 else KD):
                            if hf < 2:
                                last = pe.transpose(tp[e % 2][:, b * P:(b + 1) * P], xt2[:, 4 * hf + b, k * P:(k + 1) * P], ident[:])
                            else:
                                last = pe.transpose(tp[e % 2][:, b * NS:(b + 1) * NS], xt2[0:NS, NB, b * P:(b + 1) * P], ident[0:NS, 0:NS])
                        last.then_inc(xT_done, 1)

                @block.vector
                def _(dve):
                    for e in range(2 * KD):
                        hf, k = divmod(e, KD)
                        dve.wait_ge(xT_done, e + 1)
                        dve.tensor_copy(xT[:, k, hf * 512:(hf + 1) * 512], tp[e % 2][:]).then_inc(xT_taken, 1)
                    dve.wait_ge(xT_done, 2 * KD + 1)
                    dve.tensor_copy(xT[:, :, TP:T], tp[0][:, 0:KD * NS].rearrange("p (k n) -> p k n", k=KD)).then_inc(xT_taken, 1)

        at = buf.slabs(4)
        rstd = at("rstd", [P, T])
        mean = at("mean", [P, T])
        ntmp = at("ntmp", [P, T])
        sqr = at("sqr", [P, 2, T])
        term = at("term", [P, 2, T])
        feature_norm(nc, psum, sem, "n1", moT, sqr, ones, rstd, mean, ntmp)
        add_gated(nc, sem, "r1", xT, moT, rstd, gt1, term)

        feature_norm(nc, psum, sem, "n2", xT, sqr, ones, rstd, mean, ntmp)
        h2_hi = buf.slabs(0)("h2_hi", [P, KD, T], F32R)
        h2_lo = buf.slabs(1)("h2_lo", [P, KD, T], F32R)
        h2_ready, h2hi_ready, h2lo_ready, h2_chain, spilled = (sem(n) for n in ("h2_ready", "h2hi_ready", "h2lo_ready", "h2_chain", "spilled"))
        with nc.Block() as block:

            @block.sync
            def _(sp):
                sp.dma_start(x1_spill, xT[:]).then_inc(spilled, 16)
                sp.wait_ge(spilled, 16)

            @block.vector
            def _(dve):
                chain = Chain(dve, h2_chain)
                for k in range(KD):
                    t = term[:, k % 2]
                    if k >= 2:
                        dve.wait_ge(h2lo_ready, k - 1)
                    chain.then_wait(dve.tensor_tensor(t, xT[:, k], rstd[:], ALU.mult))
                    chain.then_wait(dve.tensor_tensor(t[:, TP:T], t[:, TP:T], sc2[:, k, 1:], ALU.mult))
                    dve.tensor_tensor(t[:, TP:T], t[:, TP:T], ada[:, 3 * KD + k, 1:], ALU.add)
                    dve.tensor_scalar(t[:, 0:TP], t[:, 0:TP], sc2[:, k, 0:1], ada[:, 3 * KD + k, 0:1], ALU.mult, ALU.add).then_inc(h2_ready, 1)

            @block.scalar
            def _(act):
                for k in range(KD):
                    act.wait_ge(h2_ready, k + 1)
                    act.activation(h2_hi[:, k], term[:, k % 2], ACT.Copy).then_inc(h2hi_ready, 1)

            @block.gpsimd
            def _(pool):
                for k in range(KD):
                    pool.wait_ge(h2hi_ready, k + 1)
                    pool.tensor_tensor(h2_lo[:, k], term[:, k % 2], h2_hi[:, k].bitcast(F32), ALU.subtract).then_inc(h2lo_ready, 1)

        f_hi = buf.slabs(2)("f_hi", [P, KD, T], F32R)
        f_lo = buf.slabs(3)("f_lo", [P, KD, T], F32R)
        fT = buf.slabs(4)("fT", [P, KD, T])
        with ExitStack() as st:
            accs = [psum(st, f"ff_acc{s}", [P, NCH, 512]) for s in range(2)]
            g = Gemm(w, accs, sem, "ff")
            relu = buf.slabs(5, 3 * 8192)("relu", [P, T])
            f32 = buf.slabs(6)("f32", [P, T])
            f_ready, fhi_ready, flo_ready, f_zeroed = (sem(n) for n in ("f_ready", "fhi_ready", "flo_ready", "f_zeroed"))
            HP = KD // 2
            with nc.Block() as block:

                @block.sync
                def _(sp):
                    def up(q, j, s, first=False):
                        g.load(sp, columns(w_ff1[0], (q * KD + 2 * j + s) * P), q * KD + j, s, first=first)

                    def down(q, j, s):
                        rows = w_ff2[0, bass.ds(q * D, D), :]
                        g.load(sp, columns(rows, (2 * j + s) * P), q * KD + HP + j, s)

                    for s in range(2):
                        up(0, 0, s, first=True)
                    with sp.Fori(1, HP) as j:
                        up(0, j, 0)
                        up(0, j, 1)
                    with sp.Fori(0, HP) as j:
                        down(0, j, 0)
                        down(0, j, 1)
                    with sp.Fori(1, NFG) as q:
                        with sp.Fori(0, HP) as j:
                            up(q, j, 0)
                            up(q, j, 1)
                        with sp.Fori(0, HP) as j:
                            down(q, j, 0)
                            down(q, j, 1)

                @block.scalar
                def _(act):
                    def hidden(q, j, s):
                        n = q * KD + j * 2 + s
                        act.wait_ge(g.freed[s], q * KD + (j + 1))
                        if s or not isinstance(j, int) or not isinstance(q, int) or q or j:
                            act.wait_ge(flo_ready, n)
                        act.activation(f32[:], relu[:], ACT.Square).then_inc(f_ready, 1)
                        act.wait_ge(f_ready, n + 1)
                        act.activation(f_hi[:, bass.ds(j * 2 + s, 1)], f32[:].unsqueeze(1), ACT.Copy).then_inc(fhi_ready, 1)

                    def pair(q, j, first=False):
                        for s in range(2):
                            g.cut_hi(act, q * KD + j, s, first=first)

                    pair(0, 0, first=True)
                    with act.Fori(1, HP) as j:
                        hidden(0, j - 1, 0)
                        g.cut_hi(act, j, 0)
                        hidden(0, j - 1, 1)
                        g.cut_hi(act, j, 1)
                    hidden(0, HP - 1, 0)
                    g.cut_hi(act, HP, 0)
                    hidden(0, HP - 1, 1)
                    g.cut_hi(act, HP, 1)
                    with act.Fori(1, HP) as j:
                        pair(0, j + HP)
                    with act.Fori(1, NFG) as q:
                        pair(q, 0)
                        with act.Fori(1, HP) as j:
                            hidden(q, j - 1, 0)
                            g.cut_hi(act, q * KD + j, 0)
                            hidden(q, j - 1, 1)
                            g.cut_hi(act, q * KD + j, 1)
                        hidden(q, HP - 1, 0)
                        g.cut_hi(act, q * KD + HP, 0)
                        hidden(q, HP - 1, 1)
                        g.cut_hi(act, q * KD + HP, 1)
                        with act.Fori(1, HP) as j:
                            pair(q, j + HP)

                @block.gpsimd
                def _(pool):
                    with pool.Fori(0, NFG * KD) as j:
                        g.cut_lo(pool, j, 0)
                        g.cut_lo(pool, j, 1)

                @block.tensor
                def _(pe):
                    def up(q, j, first=False):
                        for s in range(2):
                            g.multiply(pe, q * KD + j, s, h2_hi, h2_lo, first=first)

                    def down(q, j, peel=False):
                        for s in range(2):
                            wait = (lambda: pe.wait_ge(flo_ready, q * KD + KD)) if peel and s == 0 else None
                            if peel and s == 0:
                                pe.wait_ge(flo_ready, q * KD + (KD - 1))
                            g.multiply(pe, q * KD + HP + j, s, f_hi, f_lo, before_last=wait)

                    up(0, 0, first=True)
                    with pe.Fori(1, HP) as j:
                        up(0, j)
                    down(0, 0, peel=True)
                    with pe.Fori(1, HP) as j:
                        down(0, j)
                    with pe.Fori(1, NFG) as q:
                        with pe.Fori(0, HP) as j:
                            up(q, j)
                        down(q, 0, peel=True)
                        with pe.Fori(1, HP) as j:
                            down(q, j)

                @block.vector
                def _(dve):
                    chain = Chain(dve, f_zeroed)
                    chain.then_wait(dve.memset(fT[:], 0.0))

                    def hidden(q, j, s):
                        n = q * KD + j * 2 + s
                        dve.wait_ge(g.done, q * (2 * KD) + (j * 2 + s + 1))
                        dve.wait_ge(f_ready, n) if not (isinstance(n, int) and n == 0) else None
                        dve.tensor_scalar(by_chunk(relu[:]), g.out(s), 0.0, None, ALU.max).then_inc(g.freed[s], 1)
                        dve.wait_ge(fhi_ready, n + 1)
                        t = bass.ds(j * 2 + s, 1)
                        dve.tensor_tensor(f_lo[:, t], f32[:].unsqueeze(1), f_hi[:, t].bitcast(F32), ALU.subtract).then_inc(flo_ready, 1)

                    def collect(q, j, s):
                        dve.wait_ge(g.done, q * (2 * KD) + (j * 2 + (KD + s + 1)))
                        t = fT[:, bass.ds(j * 2 + s, 1)].rearrange("p o t -> p (o t)")
                        dve.tensor_tensor(by_chunk(t), g.out(s), by_chunk(t), ALU.add).then_inc(g.freed[s], 1)

                    for s in range(2):
                        hidden(0, 0, s)
                    with dve.Fori(1, HP) as j:
                        hidden(0, j, 0)
                        hidden(0, j, 1)
                    with dve.Fori(0, HP) as j:
                        collect(0, j, 0)
                        collect(0, j, 1)
                    with dve.Fori(1, NFG) as q:
                        with dve.Fori(0, HP) as j:
                            hidden(q, j, 0)
                            hidden(q, j, 1)
                        with dve.Fori(0, HP) as j:
                            collect(q, j, 0)
                            collect(q, j, 1)

        x1 = buf.slabs(0)("x1", [P, KD, T])
        at = buf.slabs(1)
        rstd = at("rstd2", [P, T])
        mean = at("mean2", [P, T])
        ntmp = at("ntmp2", [P, T])
        sqr = at("sqr2", [P, 2, T])
        term = at("term2", [P, 2, T])
        x1_loaded = sem("x1_loaded")
        with nc.Block() as block:

            @block.sync
            def _(sp):
                sp.dma_start(x1[:], x1_spill).then_inc(x1_loaded, 16)
                sp.wait_ge(x1_loaded, 16)

        feature_norm(nc, psum, sem, "n3", fT, sqr, ones, rstd, mean, ntmp)
        add_gated(nc, sem, "r3", x1, fT, rstd, gt2, term)
        with ExitStack() as st:
            ytok = buf.slabs(3)("ytok", [P, 3, D])
            tp = [psum(st, f"y_tp{i}", [P, D]) for i in range(3)]
            y_turned, y_taken, y_out = sem("y_turned"), sem("y_taken"), [sem(f"y_out{i}") for i in range(3)]
            with nc.Block() as block:

                @block.tensor
                def _(pe):
                    for b in range(NB + 1):
                        if b >= 3:
                            pe.wait_ge(y_taken, b - 2)
                        m = P if b < NB else NS
                        for k in range(KD):
                            last = pe.transpose(tp[b % 3][0:m, k * P:(k + 1) * P], x1[:, k, b * P:b * P + m], ident[:])
                        last.then_inc(y_turned, 1)

                def take(eng, copy, b):
                    m = P if b < NB else NS
                    eng.wait_ge(y_turned, b + 1)
                    if b >= 3:
                        eng.wait_ge(y_out[b % 3], 16 * (b // 3))
                    if b:
                        eng.wait_ge(y_taken, b)
                    copy(ytok[0:m, b % 3], tp[b % 3][0:m]).then_inc(y_taken, 1)

                @block.scalar
                def _(act):
                    for b in range(1, NB + 1, 2):
                        take(act, lambda o, i: act.activation(o, i, ACT.Copy), b)

                @block.vector
                def _(dve):
                    for b in range(0, NB + 1, 2):
                        take(dve, dve.tensor_copy, b)

                @block.sync
                def _(sp):
                    for b in range(NB + 1):
                        sp.wait_ge(y_taken, b + 1)
                        dst = y_prompt[0, b * P:(b + 1) * P, :] if b < NB else y_sample[:, 0, :]
                        sp.dma_start(dst, ytok[0:(P if b < NB else NS), b % 3]).then_inc(y_out[b % 3], 16)
                    for r in range(3):
                        sp.wait_ge(y_out[r], 16 * 3)


_INS = ["x_prompt", "x_sample", "cache_cmp_kv", "cache_sel_kv", "state_win_kv", "state_pool", "page_table",
        "c_prompt", "c_sample", "w_ada", "b_ada", "g_pre_mix", "g_post_mix", "g_pre_mlp", "g_post_mlp", "w_in",
        "w_cmp", "pos_cmp", "w_pool", "pool_scale", "w_up_nsa", "w_up_pool", "w_o", "w_ff1", "w_ff2"]
_OUTS = [((1, TP, D), "float32"), ((NS, 1, D), "float32"),
         ((1, 1, TP, 2, KVH, HD), "float32"), ((1, 1, TP, 2, KVH, HD), "float32"),
         ((1, 1, WINDOW, 2, KVH, HD), "float32"), ((1, 1, HIST, PW), "float32"),
         ((1, NS, 1, 2, KVH, HD), "float32"), ((1, NS, 1, 2, KVH, HD), "float32"),
         ((1, NS, PAST, 2, KVH, HD), "float32"), ((1, NS, HIST, PW), "float32")]


def kernel(**inputs):
    import numpy as _np
    import concourse.bacc as _bacc
    from concourse import mybir as _mybir
    from concourse.bass_utils import run_bass_kernel_spmd as _run

    nc = _bacc.Bacc("TRN2", target_bir_lowering=False, num_devices=1)
    arrays, args = {}, []
    for name in _INS:
        a = _np.ascontiguousarray(inputs[name])
        arrays[f"in_{name}_dram"] = a
        args.append(nc.dram_tensor(f"in_{name}_dram", a.shape, _mybir.dt.from_np(a.dtype), kind="ExternalInput").ap())
    for i, (shape, dtype) in enumerate(_OUTS):
        dt = _mybir.dt.from_np(_np.dtype(dtype))
        args.append(nc.dram_tensor(f"out_{i}_dram", shape, dt, kind="ExternalOutput").ap())
    hybrid_step(nc, *args)
    r = _run(nc, [arrays], core_ids=[0])
    return tuple(r.results[0][f"out_{i}_dram"] for i in range(len(_OUTS)))
```

```python
from contextlib import ExitStack

import concourse.bass as bass
from concourse import mybir

F32 = mybir.dt.float32
F32R = mybir.dt.float32r
BF16 = mybir.dt.bfloat16
I32 = mybir.dt.int32
ACT = mybir.ActivationFunctionType
ALU = mybir.AluOpType
AX = mybir.AxisListType

P = 128
D = 1024
KD = D // P
TP = 1024
NS = 8
T = TP + NS
NB = TP // P
NCH = 3
CH = T // NCH
HEADS, KVH, GRP, HD = 8, 2, 4, 64
BLOCK = 64
WINDOW = 512
WB = WINDOW // P
PAST = 256
PAGE = 128
NPG = PAST // PAGE
NPHYS = 20
NCB = TP // BLOCK
NDB = PAST // BLOCK
NCAT = NCB + NS * NDB + 1
Q_COL, KV_COL, G_COL, U_COL, M_COL = 0, 512, 1280, 1304, 1816
PW = 512
HIST = 15
FF = 4096
NFG = FF // D
EPS = 1e-6
SCALE = HD ** -0.5
MASKED = -1e30
MAX_FLOOR = -1e20
R = NS * HEADS
VB_ADA, VG_PRE_MIX, VG_POST_MIX, VG_PRE_MLP, VG_POST_MLP, V_POOL, NVEC = 0, 48, 56, 64, 72, 80, 84

NEWTON_STEPS = 4


def newton(dve, chain, y, v, t):
    chain.then_wait(dve.scalar_tensor_tensor(t, y, -0.5, y, ALU.mult, ALU.mult))
    chain.then_wait(dve.tensor_tensor(t, t, v, ALU.mult))
    chain.then_wait(dve.scalar_tensor_tensor(y, t, 1.5, y, ALU.add, ALU.mult))


class Chain:

    def __init__(self, eng, sem):
        self.eng, self.sem, self.n = eng, sem, 0

    def then_wait(self, ins):
        self.n += 1
        ins.then_inc(self.sem, 1)
        self.eng.wait_ge(self.sem, self.n)


class Buffers:

    SLAB = KD * T * 4
    CONSTS = 7424

    def __init__(self, nc):
        self.nc = nc
        self.base = (nc.sbuf_base + 31) // 32 * 32
        self.end = nc.sbuf_usable_end
        self.consts = 0
        self.tail = self.CONSTS + 6 * self.SLAB

    def at(self, name, shape, dt, offset):
        size = 2 if dt == BF16 else 4
        for n in shape[1:]:
            size *= n
        assert self.base + offset + size <= self.end, (name, self.base + offset + size - self.end)
        return self.nc.alloc_sbuf_tensor_at(name, shape, dt, offset=self.base + offset), offset + (size + 31) // 32 * 32

    def const(self, name, shape, dt=F32):
        t, self.consts = self.at(name, shape, dt, self.consts)
        assert self.consts <= self.CONSTS, self.consts
        return t

    def small(self, name, shape, dt=F32):
        t, self.tail = self.at(name, shape, dt, self.tail)
        return t

    def slabs(self, first, start=0):
        at = [self.CONSTS + first * self.SLAB + start]

        def place(name, shape, dt=F32):
            t, at[0] = self.at(name, shape, dt, at[0])
            return t

        place.at = at
        return place


class Semaphores:

    def __init__(self, nc):
        self.nc, self.used = nc, []

    def __call__(self, name):
        self.used.append(self.nc.alloc_semaphore(name=name))
        return self.used[-1]

    def recycle(self):
        self.nc.clear_and_free_semaphores(self.used)
        self.nc.all_engine_barrier()
        self.used = []


class Weights:

    def __init__(self, place):
        self.raw = place("w_raw", [P, 2, KD, P])
        self.hi = place("w_hi", [P, 2, KD, P], F32R)
        self.lo = place("w_lo", [P, 2, KD, P], F32R)


class Gemm:

    def __init__(self, w, accs, sem, name, parts=1):
        self.w, self.accs, self.parts = w, accs, parts
        self.loaded = [sem(f"{name}_w_loaded{s}") for s in range(2)]
        self.hi_ready = sem(f"{name}_w_hi_ready")
        self.lo_ready = sem(f"{name}_w_lo_ready")
        self.done = sem(f"{name}_products_done")
        self.freed = [sem(f"{name}_acc_freed{s}") for s in range(2)]

    def load(self, sp, src, j, s, first=False):
        if not first:
            sp.wait_ge(self.lo_ready, j * 2 + (s - 1))
        if self.parts == 1:
            sp.dma_start(self.w.raw[:, s, 0:src.shape[1]], src).then_inc(self.loaded[s], 16)
        else:
            for h in range(2):
                sp.dma_start(self.w.raw[:, s, :, h * HD:(h + 1) * HD], src[h]).then_inc(self.loaded[s], 16)

    def cut_hi(self, act, j, s, first=False, k=KD):
        act.wait_ge(self.loaded[s], (j * 16 + 16) * self.parts)
        if not first:
            act.wait_ge(self.done, j * 2 + (s - 1))
        act.activation(self.w.hi[:, s, 0:k], self.w.raw[:, s, 0:k], ACT.Copy).then_inc(self.hi_ready, 1)

    def cut_lo(self, pool, j, s, k=KD):
        pool.wait_ge(self.hi_ready, j * 2 + (s + 1))
        pool.tensor_tensor(self.w.lo[:, s, 0:k], self.w.raw[:, s, 0:k], self.w.hi[:, s, 0:k].bitcast(F32),
                           ALU.subtract).then_inc(self.lo_ready, 1)

    def begin(self, srcs):
        def load(sp):
            for s, src in enumerate(srcs):
                self.load(sp, src, 0, s, first=True)

        def hi(act):
            for s in range(2):
                self.cut_hi(act, 0, s, first=True)

        def lo(pool):
            for s in range(2):
                self.cut_lo(pool, 0, s)

        return load, hi, lo

    def multiply(self, pe, j, s, x_hi, x_lo, first=False, k=KD, before_last=None, before=None):
        pe.wait_ge(self.lo_ready, j * 2 + (s + 1))
        if not first:
            pe.wait_ge(self.freed[s], j * 1)
        for kk in range(k):
            if before is not None:
                before(kk)
            if before_last is not None and kk == k - 1:
                before_last()
            for n, (w, x) in enumerate(((self.w.hi, x_hi), (self.w.hi, x_lo), (self.w.lo, x_hi))):
                for c in range(NCH):
                    last = pe.matmul(self.accs[s][:, c, 0:CH], w[:, s, kk], x[:, kk, c * CH:(c + 1) * CH],
                                     start=(kk == 0 and n == 0), stop=(kk == k - 1 and n == 2))
        last.then_inc(self.done, 1)

    def out(self, s):
        return self.accs[s][:, :, 0:CH]


def by_chunk(x):
    return x.rearrange("p (c t) -> p c t", c=NCH)


def columns_of(w, n, count):
    return w.rearrange("(k p) n -> p k n", p=P)[:, :, n:n + count]


def columns(w, n):
    return w.rearrange("(k p) n -> p k n", p=P)[:, :, bass.ds(n, P)]



def finish_norm(dve, chain, acc, summed, count, mean, mean_ready, rstd, root_ready, tmp):
    dve.wait_ge(summed, count)
    dve.tensor_scalar(by_chunk(mean[:]), acc[:, :, 0:CH], 1.0 / D, EPS, ALU.mult, ALU.add).then_inc(mean_ready, 1)
    dve.wait_ge(root_ready, 1)
    chain.then_wait(dve.reciprocal(rstd[:], rstd[:]))
    newton(dve, chain, rstd[:], mean[:], tmp[:])


def add_term(dve, chain, x, t, gate, c, e):
    if e == T:
        chain.then_wait(dve.tensor_tensor(t[:, TP:T], t[:, TP:T], gate[:, 1:], ALU.mult))
        dve.tensor_tensor(x[:, TP:T], x[:, TP:T], t[:, TP:T], ALU.add)
    e = min(e, TP)
    return dve.scalar_tensor_tensor(x[:, c:e], t[:, c:e], gate[:, 0:1], x[:, c:e], ALU.mult, ALU.add)


def hybrid_step(nc, x_prompt, x_sample, cache_cmp_kv, cache_sel_kv, state_win_kv, state_pool, page_table,
                c_prompt, c_sample, w_ada, b_ada, g_pre_mix, g_post_mix, g_pre_mlp, g_post_mlp, w_in,
                w_cmp, pos_cmp, w_pool, pool_scale, w_up_nsa, w_up_pool, w_o, w_ff1, w_ff2,
                y_prompt, y_sample, n_cmp_p, n_sel_p, n_win_p, n_pool_p, n_cmp_s, n_sel_s, n_win_s, n_pool_s):
    with ExitStack() as root:
        sem = Semaphores(nc)
        buf = Buffers(nc)

        def psum(st, name, shape):
            return st.enter_context(nc.psum_tensor(name, shape, F32))

        ident = buf.const("ident", [P, P])
        identb = buf.const("identb", [P, P], BF16)
        ones = buf.const("ones", [P, P])
        causal = buf.const("causal", [P, P], BF16)
        behind = buf.const("behind", [P, P], BF16)
        cmask = buf.const("cmask", [P, NB, NCB], BF16)
        dmask = buf.const("dmask", [R, NS], BF16)
        dcmask = buf.const("dcmask", [R, NS, NDB], BF16)
        invcnt = buf.const("invcnt", [P, 4, 16])
        vecs = buf.const("vecs", [P, NVEC])
        sc1, gt1, sc2, gt2 = (buf.const(n, [P, KD, 1 + NS]) for n in ("sc1", "gt1", "sc2", "gt2"))
        ada = buf.const("ada", [P, 6 * KD, 1 + NS])
        gtok = buf.const("gtok", [P, NB, 24])
        gdec8 = buf.const("gdec8", [NS, 24])
        gdec = buf.const("gdec", [R, 3])
        x1_spill = nc.dram_tensor("x1_spill", [P, KD, T], F32, kind="Internal").ap()
        w = Weights(buf.slabs(5))

        h_hi = buf.slabs(0)("h_hi", [P, KD, T], F32R)
        h_lo = buf.slabs(1)("h_lo", [P, KD, T], F32R)

        gin = Gemm(w, None, sem, "in", parts=2)
        wq = w_in[0, :, Q_COL:KV_COL].rearrange("(k p) (h c) -> p k h c", p=P, h=KVH)
        q_weights = [[wq[:, :, h, u * HD:(u + 1) * HD] for h in range(KVH)] for u in range(GRP)]
        in_load, in_hi, in_lo = gin.begin(q_weights[0:2])

        AC = 256
        cT = buf.const("cT", [P, KD, 1 + NS])
        with ExitStack() as st:
            at = buf.slabs(2)
            xt = at("xt", [P, NB + 1, D])
            NR = 4
            wa = at("wa", [P, NR, KD, AC])
            NA = 2 * D // AC
            htmp = at("htmp", [P, 4, 512])
            arow = at("arow", [1 + NS, 2 * D])
            sq = at("sq", [P, D])
            vrow = at("vrow", [NVEC, P])
            crow = at("crow", [1 + NS, D])
            csig = at("csig", [1 + NS, D])
            ss, ms, rs, rt = (at(n, [P, NB + 1]) for n in ("ss", "ms", "rs", "rt"))
            iot = at("iot", [P, 16])
            tp = [psum(st, f"tp{i}", [P, 512]) for i in range(3)]
            adaP = [psum(st, f"adaP{i}", [1 + NS, AC]) for i in range(2)]
            vec_loaded, c_loaded, xs_loaded = sem("vec_loaded"), sem("c_loaded"), sem("xs_loaded")
            x_loaded = [sem(f"x_loaded{b}") for b in range(NB // 2)]
            wa_loaded = [sem(f"wa_loaded{r}") for r in range(NR)]
            zeroed, consts_ready, pool_chain = sem("zeroed"), sem("consts_ready"), sem("pool_chain0")
            csig_ready, silu_ready, cT_done, cT_ready = sem("csig_ready"), sem("silu_ready"), sem("cT_done"), sem("cT_ready")
            vT_done, ada_done, arow_ready, adaT_done = sem("vT_done"), sem("ada_done"), sem("arow_ready"), sem("adaT_done")
            squares_ready, ms_ready, root_ready, x_scaled = sem("squares_ready"), sem("ms_ready"), sem("root_ready"), sem("x_scaled")
            xT_done, h_ready, hhi_ready, hlo_ready, hlo_odd = (sem(n) for n in ("xT_done0", "h_ready", "hhi_ready", "hlo_ready", "hlo_odd"))
            dve_chain, act_chain = sem("dve_chain0"), sem("act_chain0")

            def vec(at_row):
                return vecs[:, at_row:at_row + KD].unsqueeze(2).broadcast_to([P, KD, 1 + NS])

            with nc.Block() as block:

                @block.sync
                def _(sp):
                    sp.dma_start(crow[0:1, :], c_prompt).then_inc(c_loaded, 16)
                    sp.dma_start(crow[1:1 + NS, :], c_sample).then_inc(c_loaded, 16)
                    for at_row, v in ((VB_ADA, b_ada), (VG_PRE_MIX, g_pre_mix), (VG_POST_MIX, g_post_mix),
                                      (VG_PRE_MLP, g_pre_mlp), (VG_POST_MLP, g_post_mlp), (V_POOL, pool_scale)):
                        v = v[0].rearrange("(r p) -> r p", p=P)
                        sp.dma_start(vrow[at_row:at_row + v.shape[0], :], v).then_inc(vec_loaded, 16)
                    for c in range(NA):
                        if c >= NR:
                            sp.wait_ge(ada_done, c - NR + 1)
                        sp.dma_start(wa[:, c % NR], columns_of(w_ada[0], c * AC, AC)).then_inc(wa_loaded[c % NR], 16)
                    in_load(sp)

                @block.scalar
                def _(act):
                    xb = x_prompt[0].rearrange("(b p) d -> p b d", p=P)
                    for b in range(0, NB, 2):
                        act.dma_start(xt[:, b:b + 2], xb[:, b:b + 2]).then_inc(x_loaded[b // 2], 16)
                    act.dma_start(xt[0:NS, NB], x_sample[:, 0, :]).then_inc(xs_loaded, 16)
                    act.wait_ge(c_loaded, 32)
                    act.activation(csig[:], crow[:], ACT.Sigmoid).then_inc(csig_ready, 1)
                    act.wait_ge(zeroed, 1)
                    chain = Chain(act, act_chain)
                    for b in range(NB):
                        if b % 2 == 0:
                            act.wait_ge(x_loaded[b // 2], 16)
                        chain.then_wait(act.activation(sq[:], xt[:, b], ACT.Square, accum_out=ss[:, b:b + 1]))
                    act.wait_ge(xs_loaded, 16)
                    act.activation(sq[0:NS], xt[0:NS, NB], ACT.Square, accum_out=ss[0:NS, NB:NB + 1]).then_inc(squares_ready, 1)
                    act.wait_ge(ms_ready, 1)
                    act.activation(rt[:], ms[:], ACT.Sqrt).then_inc(root_ready, 1)
                    in_hi(act)
                    for e in range(2 * KD):
                        act.wait_ge(h_ready, e + 1)
                        hf, k = divmod(e, KD)
                        act.activation(h_hi[:, k, hf * 512:(hf + 1) * 512], htmp[:, e % 4], ACT.Copy).then_inc(hhi_ready, 1)
                    act.wait_ge(h_ready, 2 * KD + 1)
                    act.activation(h_hi[:, :, TP:T], htmp[:, 0, 0:KD * NS].rearrange("p (k n) -> p k n", k=KD),
                                   ACT.Copy).then_inc(hhi_ready, 1)

                @block.gpsimd
                def _(pool):
                    chain = Chain(pool, pool_chain)
                    pool.memset(ss[:], 1.0).then_inc(zeroed, 1)
                    pool.memset(ident[:], 0.0)
                    pool.memset(ones[:], 1.0)
                    for m in (causal, behind, cmask, dmask):
                        pool.memset(m[:], 0.0)
                    chain.then_wait(pool.memset(dcmask[:], 0.0))
                    pool.affine_select(out=ident[:], in_=ident[:], compare_op=ALU.not_equal, fill=1.0, base=0,
                                       pattern=[[-1, P]], channel_multiplier=1)
                    pool.affine_select(out=causal[:], in_=causal[:], compare_op=ALU.is_ge, fill=MASKED, base=0,
                                       pattern=[[-1, P]], channel_multiplier=1)
                    pool.affine_select(out=behind[:], in_=behind[:], compare_op=ALU.is_gt, fill=MASKED, base=0,
                                       pattern=[[1, P]], channel_multiplier=-1)
                    pool.affine_select(out=cmask[:], in_=cmask[:], compare_op=ALU.is_ge, fill=MASKED, base=-(BLOCK - 1),
                                       pattern=[[P, NB], [-BLOCK, NCB]], channel_multiplier=1)
                    pool.affine_select(out=dmask[:], in_=dmask[:], compare_op=ALU.is_ge, fill=MASKED, base=0,
                                       pattern=[[-HEADS, NS]], channel_multiplier=1)
                    chain.then_wait(pool.affine_select(out=dcmask[:], in_=dcmask[:], compare_op=ALU.is_ge, fill=MASKED,
                                    base=0, pattern=[[-HEADS, NS], [0, NDB]], channel_multiplier=1))
                    pool.affine_select(out=dmask[:], in_=dmask[:], compare_op=ALU.is_ge, fill=MASKED, base=HEADS - 1,
                                       pattern=[[HEADS, NS]], channel_multiplier=-1)
                    pool.affine_select(out=dcmask[:], in_=dcmask[:], compare_op=ALU.is_ge, fill=MASKED, base=HEADS - 1,
                                       pattern=[[HEADS, NS], [0, NDB]], channel_multiplier=-1)
                    pool.iota(iot[:], pattern=[[1, 16]], base=1, channel_multiplier=0, allow_small_or_imprecise_dtypes=True)
                    chain.then_wait(pool.tensor_copy(identb[:], ident[:]))
                    for g in range(4):
                        last = pool.tensor_scalar(invcnt[:, g], iot[:], float(2 << g), None, ALU.min)
                    last.then_inc(consts_ready, 1)
                    in_lo(pool)
                    for e in range(0, 2 * KD, 2):
                        pool.wait_ge(hhi_ready, e + 1)
                        hf, k = divmod(e, KD)
                        c = slice(hf * 512, (hf + 1) * 512)
                        pool.tensor_tensor(h_lo[:, k, c], htmp[:, e % 4], h_hi[:, k, c].bitcast(F32), ALU.subtract)\
                            .then_inc(hlo_ready, 1)
                    pool.wait_ge(hhi_ready, 2 * KD + 1)
                    pool.tensor_tensor(h_lo[:, :, TP:T], htmp[:, 0, 0:KD * NS].rearrange("p (k n) -> p k n", k=KD),
                                       h_hi[:, :, TP:T].bitcast(F32), ALU.subtract).then_inc(hlo_ready, 1)

                @block.tensor
                def _(pe):
                    pe.wait_ge(consts_ready, 1)
                    pe.wait_ge(vec_loaded, 96)
                    pe.transpose(tp[1][:, 0:NVEC], vrow[:], ident[0:NVEC, 0:NVEC]).then_inc(vT_done, 1)
                    pe.wait_ge(silu_ready, 1)
                    for k in range(KD):
                        last = pe.transpose(tp[0][:, k * 16:k * 16 + 1 + NS], crow[:, k * P:(k + 1) * P], ident[0:1 + NS, 0:1 + NS])
                    last.then_inc(cT_done, 1)
                    pe.wait_ge(cT_ready, 1)

                    def condition(c):
                        pe.wait_ge(wa_loaded[c % NR], 16 * (c // NR + 1))
                        if c >= 2:
                            pe.wait_ge(arow_ready, c - 1)
                        for k in range(KD):
                            last = pe.matmul(adaP[c % 2][:], cT[:, k], wa[:, c % NR, k], start=(k == 0), stop=(k == KD - 1))
                        last.then_inc(ada_done, 1)

                    for c in range(NA):
                        condition(c)
                    pe.wait_ge(arow_ready, NA)
                    for n in range(2 * KD):
                        last = pe.transpose(tp[0][:, n * 16:n * 16 + 1 + NS], arow[:, n * P:(n + 1) * P], ident[0:1 + NS, 0:1 + NS])
                    last.then_inc(adaT_done, 1)
                    pe.wait_ge(x_scaled, 1)
                    for e in range(2 * KD):
                        hf, k = divmod(e, KD)
                        if e >= 2:
                            pe.wait_ge(h_ready, e - 1)
                        for b in range(4):
                            last = pe.transpose(tp[1 + e % 2][:, b * P:(b + 1) * P], xt[:, 4 * hf + b, k * P:(k + 1) * P], ident[:])
                        last.then_inc(xT_done, 1)
                    pe.wait_ge(h_ready, 1)
                    for k in range(KD):
                        last = pe.transpose(tp[0][:, k * NS:(k + 1) * NS], xt[0:NS, NB, k * P:(k + 1) * P], ident[0:NS, 0:NS])
                    last.then_inc(xT_done, 1)

                @block.vector
                def _(dve):
                    chain = Chain(dve, dve_chain)
                    dve.wait_ge(csig_ready, 1)
                    dve.tensor_tensor(crow[:], crow[:], csig[:], ALU.mult).then_inc(silu_ready, 1)
                    dve.wait_ge(vT_done, 1)
                    dve.tensor_copy(vecs[:], tp[1][:, 0:NVEC])
                    dve.wait_ge(cT_done, 1)
                    dve.tensor_copy(cT[:], tp[0][:, 0:KD * 16].rearrange("p (k n) -> p k n", k=KD)[:, :, 0:1 + NS]).then_inc(cT_ready, 1)
                    dve.wait_ge(consts_ready, 1)
                    dve.reciprocal(invcnt[:], invcnt[:])
                    dve.wait_ge(squares_ready, 1)
                    dve.tensor_scalar(ms[:], ss[:], 1.0 / D, EPS, ALU.mult, ALU.add).then_inc(ms_ready, 1)
                    dve.wait_ge(root_ready, 1)
                    chain.then_wait(dve.reciprocal(rs[:], rt[:]))
                    newton(dve, chain, rs[:], ms[:], rt[:])
                    for b in range(NB):
                        dve.tensor_scalar(xt[:, b], xt[:, b], rs[:, b:b + 1], None, ALU.mult)
                    dve.tensor_scalar(xt[0:NS, NB], xt[0:NS, NB], rs[0:NS, NB:NB + 1], None, ALU.mult).then_inc(x_scaled, 1)
                    for c in range(NA):
                        dve.wait_ge(ada_done, c + 1)
                        dve.tensor_copy(arow[:, c * AC:(c + 1) * AC], adaP[c % 2][:]).then_inc(arow_ready, 1)
                    dve.wait_ge(adaT_done, 1)
                    chain.then_wait(dve.tensor_tensor(ada[:, 0:2 * KD], tp[0][:, 0:2 * KD * 16].rearrange("p (n c) -> p n c", c=16)[:, :, 0:1 + NS], vecs[:, 0:2 * KD].unsqueeze(2).broadcast_to([P, 2 * KD, 1 + NS]), ALU.add))
                    chain.then_wait(dve.scalar_tensor_tensor(sc1[:], ada[:, KD:2 * KD], 1.0, vec(VG_PRE_MIX), ALU.add, ALU.mult))

                    def cut_odd(e):
                        hf, k = divmod(e, KD)
                        c = slice(hf * 512, (hf + 1) * 512)
                        dve.wait_ge(hhi_ready, e + 1)
                        dve.tensor_tensor(h_lo[:, k, c], htmp[:, e % 4], h_hi[:, k, c].bitcast(F32), ALU.subtract)\
                           .then_inc(hlo_odd, 1)

                    for e in range(2 * KD):
                        k = e % KD
                        dve.wait_ge(xT_done, e + 1)
                        if e >= 4:
                            dve.wait_ge(hlo_odd if e % 2 else hlo_ready, (e - 4) // 2 + 1)
                        dve.tensor_scalar(htmp[:, e % 4], tp[1 + e % 2][:], sc1[:, k, 0:1], ada[:, k, 0:1],
                                          ALU.mult, ALU.add).then_inc(h_ready, 1)
                        if e % 2 == 0 and e:
                            cut_odd(e - 1)
                    cut_odd(2 * KD - 1)
                    dve.wait_ge(xT_done, 2 * KD + 1)
                    dve.wait_ge(hlo_ready, KD - 1)
                    hd = htmp[:, 0, 0:KD * NS].rearrange("p (k n) -> p k n", k=KD)
                    chain.then_wait(dve.tensor_tensor(hd, tp[0][:, 0:KD * NS].rearrange("p (k n) -> p k n", k=KD),
                                                      sc1[:, :, 1:], ALU.mult))
                    dve.tensor_tensor(hd, hd, ada[:, 0:KD, 1:], ALU.add).then_inc(h_ready, 1)

        at = buf.slabs(2)
        qT = at("qT", [P, GRP, T])
        uT = at("uT", [P, 4, T])
        catT = at("catT", [P, 2, NCAT * BLOCK])
        kvT = at("kvT", [P, 4, T])
        gT = at("gT", [24, T])
        cnewT = at("cnewT", [P, 2, NS])
        scratch3 = at.at[0] - buf.CONSTS - 3 * buf.SLAB
        with ExitStack() as st:
            accs = [psum(st, f"in_acc{s}", [P, NCH, 512]) for s in range(2)]
            g = gin
            g.accs = accs
            NU = 15
            NA = 4 * D // AC
            wa = at("wa_rest", [P, 2, KD, AC])
            adaP = [psum(st, f"ada_rest{s}", [P, AC // P, 1 + NS]) for s in range(2)]
            wa_loaded = [sem(f"wa_rest_loaded{s}") for s in range(2)]
            ada_done, ada_taken = sem("ada_rest_done"), [sem(f"ada_rest_taken{s}") for s in range(2)]

            def condition(pe, j, s, first=False):
                pe.wait_ge(wa_loaded[s], j * 16 + 16)
                if not first:
                    pe.wait_ge(ada_taken[s], j)
                for n in range(AC // P):
                    for k in range(KD):
                        last = pe.matmul(adaP[s][:, n], wa[:, s, k, n * P:(n + 1) * P], cT[:, k], start=(k == 0), stop=(k == KD - 1))
                last.then_inc(ada_done, 1)

            with nc.Block() as block:

                def load_ada(sp, c):
                    if c >= 2:
                        sp.wait_ge(ada_done, c - 1)
                    sp.dma_start(wa[:, c % 2], columns_of(w_ada[0], 2 * D + c * AC, AC)).then_inc(wa_loaded[c % 2], 16)

                @block.sync
                def _(sp):
                    load_ada(sp, 0)
                    load_ada(sp, 1)
                    for u in range(2, NU):
                        j, s = divmod(u, 2)
                        if u < GRP:
                            src = q_weights[u]
                        else:
                            c = KV_COL + (u - 4) * P if u < 10 else G_COL if u == 10 else U_COL + (u - 11) * P
                            src = [columns(w_in[0], c)[:, :, h * HD:(h + 1) * HD] for h in range(2)]
                        g.load(sp, src, j, s)
                        load_ada(sp, u)
                    load_ada(sp, NU)

                @block.scalar
                def _(act):
                    with act.Fori(1, NU // 2) as j:
                        g.cut_hi(act, j, 0)
                        g.cut_hi(act, j, 1)
                    g.cut_hi(act, NU // 2, 0)

                @block.gpsimd
                def _(pool):
                    with pool.Fori(1, NU // 2) as j:
                        g.cut_lo(pool, j, 0)
                        g.cut_lo(pool, j, 1)
                    g.cut_lo(pool, NU // 2, 0)

                @block.tensor
                def _(pe):
                    for s in range(2):
                        g.multiply(pe, 0, s, h_hi, h_lo, first=True)
                        condition(pe, 0, s, first=True)
                    with pe.Fori(1, NU // 2) as j:
                        for s in range(2):
                            g.multiply(pe, j, s, h_hi, h_lo)
                            condition(pe, j, s)
                    g.multiply(pe, NU // 2, 0, h_hi, h_lo)
                    condition(pe, NU // 2, 0)
                    condition(pe, NU // 2, 1)

                @block.vector
                def _(dve):
                    def take_ada(c):
                        at_c, n = 2 * KD + c * AC // P, AC // P
                        dve.wait_ge(ada_done, c + 1)
                        dve.tensor_tensor(ada[:, at_c:at_c + n], adaP[c % 2][:],
                                          vecs[:, at_c:at_c + n].unsqueeze(2).broadcast_to([P, n, 1 + NS]), ALU.add)\
                           .then_inc(ada_taken[c % 2], 1)

                    for u in range(NU):
                        j, s = divmod(u, 2)
                        dve.wait_ge(g.done, u + 1)
                        if u in (4, 5):
                            k = u - 4
                            dve.tensor_copy(catT[:, k, 0:2 * CH].rearrange("p (c t) -> p c t", c=2), accs[s][:, 0:2, 0:CH])
                            dve.tensor_copy(catT[:, k, 2 * CH:TP], accs[s][:, 2, 0:TP - 2 * CH])
                            last = dve.tensor_copy(cnewT[:, k], accs[s][:, 2, TP - 2 * CH:CH])
                        elif u == 10:
                            last = dve.tensor_copy(by_chunk(gT[:]), accs[s][0:24, :, 0:CH])
                        else:
                            dst = qT[:, u] if u < 4 else kvT[:, u - 6] if u < 10 else uT[:, u - 11]
                            last = dve.tensor_copy(by_chunk(dst), g.out(s))
                        last.then_inc(g.freed[s], 1)
                        take_ada(u)
                    take_ada(NU)
                    dve.wait_ge(ada_taken[0], NA // 2)
                    dve.wait_ge(ada_taken[1], NA // 2)
                    dve.tensor_tensor(gt1[:], ada[:, 2 * KD:3 * KD], vec(VG_POST_MIX), ALU.mult)
                    dve.scalar_tensor_tensor(sc2[:], ada[:, 4 * KD:5 * KD], 1.0, vec(VG_PRE_MLP), ALU.add, ALU.mult)
                    dve.tensor_tensor(gt2[:], ada[:, 5 * KD:6 * KD], vec(VG_POST_MLP), ALU.mult)

        at = buf.slabs(5)
        kT_hi = at("kT_hi", [P, 2, T], F32R)
        kT_lo = at("kT_lo", [P, 2, T], F32R)
        v_hi = at("v_hi", [P, 2, NB, P], F32R)
        v_lo = at("v_lo", [P, 2, NB, P], F32R)
        kcT = buf.small("kcT", [P, 2, NCAT])
        kc_hi = buf.small("kc_hi", [P, NCB], F32R)
        kc_lo = buf.small("kc_lo", [P, NCB], F32R)
        vc_hi = buf.small("vc_hi", [NCB, P], F32R)
        vc_lo = buf.small("vc_lo", [NCB, P], F32R)
        vc_dec = buf.small("vc_dec", [NS * NDB, P])
        v_new = buf.small("v_new", [NS, 2, P])
        knew = buf.const("knew", [P, 2, NS])
        with ExitStack() as st:
            at = buf.slabs(3, scratch3)
            JC = 8
            NWC = BLOCK // JC
            RWC = 2
            wc = at("wc", [P, RWC, JC, P])

            def load_wc(eng, h, q):
                if q < RWC:
                    eng.wait_ge(wc_zeroed, 1)
                else:
                    eng.wait_ge(wc_used, q - RWC + 1)
                s, c = divmod(q, NWC)
                eng.dma_start(wc[h * HD:(h + 1) * HD, q % RWC, :, h * HD:(h + 1) * HD], w_cmp[0, s, c * JC:(c + 1) * JC].rearrange("j d e -> d j e"))\
                   .then_inc(wc_loaded[q % RWC], 16)

            ck = at("ck", [P, 2, NPG, 2 * P])
            tok = at("tok", [P, 2, 6 * P])
            behind_all = buf.tail
            posd = buf.small("posd", [BLOCK, 2, KVH, HD])
            tp = [psum(st, f"sh_tp{i}", [P, 1024]) for i in range(2)]
            cps = psum(st, "cps", [NCAT, 2, P])
            crows = at("crows", [NCAT, 2, P])
            pos_loaded, ck_loaded = sem("pos_loaded"), [sem(f"ck_loaded{i}") for i in range(2)]
            wc_zeroed, wc_loaded = sem("wc_zeroed"), [sem(f"wc_loaded{i}") for i in range(RWC)]
            tp_done, tp_taken, wc_used = sem("tp_done"), sem("tp_taken"), sem("wc_used")
            gates_ready, rows_out, small_out = sem("gates_ready"), [sem(f"rows_out{i}") for i in range(2)], sem("small_out")
            vhi_ready, vlo_ready, khi_ready, klo_ready = sem("vhi_ready"), sem("vlo_ready"), sem("khi_ready"), sem("klo_ready")
            kc_done, kc_ready, kchi_ready, kclo_ready, vchi_ready = (sem(n) for n in ("kc_done", "kc_ready", "kchi_ready", "kclo_ready", "vchi_ready"))
            crows_ready, crows_turned, dchain, page_loaded = (sem(n) for n in ("crows_ready", "crows_turned", "dve_chain1", "page_loaded"))
            pt_sb = buf.const("pt_sb", [1, NS * NPG], I32)
            E_POS, E_GATE, E_TOK, E_CK = 0, 1, [2 + 2 * b for b in range(NB)], [3 + 2 * n for n in range(NS)]
            E_NEW, E_U, E_UNEW, E_VC = 18, 19, 20, 21
            utok = buf.small("utok", [HIST, PW])
            with nc.Block() as block:

                @block.sync
                def _(sp):
                    sp.dma_start(pt_sb[:], page_table.rearrange("n (o g) -> o (n g)", o=1)).then_inc(page_loaded, 16)
                    for h in range(KVH):
                        sp.dma_start(posd[:, :, h], pos_cmp[0]).then_inc(pos_loaded, 16)
                    for q in range(RWC):
                        load_wc(sp, 1, q)
                    sp.wait_ge(page_loaded, 16)
                    for n in range(NS):
                        if n >= 2:
                            sp.wait_ge(tp_done, E_CK[n - 2] + 1)
                        for g in range(NPG):
                            page = sp.value_load(pt_sb[0:1, n * NPG + g:n * NPG + g + 1], min_val=0, max_val=NPHYS - 1)
                            sp.dma_start(ck[:, n % 2, g], cache_cmp_kv[0].rearrange("n s a h d -> n s (a h d)")[bass.ds(page, 1)]
                                         .rearrange("n s c -> (n s) c")).then_inc(ck_loaded[n % 2], 16)
                    for q in range(RWC, 2 * NWC):
                        load_wc(sp, 1, q)
                    sp.wait_ge(small_out, 16 * 7)

                @block.gpsimd
                def _(pool):
                    pool.memset(wc[:], 0.0).then_inc(wc_zeroed, 1)
                    pool.wait_ge(khi_ready, 1)
                    for s in range(2):
                        last = pool.tensor_tensor(kT_lo[:, s], kvT[:, 2 * s], kT_hi[:, s].bitcast(F32), ALU.subtract)
                    last.then_inc(klo_ready, 1)
                    for b in range(NB):
                        pool.wait_ge(vhi_ready, b + 1)
                        t = tok[:, b % 2].rearrange("p (a s c) -> p a s c", a=3, s=2)[:, 1:3, 1]
                        pool.tensor_tensor(v_lo[:, :, b], t, v_hi[:, :, b].bitcast(F32), ALU.subtract).then_inc(vlo_ready, 1)

                @block.scalar
                def _(act):
                    for q in range(RWC):
                        load_wc(act, 0, q)
                    act.activation(gT[:], gT[:], ACT.Sigmoid).then_inc(gates_ready, 1)
                    for s in range(2):
                        last = act.activation(kT_hi[:, s], kvT[:, 2 * s], ACT.Copy)
                    last.then_inc(khi_ready, 1)
                    act.activation(knew[:], kvT[:].rearrange("p (b s) t -> p b s t", b=2)[:, :, 0, TP:T], ACT.Copy)
                    for b in range(NB):
                        act.wait_ge(tp_taken, E_TOK[b] + 1)
                        t = tok[:, b % 2]
                        for c, dst in ((0, n_cmp_p), (1, n_sel_p)):
                            act.dma_start(dst[0, 0, b * P:(b + 1) * P].rearrange("t a h d -> t (a h d)"),
                                          t[:, c * 256:(c + 1) * 256]).then_inc(rows_out[b % 2], 16)
                        if b >= NB - WB:
                            w0 = (b - (NB - WB)) * P
                            act.dma_start(n_win_p[0, 0, w0:w0 + P].rearrange("t a h d -> t (a h d)"),
                                          t[:, 512:768]).then_inc(rows_out[b % 2], 16)
                        act.activation(v_hi[:, :, b], t.rearrange("p (a s c) -> p a s c", a=3, s=2)[:, 1:3, 1],
                                       ACT.Copy).then_inc(vhi_ready, 1)
                    act.wait_ge(tp_taken, E_NEW + 1)
                    for c, dst in ((0, n_cmp_s), (1, n_sel_s)):
                        act.dma_start(dst[0, :, 0].rearrange("n a h d -> n (a h d)"), tok[0:NS, 0, c * 256:(c + 1) * 256]).then_inc(small_out, 16)
                    act.dma_start(n_win_s[0, :, PAST - 1].rearrange("n a h d -> n (a h d)"), tok[0:NS, 0, 512:768]).then_inc(small_out, 16)
                    act.dma_start(n_win_s[0, :, 0:PAST - 1].rearrange("n t a h d -> n (t a h d)"),
                                  state_win_kv[0, :, 1:PAST].rearrange("n t a h d -> n (t a h d)")).then_inc(small_out, 16)
                    act.dma_start(n_pool_s[0, :, 0:HIST - 1], state_pool[0, :, 1:HIST]).then_inc(small_out, 16)
                    act.wait_ge(tp_taken, E_U + 1)
                    act.dma_start(n_pool_p[0, 0], utok[:]).then_inc(small_out, 16)
                    act.wait_ge(tp_taken, E_UNEW + 1)
                    act.dma_start(n_pool_s[0, :, HIST - 1], tok[0:NS, 1, 0:PW]).then_inc(small_out, 16)
                    for q in range(RWC, 2 * NWC):
                        load_wc(act, 0, q)
                    act.wait_ge(kc_ready, 1)
                    act.activation(kc_hi[:], kcT[:, 0, 0:NCB], ACT.Copy).then_inc(kchi_ready, 1)
                    act.wait_ge(tp_done, E_VC + 1)
                    act.activation(vc_hi[:], tp[E_VC % 2][0:NCB, 0:P], ACT.Copy).then_inc(vchi_ready, 1)
                    act.wait_ge(rows_out[0], 16 * (2 * 4 + 2))
                    act.wait_ge(rows_out[1], 16 * (2 * 4 + 2))

                @block.tensor
                def _(pe):
                    def slot(e):
                        if e >= 2:
                            pe.wait_ge(tp_taken, e - 1)
                        return tp[e % 2]

                    t = slot(E_POS)
                    pe.wait_ge(pos_loaded, 32)
                    for s in range(2):
                        last = pe.transpose(t[:, s * BLOCK:(s + 1) * BLOCK], posd[:, s].rearrange("j h d -> j (h d)"), ident[0:BLOCK, 0:BLOCK])
                    last.then_inc(tp_done, 1)
                    t = slot(E_GATE)
                    pe.wait_ge(gates_ready, 1)
                    for b in range(NB):
                        pe.transpose(t[:, b * 24:(b + 1) * 24], gT[:, b * P:(b + 1) * P], ident[0:24, 0:24])
                    pe.transpose(t[0:NS, NB * 24:(NB + 1) * 24], gT[:, TP:T], ident[0:24, 0:24]).then_inc(tp_done, 1)
                    sources = [catT[:, 0], catT[:, 1], kvT[:, 0], kvT[:, 1], kvT[:, 2], kvT[:, 3]]
                    for b in range(NB):
                        t = slot(E_TOK[b])
                        for n, x in enumerate(sources):
                            last = pe.transpose(t[:, n * P:(n + 1) * P], x[:, b * P:(b + 1) * P], ident[:])
                        last.then_inc(tp_done, 1)
                        n = b
                        t = slot(E_CK[n])
                        pe.wait_ge(ck_loaded[n % 2], 16 * NPG * (n // 2 + 1))
                        for s in range(2):
                            for g in range(NPG):
                                last = pe.transpose(t[:, (s * NPG + g) * P:(s * NPG + g + 1) * P], ck[:, n % 2, g, s * P:(s + 1) * P], ident[:])
                        last.then_inc(tp_done, 1)
                    t = slot(E_NEW)
                    for n in range(6):
                        x = cnewT[:, n] if n < 2 else kvT[:, n - 2, TP:T]
                        last = pe.transpose(t[0:NS, n * P:(n + 1) * P], x, ident[:])
                    last.then_inc(tp_done, 1)
                    t = slot(E_U)
                    for n in range(4):
                        last = pe.transpose(t[0:HIST, n * P:(n + 1) * P], uT[:, n, TP - HIST:TP], ident[:])
                    last.then_inc(tp_done, 1)
                    t = slot(E_UNEW)
                    for n in range(4):
                        last = pe.transpose(t[0:NS, n * P:(n + 1) * P], uT[:, n, TP:T], ident[:])
                    last.then_inc(tp_done, 1)
                    pe.wait_ge(tp_taken, E_VC)
                    for q in range(2 * NWC):
                        s, c = divmod(q, NWC)
                        pe.wait_ge(wc_loaded[q % RWC], 32 * (q // RWC + 1))
                        rows = catT[:, s].rearrange("p (b j) -> p j b", j=BLOCK)
                        for jj in range(JC):
                            j = c * JC + jj
                            last = pe.matmul(cps[:, s], rows[:, j], wc[:, q % RWC, jj], start=(j == 0), stop=(j == BLOCK - 1))
                        last.then_inc(wc_used, 1)
                    pe.wait_ge(crows_ready, 1)
                    for s in range(2):
                        last = pe.transpose(tp[(E_VC + 1) % 2][:, s * 64:s * 64 + NCAT], crows[:, s], ident[0:NCAT, 0:NCAT])
                    last.then_inc(crows_turned, 1)
                    t = slot(E_VC)
                    pe.wait_ge(kc_ready, 1)
                    pe.transpose(t[0:NCB, 0:P], kcT[:, 1, 0:NCB], ident[:])
                    pe.transpose(t[0:NS * NDB, P:2 * P], kcT[:, 1, NCB:NCAT - 1], ident[:]).then_inc(tp_done, 1)

                @block.vector
                def _(dve):
                    chain = Chain(dve, dchain)
                    for e in range(E_VC):
                        dve.wait_ge(tp_done, e + 1)
                        t = tp[e % 2]
                        if e == E_POS:
                            last = dve.tensor_copy(catT[:, :, (NCAT - 1) * BLOCK:], t[:, 0:2 * BLOCK].rearrange("p (s j) -> p s j", s=2))
                        elif e == E_GATE:
                            dve.tensor_copy(gtok[:], t[:, 0:NB * 24].rearrange("p (b c) -> p b c", b=NB))
                            last = dve.tensor_copy(gdec8[:], t[0:NS, NB * 24:(NB + 1) * 24])
                        elif e in E_TOK:
                            b = E_TOK.index(e)
                            if b >= 2:
                                dve.wait_ge(vlo_ready, b - 1)
                                dve.wait_ge(rows_out[b % 2], 16 * (2 * (b // 2) + max(0, b // 2 - 2)))
                            last = dve.tensor_copy(tok[:, b % 2], t[:, 0:6 * P])
                        elif e == E_NEW:
                            dve.wait_ge(vlo_ready, NB)
                            dve.wait_ge(rows_out[0], 16 * 10)
                            chain.then_wait(dve.tensor_copy(tok[0:NS, 0], t[0:NS, 0:6 * P]))
                            last = dve.tensor_copy(v_new[:], tok[0:NS, 0].rearrange("p (a s c) -> p a s c", a=3, s=2)[:, 1:3, 1])
                        elif e == E_U:
                            last = dve.tensor_copy(utok[:], t[0:HIST, 0:PW])
                        elif e == E_UNEW:
                            dve.wait_ge(rows_out[1], 16 * 10)
                            last = dve.tensor_copy(tok[0:NS, 1, 0:PW], t[0:NS, 0:PW])
                        else:
                            c = TP + E_CK.index(e) * PAST
                            last = dve.tensor_copy(catT[:, :, c:c + PAST], t[:, 0:2 * PAST].rearrange("p (s c) -> p s c", s=2))
                        last.then_inc(tp_taken, 1)
                    dve.wait_ge(wc_used, 2 * NWC)
                    dve.tensor_copy(crows[:], cps[:]).then_inc(crows_ready, 1)
                    dve.wait_ge(crows_turned, 1)
                    chain.then_wait(dve.tensor_copy(kcT[:], tp[(E_VC + 1) % 2][:, 0:2 * 64].rearrange("p (s c) -> p s c", s=2)[:, :, 0:NCAT]))
                    for s in range(2):
                        last = dve.tensor_scalar(kcT[:, s, 0:NCAT - 1], kcT[:, s, 0:NCAT - 1], kcT[:, s, NCAT - 1:NCAT], None, ALU.add)
                    last.then_inc(kc_ready, 1)
                    dve.wait_ge(kchi_ready, 1)
                    dve.tensor_tensor(kc_lo[:], kcT[:, 0, 0:NCB], kc_hi[:].bitcast(F32), ALU.subtract)
                    dve.wait_ge(vchi_ready, 1)
                    dve.tensor_tensor(vc_lo[:], tp[E_VC % 2][0:NCB, 0:P], vc_hi[:].bitcast(F32), ALU.subtract)
                    dve.tensor_copy(vc_dec[:], tp[E_VC % 2][0:NS * NDB, P:2 * P]).then_inc(kclo_ready, 1)

        with ExitStack() as st:
            at = buf.slabs(3)
            wsum = at("wsum", [P, 2, TP])
            hist = at("hist", [NS * HIST, PW])
            ext = at("ext", [P, 4, NS, 16])
            dsum = at("dsum", [P, 4, NS])
            pooled = at("pooled", [P, 4, T])
            wp = at("wp", [P, 4, P])
            ph = psum(st, "ph", [P, 512])
            pp = [psum(st, f"pp{i}", [P, NCH, 512]) for i in range(2)]
            hist_loaded, wp_loaded, hT_done, pooled_ready, mixed_done = (sem(n) for n in ("hist_loaded", "wp_loaded", "hT_done", "pooled_ready", "mixed_done"))
            pchain, gd_loaded, mix_taken = sem("dve_chain2"), sem("gd_loaded"), sem("mix_taken")
            with nc.Block() as block:

                @block.sync
                def _(sp):
                    sp.dma_start(hist[:], state_pool[0].rearrange("n t c -> (n t) c")).then_inc(hist_loaded, 16)
                    sp.dma_start(wp[:], w_pool[0].rearrange("g c d -> c g d")).then_inc(wp_loaded, 16)
                    for n in range(NS):
                        sp.dma_start(gdec[n * HEADS:(n + 1) * HEADS, :], gdec8[n:n + 1, :]).then_inc(gd_loaded, 16)
                    sp.wait_ge(gd_loaded, 16 * NS)

                @block.tensor
                def _(pe):
                    pe.wait_ge(hist_loaded, 16)
                    n = NS * HIST
                    for g in range(4):
                        last = pe.transpose(ph[:, g * n:(g + 1) * n], hist[:, g * P:(g + 1) * P], ident[0:n, 0:n])
                    last.then_inc(hT_done, 1)
                    pe.wait_ge(wp_loaded, 16)
                    for g in range(4):
                        pe.wait_ge(pooled_ready, g + 1)
                        if g >= 2:
                            pe.wait_ge(mix_taken, g - 1)
                        for c in range(NCH):
                            last = pe.matmul(pp[g % 2][:, c, 0:CH], wp[:, g], pooled[:, g, c * CH:(c + 1) * CH], start=True, stop=True)
                        last.then_inc(mixed_done, 1)

                @block.scalar
                def _(act):
                    for g in range(4):
                        act.wait_ge(mixed_done, g + 1)
                        act.activation(by_chunk(uT[:, g]), pp[g % 2][:, :, 0:CH], ACT.Copy, scale=vecs[:, V_POOL + g:V_POOL + g + 1])\
                           .then_inc(mix_taken, 1)

                @block.vector
                def _(dve):
                    chain = Chain(dve, pchain)
                    for g in range(4):
                        win = 2 << g
                        src, n = uT[:, g, 0:TP], 1
                        for r in range(g + 1):
                            dst = wsum[:, r % 2]
                            dve.tensor_copy(dst[:, 0:n], src[:, 0:n])
                            chain.then_wait(dve.tensor_tensor(dst[:, n:TP], src[:, n:TP], src[:, 0:TP - n], ALU.add))
                            src, n = dst, 2 * n
                        chain.then_wait(dve.tensor_tensor(src[:, 0:16], src[:, 0:16], invcnt[:, g], ALU.mult))
                        dve.scalar_tensor_tensor(pooled[:, g, 0:16], uT[:, g, 0:16], -1.0, src[:, 0:16], ALU.mult, ALU.add)
                        dve.scalar_tensor_tensor(pooled[:, g, 16:TP], src[:, 16:TP], 1.0 / win, uT[:, g, 16:TP], ALU.mult, ALU.subtract)
                        if g == 0:
                            dve.wait_ge(hT_done, 1)
                            dve.tensor_copy(ext[:, :, :, 0:HIST], ph[:, 0:4 * NS * HIST].rearrange("p (g n t) -> p g n t", g=4, n=NS))
                            chain.then_wait(dve.tensor_copy(ext[:, :, :, HIST], uT[:, :, TP:T]))
                        chain.then_wait(dve.tensor_reduce(dsum[:, g], ext[:, g, :, 16 - win:16], AX.X, ALU.add))
                        dve.scalar_tensor_tensor(pooled[:, g, TP:T], dsum[:, g], 1.0 / win, uT[:, g, TP:T],
                                                 ALU.mult, ALU.subtract).then_inc(pooled_ready, 1)

        SEL, WIN, CMP = 0, TP, TP + WINDOW + P
        NKP = CMP + NCB
        NG = NB * KVH
        JOBS = 2 * GRP
        PAIRS = JOBS // 2
        LAG = 2

        def dve_heads(i):
            return 1 if i >= 6 else 0

        RING = LAG + 1
        groups = [divmod(n, KVH) for n in range(NG)]

        def key_blocks(i):
            first = max(0, i - WB)
            win = [(1, b, WIN + (b - first) * P, P) for b in range(first, i + 1)]
            sel = [(0, b, SEL + b * P, P) for b in range(i + 1)]
            return win + [(2, 0, CMP, NCB)] + sel

        blocks_before = [sum(len(key_blocks(i)) for i, _ in groups[:n]) for n in range(NG + 1)]
        blocks = [(n, z) for n, (i, _) in enumerate(groups) for z in range(len(key_blocks(i)))]
        NBL = len(blocks)
        ends = [b - 1 for b in blocks_before[1:]]

        def jobs_at(t):
            n, z = blocks[t]
            size = len(key_blocks(groups[n][0]))
            return [(n + 1, k) for k in range(JOBS) if k * (size - 2) // JOBS == z and n + 1 < NG]

        def sel_before(n):
            return sum(PAIRS // 2 for i, _ in groups[:n] if dve_heads(i))

        with ExitStack() as st:
            at = buf.slabs(3)
            prob = at("prob", [P, 2, GRP, NKP])
            q_hi = at("q_hi", [P, GRP, P], F32R)
            q_lo = at("q_lo", [P, GRP, P], F32R)
            p_hi = at("p_hi", [P, RING, GRP * P], F32R)
            buf.tail = behind_all
            p_lo = [at("p_lo0", [P, GRP * P], F32R)] + [buf.small(f"p_lo{r}", [P, GRP * P], F32R) for r in range(1, RING)]
            top = buf.const("top", [P, 2, GRP, 3])
            bias = buf.const("bias", [P, 2, GRP, 3])
            total = buf.const("total", [P, 2, GRP, 3])
            share = buf.const("share", [P, 2, GRP, 3])
            sps = [psum(st, f"scores{i}", [P, 1024]) for i in range(2)]
            pT = [psum(st, f"pT{i}", [P, 512]) for i in range(RING)]
            out = psum(st, "attn_out", [P, 512])
            qhi_ready, qlo_ready, scores_done, bias_ready, exp_done = (sem(n) for n in ("qhi_ready", "qlo_ready", "scores_done", "bias_ready", "exp_done"))
            share_ready, win_scaled, rest_scaled, sel_scaled, pT_done, phi_ready, plo_ready, pv_done, out_taken = (
                sem(n) for n in ("share_ready", "win_scaled", "rest_scaled", "sel_scaled", "pT_done", "phi_ready", "plo_ready", "pv_done", "out_taken"))
            achain = sem("dve_chain3")

            def rows_of(kv):
                return slice(kv * HD, (kv + 1) * HD)

            with nc.Block() as block:

                @block.tensor
                def _(pe):
                    def product(dst, rows, g, keys_hi, keys_lo, start, more):
                        for m, (a, b) in enumerate(((q_hi, keys_hi), (q_hi, keys_lo), (q_lo, keys_hi))):
                            last = pe.matmul(dst, a[rows, g], b, start=start and m == 0, stop=(m == 2 and not more),
                                             skip_group_check=True)
                        return last

                    def branch(ps, s, rows, g, k0, k1, masks):
                        for c in range(k0, k1, 512):
                            e = min(c + 512, k1)
                            inside = [(at, m) for at, m in masks if c <= at < e]
                            last = product(ps[:, c - k0:e - k0], rows, g, kT_hi[rows, s, c:e], kT_lo[rows, s, c:e], True, bool(inside))
                            for z, (at_key, m) in enumerate(inside):
                                last = pe.matmul(ps[:, at_key - k0:at_key - k0 + P], identb[:], m[:], start=False,
                                                 stop=(z == len(inside) - 1), skip_group_check=True)
                        return last

                    def scores(n, k):
                        i, kv = groups[n]
                        rows, g, job = rows_of(kv), k % GRP, n * JOBS + k
                        ps = sps[job % 2]
                        if k == 0 and kv == 0:
                            pe.wait_ge(qlo_ready, i + 1)
                        if job >= 2:
                            pe.wait_ge(exp_done, job - 1)
                        if k >= GRP:
                            last = branch(ps, 0, rows, g, 0, (i + 1) * P, [(i * P, causal)])
                        else:
                            first = max(0, i - WB) * P
                            branch(ps, 1, rows, g, first, (i + 1) * P, [(i * P, causal)] + ([(first, behind)] if i >= WB else []))
                            whole = i < WB
                            c0 = WINDOW + P
                            product(ps[:, c0:c0 + NCB], rows, g, kc_hi[rows, :], kc_lo[rows, :], whole, True)
                            last = pe.matmul(ps[:, c0:c0 + NCB], identb[:], cmask[:, i], start=False, stop=True,
                                             skip_group_check=True)
                        last.then_inc(scores_done, 1)

                    def turn(t):
                        n, z = blocks[t]
                        br, _, c, m = key_blocks(groups[n][0])[z]
                        if z == 0:
                            pe.wait_ge(win_scaled, (n + 1) * PAIRS // 2)
                        elif br == 0:
                            pe.wait_ge(rest_scaled, (n + 1) * PAIRS // 2)
                            if dve_heads(groups[n][0]):
                                pe.wait_ge(sel_scaled, sel_before(n + 1))
                        if t >= RING:
                            pe.wait_ge(plo_ready, t - RING + 1)
                        for g in range(GRP):
                            last = pe.transpose(pT[t % RING][0:m, g * P:(g + 1) * P], prob[:, n % 2, g, c:c + m], ident[:])
                        last.then_inc(pT_done, 1)

                    def values(t):
                        n, z = blocks[t]
                        br, b, _, m = key_blocks(groups[n][0])[z]
                        if z == 0 and n:
                            pe.wait_ge(out_taken, n)
                        pe.wait_ge(plo_ready, t + 1)
                        a_hi, a_lo = (vc_hi[:], vc_lo[:]) if br == 2 else (v_hi[:, br, b], v_lo[:, br, b])
                        hi, lo = p_hi[0:m, t % RING], p_lo[t % RING][0:m]
                        for x, (a, p) in enumerate(((a_hi, hi), (a_hi, lo), (a_lo, hi))):
                            last = pe.matmul(out[:], a, p, start=(z == 0 and x == 0),
                                             stop=(t + 1 == blocks_before[n + 1] and x == 2), skip_group_check=True)
                        last.then_inc(pv_done, 1)

                    for k in range(JOBS):
                        scores(0, k)
                    for t in range(NBL):
                        for n, k in jobs_at(t):
                            scores(n, k)
                        turn(t)
                        if t >= LAG:
                            values(t - LAG)
                    for t in range(NBL - LAG, NBL):
                        values(t)

                @block.scalar
                def _(act):
                    def exps(n, k):
                        i, _ = groups[n]
                        g, job = k % GRP, n * JOBS + k
                        ps = sps[job % 2]
                        if k == 0 and n >= 2:
                            act.wait_ge(pT_done, blocks_before[n - 1])
                        act.wait_ge(bias_ready, job + 1)
                        nw = (min(i, WB) + 1) * P
                        todo = [(2, 0, nw, WIN), (0, WINDOW + P, NCB, CMP)] if k < GRP else [(1, 0, (i + 1) * P, SEL)]
                        for which, c0, m, to in todo:
                            last = act.activation(prob[:, n % 2, g, to:to + m], ps[:, c0:c0 + m], ACT.Exp, scale=SCALE,
                                                  bias=bias[:, n % 2, g, which:which + 1],
                                                  accum_out=total[:, n % 2, g, which:which + 1])
                        last.then_inc(exp_done, 1)

                    def cut(t):
                        n, z = blocks[t]
                        m = key_blocks(groups[n][0])[z][3]
                        act.wait_ge(pT_done, t + 1)
                        if t >= RING:
                            act.wait_ge(pv_done, t - RING + 1)
                        act.activation(p_hi[0:m, t % RING], pT[t % RING][0:m, :], ACT.Copy).then_inc(phi_ready, 1)

                    def cut_q(i):
                        if i:
                            act.wait_ge(scores_done, JOBS * KVH * i)
                        act.activation(q_hi[:], qT[:, :, i * P:(i + 1) * P], ACT.Copy).then_inc(qhi_ready, 1)

                    def take(n):
                        i, kv = groups[n]
                        rows = rows_of(kv)
                        act.wait_ge(pv_done, blocks_before[n + 1])
                        act.activation(qT[rows, :, i * P:(i + 1) * P], out[rows].rearrange("p (g t) -> p g t", g=GRP),
                                       ACT.Copy).then_inc(out_taken, 1)

                    cut_q(0)
                    for k in range(JOBS):
                        exps(0, k)
                    for t in range(NBL):
                        jobs = jobs_at(t)
                        for n, k in jobs[:-1]:
                            exps(n, k)
                        cut(t)
                        if t - LAG in ends:
                            take(ends.index(t - LAG))
                        for n, k in jobs[-1:]:
                            exps(n, k)
                            if k == JOBS - 1 and n % KVH == KVH - 1 and n + 1 < NG:
                                cut_q((n + 1) // KVH)
                    take(NG - 1)

                @block.gpsimd
                def _(pool):
                    for n in range(NG):
                        i, _ = groups[n]
                        nw = (min(i, WB) + 1) * P
                        for pair in range(PAIRS):
                            pool.wait_ge(share_ready, n * PAIRS + pair + 1)
                            win = pair < PAIRS // 2
                            todo = [(2, WIN, nw), (0, CMP, NCB)] if win else [(1, SEL, (i + 1) * P)]
                            g0 = 2 * pair % GRP
                            for g in (g0, g0 + 1) if win else range(g0 + dve_heads(i), g0 + 2):
                                for which, c, m in todo:
                                    y = prob[:, n % 2, g, c:c + m]
                                    last = pool.tensor_scalar(y, y, share[:, n % 2, g, which:which + 1], None, ALU.mult)
                            last.then_inc(win_scaled if win else rest_scaled, 1)

                @block.vector
                def _(dve):
                    chain = Chain(dve, achain)

                    def maxima(n, k):
                        i, _ = groups[n]
                        g, job = k % GRP, n * JOBS + k
                        ps, tp_, bs = sps[job % 2], top[:, n % 2, g], bias[:, n % 2, g]
                        dve.wait_ge(scores_done, job + 1)
                        if k >= GRP:
                            chain.then_wait(dve.tensor_reduce(tp_[:, 1:2], ps[:, 0:(i + 1) * P], AX.X, ALU.max))
                            dve.tensor_scalar(bs[:, 1:2], tp_[:, 1:2], -SCALE, None, ALU.mult).then_inc(bias_ready, 1)
                        else:
                            dve.tensor_reduce(tp_[:, 2:3], ps[:, 0:(min(i, WB) + 1) * P], AX.X, ALU.max)
                            chain.then_wait(dve.tensor_reduce(tp_[:, 0:1], ps[:, WINDOW + P:WINDOW + P + NCB], AX.X, ALU.max))
                            dve.tensor_scalar(bs[:, 0:3:2], tp_[:, 0:3:2], MAX_FLOOR, -SCALE, ALU.max, ALU.mult).then_inc(bias_ready, 1)

                    def shares(n, pair):
                        i, kv = groups[n]
                        dve.wait_ge(exp_done, n * JOBS + 2 * pair + 2)
                        g0 = 2 * pair % GRP
                        g = slice(g0, g0 + 2)
                        which = slice(0, 3, 2) if pair < PAIRS // 2 else slice(1, 2)
                        x = share[:, n % 2, g, which]
                        gates = gtok[:, i].rearrange("p (k g b) -> p k g b", k=KVH, g=GRP)[:, kv, g, which]
                        chain.then_wait(dve.tensor_scalar(x, total[:, n % 2, g, which], 1e-30, None, ALU.max))
                        chain.then_wait(dve.reciprocal(x, x))
                        dve.tensor_tensor(x, x, gates, ALU.mult).then_inc(share_ready, 1)
                        if pair >= PAIRS // 2 and dve_heads(i):
                            dve.wait_ge(share_ready, n * PAIRS + pair + 1)
                            for h in range(g0, g0 + dve_heads(i)):
                                y = prob[:, n % 2, h, SEL:SEL + (i + 1) * P]
                                last = dve.tensor_scalar(y, y, share[:, n % 2, h, 1:2], None, ALU.mult)
                            last.then_inc(sel_scaled, 1)

                    def cut(t):
                        n, z = blocks[t]
                        m = key_blocks(groups[n][0])[z][3]
                        dve.wait_ge(phi_ready, t + 1)
                        dve.tensor_tensor(p_lo[t % RING][0:m], pT[t % RING][0:m, :], p_hi[0:m, t % RING].bitcast(F32), ALU.subtract)\
                           .then_inc(plo_ready, 1)

                    def cut_q(i):
                        dve.wait_ge(qhi_ready, i + 1)
                        dve.tensor_tensor(q_lo[:], qT[:, :, i * P:(i + 1) * P], q_hi[:].bitcast(F32), ALU.subtract).then_inc(qlo_ready, 1)

                    cut_q(0)
                    for k in range(JOBS):
                        maxima(0, k)
                        if k >= 3 and k % 2:
                            shares(0, k // 2 - 1)
                    shares(0, PAIRS - 1)
                    for t in range(NBL):
                        for n, k in jobs_at(t):
                            maxima(n, k)
                        cut(t)
                        for n, k in jobs_at(t - 1) if t else []:
                            if k % 2:
                                shares(n, k // 2)
                        for n, k in jobs_at(t):
                            if k == JOBS - 1 and n % KVH == KVH - 1 and n + 1 < NG:
                                cut_q((n + 1) // KVH)

        sem.recycle()
        gm = Gemm(w, None, sem, "merge")
        up_nsa = w_up_nsa[0].rearrange("(h g d) n -> h d g n", h=KVH, g=GRP)
        up_loaded = sem("up_loaded")

        GATE = (1, 2, 0)
        with ExitStack() as st:
            at = buf.slabs(3)
            cs = at("cs", [P, NS, NPG, 2 * P])
            cw = at("cw", [P, NS, NPG, 2 * P])
            keysT = at("keysT", [P, 2, NS, PAST])
            qz = at("qz", [P, NS * (R + HEADS)])
            qall = at("qall", [P, NS, HEADS])
            NKD = 2 * (PAST + NS) + NS * NDB
            NKS, NKW, NKC = 0, PAST + NS, 2 * (PAST + NS)
            pd = at("pd", [R, NKD])
            chunks = [(NKS, P), (NKS + P, P), (NKS + PAST, NS), (NKW, P), (NKW + P, P), (NKW + PAST, NS), (NKC, NS * NDB)]
            pdT = at("pdT", [P, len(chunks), R])
            dtop, dbias, dtotal, dshare = (at(n, [R, 3]) for n in ("dtop", "dbias", "dtotal", "dshare"))
            dps = psum(st, "dps", [P, 3, 512])
            tpd = [psum(st, f"tpd{i}", [P, 512]) for i in range(2)]
            ptp = psum(st, "ptp", [P, len(chunks), R])
            dout = psum(st, "dout", [P, R])
            cs_loaded, cw_loaded = [sem(f"cs_loaded{m}") for m in range(NS // 2)], [sem(f"cw_loaded{m}") for m in range(NS // 2)]
            qz_zeroed, qz_ready = sem("qz_zeroed"), sem("qz_ready")
            kt_done, kt_taken, dsc_done, dbias_ready, dexp_done = (sem(n) for n in ("kt_done", "kt_taken", "dsc_done", "dbias_ready", "dexp_done"))
            pd_ready, pdT_done, pdT_ready, dout_done, ddchain = (sem(n) for n in ("pd_ready", "pdT_done", "pdT_ready", "dout_done", "dve_chain4"))
            with nc.Block() as block:

                @block.sync
                def _(sp):
                    for n in range(NS):
                        for g in range(NPG):
                            page = sp.value_load(pt_sb[0:1, n * NPG + g:n * NPG + g + 1], min_val=0, max_val=NPHYS - 1)
                            sp.dma_start(cs[:, n, g], cache_sel_kv[0].rearrange("n s a h d -> n s (a h d)")[bass.ds(page, 1)]
                                         .rearrange("n s c -> (n s) c")).then_inc(cs_loaded[n // 2], 16)
                    gm.load(sp, columns(w_in[0], M_COL), 0, 0, first=True)
                    for h in range(KVH):
                        sp.dma_start(w.raw[h * HD:(h + 1) * HD, 1, 0:4], up_nsa[h, :, :, 0:P]).then_inc(up_loaded, 16)

                @block.gpsimd
                def _(pool):
                    pool.memset(qz[:], 0.0).then_inc(qz_zeroed, 1)
                    gm.cut_lo(pool, 0, 0)
                    gm.cut_lo(pool, 0, 1, k=4)

                @block.tensor
                def _(pe):
                    for br, (c, loaded) in enumerate(((cs, cs_loaded), (cw, cw_loaded))):
                        for m in range(NS // 2):
                            pe.wait_ge(loaded[m], 16 * 2 * (NPG if br == 0 else 1))
                            e = br * (NS // 2) + m
                            if e >= 2:
                                pe.wait_ge(kt_taken, e - 1)
                            for x in range(2 * NPG):
                                last = pe.transpose(tpd[e % 2][:, x * P:(x + 1) * P], c[:, 2 * m + x // NPG, x % NPG, 0:P], ident[:])
                            last.then_inc(kt_done, 1)
                    pe.wait_ge(kt_taken, NS)
                    pe.wait_ge(qz_ready, 1)
                    qa = qall[:].rearrange("p n h -> p (n h)")
                    for br in range(2):
                        ps = dps[0:R, br]
                        pe.matmul(ps[:, PAST:PAST + NS], qa, knew[:, br], start=True, stop=False, skip_group_check=True)
                        pe.matmul(ps[:, PAST:PAST + NS], identb[0:R, 0:R], dmask[:], start=False, stop=True, skip_group_check=True)
                        for n in range(NS):
                            pe.matmul(ps[:, 0:PAST], qz[:, n * R:(n + 1) * R], keysT[:, br, n], start=False, stop=(n == NS - 1),
                                      skip_group_check=True)
                    pe.matmul(dps[0:R, 2, 0:NS * NDB], qa, kcT[:, 0, NCB:NCAT - 1], start=True, stop=False)
                    pe.matmul(dps[0:R, 2, 0:NS * NDB], identb[0:R, 0:R], dcmask[:].rearrange("p n b -> p (n b)"),
                              start=False, stop=True).then_inc(dsc_done, 1)
                    pe.wait_ge(pd_ready, 1)
                    for x, (c, m) in enumerate(chunks):
                        last = pe.transpose(ptp[0:m, x], pd[:, c:c + m], ident[0:R, 0:R])
                    last.then_inc(pdT_done, 1)
                    pe.wait_ge(pdT_ready, 1)
                    pe.matmul(dout[:], vc_dec[:], pdT[0:NS * NDB, 6], start=True, stop=False, skip_group_check=True)
                    for br, (c, x) in enumerate(((cs, 0), (cw, 3))):
                        pe.matmul(dout[:], v_new[:, br], pdT[0:NS, x + 2], start=False, stop=False, skip_group_check=True)
                        for n in range(NS):
                            own = slice(n * HEADS, (n + 1) * HEADS)
                            for g in range(NPG):
                                last = pe.matmul(dout[:, own], c[:, n, g, P:2 * P], pdT[:, x + g, own], start=False,
                                                 stop=(br == 1 and g == NPG - 1), skip_group_check=True)
                    last.then_inc(dout_done, 1)

                @block.scalar
                def _(act):
                    for n in range(NS):
                        act.dma_start(cw[:, n], state_win_kv[0, n].rearrange("(g s) a h d -> s g (a h d)", g=NPG)).then_inc(cw_loaded[n // 2], 16)
                    gm.cut_hi(act, 0, 0, first=True)
                    act.wait_ge(up_loaded, 32)
                    act.activation(w.hi[:, 1, 0:4], w.raw[:, 1, 0:4], ACT.Copy).then_inc(gm.hi_ready, 1)
                    act.wait_ge(dbias_ready, 1)
                    for br, (c, m) in enumerate(((NKS, PAST + NS), (NKW, PAST + NS), (NKC, NS * NDB))):
                        last = act.activation(pd[:, c:c + m], dps[0:R, br, 0:m], ACT.Exp, scale=SCALE, bias=dbias[:, br:br + 1],
                                              accum_out=dtotal[:, GATE[br]:GATE[br] + 1])
                    last.then_inc(dexp_done, 1)

                @block.vector
                def _(dve):
                    chain = Chain(dve, ddchain)
                    dve.wait_ge(qz_zeroed, 1)
                    qzn = qz[:].rearrange("p (n c) -> p n c", c=R + HEADS)
                    for kv in range(KVH):
                        rows = slice(kv * HD, (kv + 1) * HD)
                        heads = slice(kv * GRP, (kv + 1) * GRP)
                        chain.then_wait(dve.tensor_copy(qzn[rows, :, heads], qT[rows, :, TP:T].rearrange("p g n -> p n g")))
                    dve.tensor_copy(qall[:], qzn[:, :, 0:HEADS]).then_inc(qz_ready, 1)
                    for e in range(NS):
                        dve.wait_ge(kt_done, e + 1)
                        br, m = divmod(e, NS // 2)
                        dve.tensor_copy(keysT[:, br, 2 * m:2 * m + 2], tpd[e % 2][:].rearrange("p (n k) -> p n k", n=2)).then_inc(kt_taken, 1)
                    dve.wait_ge(dsc_done, 1)
                    dve.tensor_reduce(dtop[:, 0:2], dps[0:R, 0:2, 0:PAST + NS], AX.X, ALU.max)
                    chain.then_wait(dve.tensor_reduce(dtop[:, 2:3], dps[0:R, 2, 0:NS * NDB], AX.X, ALU.max))
                    dve.tensor_scalar(dbias[:], dtop[:], -SCALE, None, ALU.mult).then_inc(dbias_ready, 1)
                    dve.wait_ge(dexp_done, 1)
                    chain.then_wait(dve.reciprocal(dshare[:], dtotal[:]))
                    chain.then_wait(dve.tensor_tensor(dshare[:], dshare[:], gdec[:], ALU.mult))
                    for br, (c, m) in enumerate(((NKS, PAST + NS), (NKW, PAST + NS), (NKC, NS * NDB))):
                        last = dve.tensor_scalar(pd[:, c:c + m], pd[:, c:c + m], dshare[:, GATE[br]:GATE[br] + 1], None, ALU.mult)
                    last.then_inc(pd_ready, 1)
                    dve.wait_ge(pdT_done, 1)
                    for x, (c, m) in enumerate(chunks):
                        last = dve.tensor_copy(pdT[0:m, x], ptp[0:m, x])
                    last.then_inc(pdT_ready, 1)
                    dve.wait_ge(dout_done, 1)
                    for kv in range(KVH):
                        rows = slice(kv * HD, (kv + 1) * HD)
                        dve.tensor_copy(qT[rows, :, TP:T].rearrange("p g n -> p n g"),
                                        dout[rows].rearrange("p (n h) -> p n h", n=NS)[:, :, kv * GRP:(kv + 1) * GRP])

        at = buf.slabs(2)
        b_hi = [at("o_hi", [P, 4, T], F32R), at("pool_hi", [P, 4, T], F32R)]
        at = buf.slabs(3)
        b_lo = [at("o_lo", [P, 4, T], F32R), at("pool_lo", [P, 4, T], F32R)]
        halves = [(x[:, k], hi[:, k], lo[:, k]) for x, hi, lo in zip((qT, uT), b_hi, b_lo) for k in range(4)]
        cut_tmp = buf.slabs(4, 4 * T * 4)("cut_tmp", [P, 4, T], F32R)
        tmp_ready, lo_cut, halves_ready = sem("mix_tmp_ready"), sem("mix_lo_cut"), sem("mix_halves_ready")

        mT = buf.slabs(4)("mT", [P, KD, T])
        go = Gemm(w, None, sem, "wo")
        with ExitStack() as st:
            accs = [psum(st, f"merge_acc{s}", [P, NCH, 512]) for s in range(2)]
            g = gm
            g.accs = accs
            sig = buf.slabs(5, 3 * 8192)("sig", [P, T])
            prod = buf.slabs(6)("prod", [P, T])
            m_chain = sem("m_chain")
            with nc.Block() as block:

                @block.sync
                def _(sp):
                    def tile(t, first=False):
                        at_a, at_b, at_up = ((sp.snap(t * P + c) if not first else c) for c in (M_COL, M_COL + D, 0))
                        if not first:
                            g.load(sp, columns(w_in[0], at_a), t * 2, 0)
                            sp.wait_ge(g.lo_ready, t * 4)
                            for h in reversed(range(KVH)):
                                sp.dma_start(w.raw[h * HD:(h + 1) * HD, 1, 0:4], up_nsa[h, :, :, bass.ds(at_up, P)]).then_inc(up_loaded, 16)
                        g.load(sp, columns(w_in[0], at_b), t * 2 + 1, 0)
                        sp.wait_ge(g.lo_ready, t * 4 + 2)
                        sp.dma_start(w.raw[:, 1, 0:4], columns(w_up_pool[0], at_up)).then_inc(g.loaded[1], 16)

                    tile(0, first=True)
                    with sp.Fori(1, KD) as t:
                        tile(t)
                    for s in range(2):
                        sp.wait_ge(g.lo_ready, 4 * KD - 1 + s)
                        go.load(sp, columns(w_o[0], s * P), 0, s, first=True)

                @block.scalar
                def _(act):
                    def gate(t, s):
                        act.wait_ge(g.done, t * 4 + (2 * s + 1))
                        act.wait_ge(g.freed[1], t * 2 + s) if not isinstance(t, int) or 2 * t + s > 0 else None
                        act.activation(by_chunk(sig[:]), g.out(0), ACT.Sigmoid).then_inc(g.freed[0], 1)

                    def cut(t, x):
                        if x == 1:
                            act.wait_ge(up_loaded, t * 32 + 32)
                            act.wait_ge(g.done, t * 4)
                            act.activation(w.hi[:, 1, 0:4], w.raw[:, 1, 0:4], ACT.Copy).then_inc(g.hi_ready, 1)
                        elif x == 3:
                            act.wait_ge(g.loaded[1], t * 16 + 16)
                            act.wait_ge(g.done, t * 4 + 2)
                            act.activation(w.hi[:, 1, 0:4], w.raw[:, 1, 0:4], ACT.Copy).then_inc(g.hi_ready, 1)
                        else:
                            g.cut_hi(act, t * 2 + x // 2, 0)

                    def tile(t, more=True):
                        gate(t, 0)
                        cut(t, 2)
                        cut(t, 3)
                        gate(t, 1)
                        if more:
                            cut(t + 1, 0)
                            cut(t + 1, 1)

                    def halve(first):
                        for n in range(first, first + 4):
                            if n >= 4:
                                act.wait_ge(lo_cut, n - 3)
                            act.activation(cut_tmp[:, n % 4], halves[n][0], ACT.Copy).then_inc(tmp_ready, 1)
                        for n in range(first, first + 4):
                            act.wait_ge(lo_cut, n + 1)
                            act.activation(halves[n][1], halves[n][0], ACT.Copy).then_inc(halves_ready, 1)

                    halve(0)
                    gate(0, 0)
                    cut(0, 2)
                    halve(4)
                    cut(0, 3)
                    gate(0, 1)
                    cut(1, 0)
                    cut(1, 1)
                    with act.Fori(1, KD - 1) as t:
                        tile(t)
                    tile(KD - 1, more=False)

                @block.gpsimd
                def _(pool):
                    g.cut_lo(pool, 1, 0)
                    g.cut_lo(pool, 1, 1, k=4)
                    with pool.Fori(1, KD) as t:
                        for j in range(2):
                            g.cut_lo(pool, t * 2 + j, 0)
                            g.cut_lo(pool, t * 2 + j, 1, k=4)

                @block.tensor
                def _(pe):
                    def tile(t, first=False):
                        def part(n):
                            return (lambda k: pe.wait_ge(halves_ready, n + k + 1)) if first else None

                        g.multiply(pe, t * 2, 0, h_hi, h_lo, first=first)
                        g.multiply(pe, t * 2, 1, b_hi[0], b_lo[0], first=first, k=4, before=part(0))
                        g.multiply(pe, t * 2 + 1, 0, h_hi, h_lo)
                        g.multiply(pe, t * 2 + 1, 1, b_hi[1], b_lo[1], k=4, before=part(4))

                    tile(0, first=True)
                    with pe.Fori(1, KD) as t:
                        tile(t)

                @block.vector
                def _(dve):
                    for n, (x, _, lo) in enumerate(halves):
                        dve.wait_ge(tmp_ready, n + 1)
                        dve.tensor_tensor(lo, x, cut_tmp[:, n % 4].bitcast(F32), ALU.subtract).then_inc(lo_cut, 1)
                    with dve.Fori(0, KD) as t:
                        m = mT[:, bass.ds(t, 1)].rearrange("p o t -> p (o t)")
                        dve.wait_ge(g.done, t * 4 + 2)
                        dve.wait_ge(g.freed[0], t * 2 + 1)
                        dve.tensor_tensor(by_chunk(m), g.out(1), by_chunk(sig[:]), ALU.mult).then_inc(g.freed[1], 1)
                        dve.wait_ge(g.done, t * 4 + 4)
                        dve.wait_ge(g.freed[0], t * 2 + 2)
                        dve.tensor_tensor(by_chunk(prod[:]), g.out(1), by_chunk(sig[:]), ALU.mult).then_inc(g.freed[1], 1)
                        dve.wait_ge(g.freed[1], t * 2 + 2)
                        dve.tensor_tensor(m, m, prod[:], ALU.add).then_inc(m_chain, 1)
                        dve.wait_ge(m_chain, t + 1)

        m_hi = buf.slabs(0)("m_hi", [P, KD, T], F32R)
        m_lo = buf.slabs(1)("m_lo", [P, KD, T], F32R)
        moT = buf.slabs(2)("moT", [P, KD, T])
        xT = buf.slabs(3)("xT", [P, KD, T])
        xt2 = buf.slabs(4)("xt2", [P, NB, D])
        at = buf.slabs(4)
        rstd, mean, ntmp = (at(n, [P, T]) for n in ("rstd", "mean", "ntmp"))
        term = at("term", [P, 4, T])
        at = buf.slabs(5, 3 * 8192)
        sqr = at("sqr", [P, 2, T])
        sqsum = at("sqsum", [P, T])
        with ExitStack() as st:
            accs = [psum(st, f"wo_acc{s}", [P, NCH, 512]) for s in range(2)]
            tp = [psum(st, f"x_tp{i}", [P, 512]) for i in range(2)]
            g = go
            g.accs = accs
            pairs = KD // 2
            mhi_ready, mlo_ready, squared, sq_added, summed = (sem(n) for n in ("mhi_ready", "mlo_ready", "n1_squared", "n1_added", "n1_summed"))
            x2_loaded, xs2_loaded, xT_done, xT_taken = sem("x2_loaded"), sem("xs2_loaded"), sem("xT_done1"), sem("xT_taken1")
            mean_ready, root_ready, nchain, pchain = sem("n1_mean"), sem("n1_root"), sem("n1_chain"), sem("n1_pool_chain")
            with nc.Block() as block:

                @block.sync
                def _(sp):
                    with sp.Fori(1, pairs) as j:
                        for s in range(2):
                            g.load(sp, columns(w_o[0], (2 * j + s) * P), j, s)
                    sp.wait_ge(mlo_ready, KD)
                    sp.dma_start(xt2[:], x_prompt[0].rearrange("(b p) d -> p b d", p=P)).then_inc(x2_loaded, 16)
                    sp.wait_ge(xT_done, KD)
                    sp.dma_start(xt2[0:NS, 0], x_sample[:, 0, :]).then_inc(xs2_loaded, 16)

                @block.scalar
                def _(act):
                    for s in range(2):
                        g.cut_hi(act, 0, s, first=True)
                    for k in range(KD):
                        act.activation(m_hi[:, k], mT[:, k], ACT.Copy).then_inc(mhi_ready, 1)

                    def square(j, s):
                        act.wait_ge(g.freed[s], j + 1)
                        if not isinstance(j, int) or j:
                            act.wait_ge(sq_added, j * 2 + (s - 1))
                        act.activation(sqr[:, s].unsqueeze(1), moT[:, bass.ds(j * 2 + s, 1)], ACT.Square).then_inc(squared, 1)

                    for s in range(2):
                        g.cut_hi(act, 1, s)
                        square(0, s)
                    with act.Fori(2, pairs) as j:
                        for s in range(2):
                            g.cut_hi(act, j, s)
                            square(j - 1, s)
                    for s in range(2):
                        square(pairs - 1, s)
                    act.wait_ge(mean_ready, 1)
                    act.activation(rstd[:], mean[:], ACT.Sqrt).then_inc(root_ready, 1)

                @block.gpsimd
                def _(pool):
                    chain = Chain(pool, pchain)
                    for s in range(2):
                        g.cut_lo(pool, 0, s)
                    chain.then_wait(pool.memset(sqsum[:], 0.0))

                    def add(j, s):
                        pool.wait_ge(squared, j * 2 + (s + 1))
                        if s or not isinstance(j, int) or j:
                            pool.wait_ge(sq_added, j * 2 + s)
                        pool.tensor_tensor(sqsum[:], sqsum[:], sqr[:, s], ALU.add).then_inc(sq_added, 1)

                    for s in range(2):
                        g.cut_lo(pool, 1, s)
                        add(0, s)
                    with pool.Fori(2, pairs) as j:
                        for s in range(2):
                            g.cut_lo(pool, j, s)
                            add(j - 1, s)
                    for s in range(2):
                        add(pairs - 1, s)

                @block.tensor
                def _(pe):
                    g.multiply(pe, 0, 0, m_hi, m_lo, first=True, before=lambda k: pe.wait_ge(mlo_ready, k + 1))
                    g.multiply(pe, 0, 1, m_hi, m_lo, first=True)
                    with pe.Fori(1, pairs - 1) as j:
                        for s in range(2):
                            g.multiply(pe, j, s, m_hi, m_lo)
                    pe.wait_ge(x2_loaded, 16)
                    for e in range(2 * KD):
                        hf, k = divmod(e, KD)
                        if e >= 2:
                            pe.wait_ge(xT_taken, e - 1)
                        for b in range(4):
                            last = pe.transpose(tp[e % 2][:, b * P:(b + 1) * P], xt2[:, 4 * hf + b, k * P:(k + 1) * P], ident[:])
                        last.then_inc(xT_done, 1)
                    g.multiply(pe, pairs - 1, 0, m_hi, m_lo)
                    pe.wait_ge(xs2_loaded, 16)
                    pe.wait_ge(xT_taken, 2 * KD - 1)
                    for k in range(KD):
                        last = pe.transpose(tp[0][:, k * NS:(k + 1) * NS], xt2[0:NS, 0, k * P:(k + 1) * P], ident[0:NS, 0:NS])
                    last.then_inc(xT_done, 1)
                    g.multiply(pe, pairs - 1, 1, m_hi, m_lo)
                    pe.wait_ge(sq_added, KD)
                    for c in range(NCH):
                        last = pe.matmul(accs[0][:, c, 0:CH], ones[:], sqsum[:, c * CH:(c + 1) * CH], start=True, stop=True)
                    last.then_inc(summed, 1)

                @block.vector
                def _(dve):
                    chain = Chain(dve, nchain)
                    for k in range(KD):
                        dve.wait_ge(mhi_ready, k + 1)
                        dve.tensor_tensor(m_lo[:, k], mT[:, k], m_hi[:, k].bitcast(F32), ALU.subtract).then_inc(mlo_ready, 1)

                    def collect(j, s):
                        dve.wait_ge(g.done, j * 2 + (s + 1))
                        o = moT[:, bass.ds(j * 2 + s, 1)].rearrange("p o t -> p (o t)")
                        dve.tensor_copy(by_chunk(o), g.out(s)).then_inc(g.freed[s], 1)

                    with dve.Fori(0, pairs - 1) as j:
                        for s in range(2):
                            collect(j, s)
                    for e in range(2 * KD):
                        hf, k = divmod(e, KD)
                        dve.wait_ge(xT_done, e + 1)
                        dve.tensor_copy(xT[:, k, hf * 512:(hf + 1) * 512], tp[e % 2][:]).then_inc(xT_taken, 1)
                    collect(pairs - 1, 0)
                    dve.wait_ge(xT_done, 2 * KD + 1)
                    dve.tensor_copy(xT[:, :, TP:T], tp[0][:, 0:KD * NS].rearrange("p (k n) -> p k n", k=KD)).then_inc(xT_taken, 1)
                    collect(pairs - 1, 1)
                    finish_norm(dve, chain, accs[0], summed, 1, mean, mean_ready, rstd, root_ready, ntmp)

        gf = Gemm(w, None, sem, "ff")
        ff_load, ff_hi, ff_lo = gf.begin([columns(w_ff1[0], s * P) for s in range(2)])
        spilled = sem("spilled")
        with ExitStack() as st:
            acc = psum(st, "n2_ps", [P, NCH, 512])
            scaled, x1_ready, squared, summed, mean_ready, root_ready, nchain = (
                sem(f"n2_{n}") for n in ("scaled", "x1_ready", "squared", "summed", "mean", "root", "chain"))
            with nc.Block() as block:

                @block.sync
                def _(sp):
                    ff_load(sp)
                    sp.wait_ge(x1_ready, KD)
                    sp.dma_start(x1_spill, xT[:]).then_inc(spilled, 16)

                @block.gpsimd
                def _(pool):
                    for k in range(1, KD, 2):
                        if k >= 4:
                            pool.wait_ge(x1_ready, k - 3)
                        pool.tensor_tensor(term[:, k % 4], moT[:, k], rstd[:], ALU.mult).then_inc(scaled, 1)
                    ff_lo(pool)

                @block.scalar
                def _(act):
                    ff_hi(act)
                    for k in range(KD):
                        act.wait_ge(x1_ready, k + 1)
                        if k >= 2:
                            act.wait_ge(summed, k - 1)
                        act.activation(sqr[:, k % 2], xT[:, k], ACT.Square).then_inc(squared, 1)
                    act.wait_ge(mean_ready, 1)
                    act.activation(rstd[:], mean[:], ACT.Sqrt).then_inc(root_ready, 1)

                @block.tensor
                def _(pe):
                    for k in range(KD):
                        pe.wait_ge(squared, k + 1)
                        for c in range(NCH):
                            last = pe.matmul(acc[:, c, 0:CH], ones[:], sqr[:, k % 2, c * CH:(c + 1) * CH], start=(k == 0), stop=(k == KD - 1))
                        last.then_inc(summed, 1)

                @block.vector
                def _(dve):
                    chain = Chain(dve, nchain)
                    for k in range(KD):
                        t = term[:, k % 4]
                        if k % 2:
                            dve.wait_ge(scaled, k // 2 + 1)
                        else:
                            chain.then_wait(dve.tensor_tensor(t, moT[:, k], rstd[:], ALU.mult))
                        add_term(dve, chain, xT[:, k], t, gt1[:, k], 0, T).then_inc(x1_ready, 1)
                    finish_norm(dve, chain, acc, summed, KD, mean, mean_ready, rstd, root_ready, ntmp)

        h2_hi = buf.slabs(0)("h2_hi", [P, KD, T], F32R)
        h2_lo = buf.slabs(1)("h2_lo", [P, KD, T], F32R)
        h2_ready, h2hi_ready, h2lo_ready, h2_chain = (sem(n) for n in ("h2_ready", "h2hi_ready", "h2lo_ready", "h2_chain"))
        x1 = buf.slabs(0)("x1", [P, KD, T])
        f_hi = buf.slabs(2)("f_hi", [P, KD, T], F32R)
        f_lo = buf.slabs(3)("f_lo", [P, KD, T], F32R)
        fT = buf.slabs(4)("fT", [P, KD, T])
        with ExitStack() as st:
            accs = [psum(st, f"ff_acc{s}", [P, NCH, 512]) for s in range(2)]
            g = gf
            g.accs = accs
            at = buf.slabs(5, 3 * 8192)
            relu, f32, fsum = (at(n, [P, T]) for n in ("relu", "f32", "fsum"))
            fsq = (relu, f32)
            x1_loaded, fsquared, fsq_added, fs_chain = (sem(n) for n in ("x1_loaded", "f_squared", "f_sq_added", "fsum_chain"))
            f_ready, fhi_ready, flo_ready = (sem(n) for n in ("f_ready", "fhi_ready", "flo_ready"))
            HP = KD // 2
            with nc.Block() as block:

                @block.sync
                def _(sp):
                    def up(q, j, s, first=False):
                        g.load(sp, columns(w_ff1[0], (q * KD + 2 * j + s) * P), q * KD + j, s, first=first)

                    def down(q, j, s):
                        rows = w_ff2[0, bass.ds(q * D, D), :]
                        g.load(sp, columns(rows, (2 * j + s) * P), q * KD + HP + j, s)

                    with sp.Fori(1, HP) as j:
                        up(0, j, 0)
                        up(0, j, 1)
                    with sp.Fori(0, HP) as j:
                        down(0, j, 0)
                        down(0, j, 1)
                    with sp.Fori(1, NFG) as q:
                        with sp.Fori(0, HP) as j:
                            up(q, j, 0)
                            up(q, j, 1)
                        with sp.Fori(0, HP) as j:
                            down(q, j, 0)
                            down(q, j, 1)
                    sp.wait_ge(spilled, 16)
                    sp.wait_ge(g.done, (NFG - 1) * 2 * KD + KD)
                    sp.dma_start(x1[:], x1_spill).then_inc(x1_loaded, 16)

                @block.scalar
                def _(act):
                    def hidden(q, j, s):
                        n = q * KD + j * 2 + s
                        act.wait_ge(g.freed[s], q * KD + (j + 1))
                        if s or not isinstance(j, int) or not isinstance(q, int) or q or j:
                            act.wait_ge(flo_ready, n)
                        act.activation(f32[:], relu[:], ACT.Square).then_inc(f_ready, 1)
                        act.wait_ge(f_ready, n + 1)
                        act.activation(f_hi[:, bass.ds(j * 2 + s, 1)], f32[:].unsqueeze(1), ACT.Copy).then_inc(fhi_ready, 1)

                    def pair(q, j):
                        for s in range(2):
                            g.cut_hi(act, q * KD + j, s)

                    def square(j, s):
                        act.wait_ge(g.freed[s], (NFG - 1) * KD + HP + j + 1)
                        if not isinstance(j, int) or j:
                            act.wait_ge(fsq_added, j * 2 + (s - 1))
                        act.activation(fsq[s][:].unsqueeze(1), fT[:, bass.ds(j * 2 + s, 1)], ACT.Square).then_inc(fsquared, 1)

                    for k in range(KD):
                        act.wait_ge(h2_ready, k + 1)
                        act.activation(h2_hi[:, k], term[:, k % 2], ACT.Copy).then_inc(h2hi_ready, 1)
                    with act.Fori(1, HP) as j:
                        hidden(0, j - 1, 0)
                        g.cut_hi(act, j, 0)
                        hidden(0, j - 1, 1)
                        g.cut_hi(act, j, 1)
                    hidden(0, HP - 1, 0)
                    g.cut_hi(act, HP, 0)
                    hidden(0, HP - 1, 1)
                    g.cut_hi(act, HP, 1)
                    with act.Fori(1, HP) as j:
                        pair(0, j + HP)

                    def group(q):
                        pair(q, 0)
                        with act.Fori(1, HP) as j:
                            hidden(q, j - 1, 0)
                            g.cut_hi(act, q * KD + j, 0)
                            hidden(q, j - 1, 1)
                            g.cut_hi(act, q * KD + j, 1)
                        hidden(q, HP - 1, 0)
                        g.cut_hi(act, q * KD + HP, 0)
                        hidden(q, HP - 1, 1)
                        g.cut_hi(act, q * KD + HP, 1)

                    with act.Fori(1, NFG - 1) as q:
                        group(q)
                        with act.Fori(1, HP) as j:
                            pair(q, j + HP)
                    group(NFG - 1)
                    act.wait_ge(flo_ready, NFG * KD)
                    for j in range(1, HP):
                        for s in range(2):
                            g.cut_hi(act, (NFG - 1) * KD + HP + j, s)
                            square(j - 1, s)
                    for s in range(2):
                        square(HP - 1, s)

                @block.gpsimd
                def _(pool):
                    chain = Chain(pool, fs_chain)
                    for k in range(KD):
                        pool.wait_ge(h2hi_ready, k + 1)
                        pool.tensor_tensor(h2_lo[:, k], term[:, k % 2], h2_hi[:, k].bitcast(F32), ALU.subtract).then_inc(h2lo_ready, 1)
                    chain.then_wait(pool.memset(fsum[:], 0.0))
                    with pool.Fori(1, NFG * KD - HP + 1) as j:
                        g.cut_lo(pool, j, 0)
                        g.cut_lo(pool, j, 1)

                    def add(n):
                        pool.wait_ge(fsquared, n + 1)
                        if n:
                            pool.wait_ge(fsq_added, n)
                        pool.tensor_tensor(fsum[:], fsum[:], fsq[n % 2][:], ALU.add).then_inc(fsq_added, 1)

                    for n in range(2 * (HP - 1)):
                        g.cut_lo(pool, NFG * KD - HP + 1 + n // 2, n % 2)
                        add(n)
                    add(KD - 2)
                    add(KD - 1)

                @block.tensor
                def _(pe):
                    def up(q, j):
                        for s in range(2):
                            g.multiply(pe, q * KD + j, s, h2_hi, h2_lo)

                    def down(q, j, peel=False):
                        for s in range(2):
                            wait = (lambda: pe.wait_ge(flo_ready, q * KD + KD)) if peel and s == 0 else None
                            if peel and s == 0:
                                pe.wait_ge(flo_ready, q * KD + (KD - 1))
                            g.multiply(pe, q * KD + HP + j, s, f_hi, f_lo, before_last=wait)

                    g.multiply(pe, 0, 0, h2_hi, h2_lo, first=True, before=lambda k: pe.wait_ge(h2lo_ready, k + 1))
                    g.multiply(pe, 0, 1, h2_hi, h2_lo, first=True)
                    with pe.Fori(1, HP) as j:
                        up(0, j)
                    down(0, 0, peel=True)
                    with pe.Fori(1, HP) as j:
                        down(0, j)
                    with pe.Fori(1, NFG) as q:
                        with pe.Fori(0, HP) as j:
                            up(q, j)
                        down(q, 0, peel=True)
                        with pe.Fori(1, HP) as j:
                            down(q, j)

                @block.vector
                def _(dve):
                    chain = Chain(dve, h2_chain)
                    for k in range(KD):
                        t = term[:, k % 2]
                        if k >= 2:
                            dve.wait_ge(h2lo_ready, k - 1)
                        chain.then_wait(dve.tensor_tensor(t, xT[:, k], rstd[:], ALU.mult))
                        chain.then_wait(dve.tensor_tensor(t[:, TP:T], t[:, TP:T], sc2[:, k, 1:], ALU.mult))
                        dve.tensor_tensor(t[:, TP:T], t[:, TP:T], ada[:, 3 * KD + k, 1:], ALU.add)
                        dve.tensor_scalar(t[:, 0:TP], t[:, 0:TP], sc2[:, k, 0:1], ada[:, 3 * KD + k, 0:1], ALU.mult, ALU.add).then_inc(h2_ready, 1)
                    dve.wait_ge(h2lo_ready, KD)
                    dve.wait_ge(spilled, 16)

                    def hidden(q, j, s):
                        n = q * KD + j * 2 + s
                        dve.wait_ge(g.done, q * (2 * KD) + (j * 2 + s + 1))
                        dve.wait_ge(f_ready, n) if not (isinstance(n, int) and n == 0) else None
                        dve.tensor_scalar(by_chunk(relu[:]), g.out(s), 0.0, None, ALU.max).then_inc(g.freed[s], 1)
                        dve.wait_ge(fhi_ready, n + 1)
                        t = bass.ds(j * 2 + s, 1)
                        dve.tensor_tensor(f_lo[:, t], f32[:].unsqueeze(1), f_hi[:, t].bitcast(F32), ALU.subtract).then_inc(flo_ready, 1)

                    def collect(q, j, s):
                        dve.wait_ge(g.done, q * (2 * KD) + (j * 2 + (KD + s + 1)))
                        t = fT[:, bass.ds(j * 2 + s, 1)].rearrange("p o t -> p (o t)")
                        if isinstance(q, int):
                            dve.tensor_copy(by_chunk(t), g.out(s)).then_inc(g.freed[s], 1)
                            return
                        dve.tensor_tensor(by_chunk(t), g.out(s), by_chunk(t), ALU.add).then_inc(g.freed[s], 1)

                    for s in range(2):
                        hidden(0, 0, s)
                    with dve.Fori(1, HP) as j:
                        hidden(0, j, 0)
                        hidden(0, j, 1)
                    with dve.Fori(0, HP) as j:
                        collect(0, j, 0)
                        collect(0, j, 1)
                    with dve.Fori(1, NFG) as q:
                        with dve.Fori(0, HP) as j:
                            hidden(q, j, 0)
                            hidden(q, j, 1)
                        with dve.Fori(0, HP) as j:
                            collect(q, j, 0)
                            collect(q, j, 1)

        at = buf.slabs(1)
        rstd, mean, ntmp = (at(n, [P, T]) for n in ("rstd2", "mean2", "ntmp2"))
        term = at("term2", [P, 4, T])
        HALVES = ((0, TP // 2), (TP // 2, T))
        with ExitStack() as st:
            ytok = buf.slabs(3)("ytok", [P, 4, D])
            acc = psum(st, "n3_ps", [P, NCH, 512])
            tp = [psum(st, f"y_tp{i}", [P, D]) for i in range(2)]
            summed, mean_ready, root_ready, nchain = (sem(f"n3_{n}") for n in ("summed", "mean", "root", "chain"))
            scaled, y_ready, y_turned, y_taken = (sem(n) for n in ("y_scaled", "y_ready", "y_turned", "y_taken"))
            y_out = [sem(f"y_out{i}") for i in range(4)]
            with nc.Block() as block:

                @block.tensor
                def _(pe):
                    for c in range(NCH):
                        last = pe.matmul(acc[:, c, 0:CH], ones[:], fsum[:, c * CH:(c + 1) * CH], start=True, stop=True)
                    last.then_inc(summed, 1)
                    for b in range(NB + 1):
                        pe.wait_ge(y_ready, KD if b < NB // 2 else 2 * KD)
                        if b >= 2:
                            pe.wait_ge(y_taken, b - 1)
                        m = P if b < NB else NS
                        for k in range(KD):
                            last = pe.transpose(tp[b % 2][0:m, k * P:(k + 1) * P], x1[:, k, b * P:b * P + m], ident[:])
                        last.then_inc(y_turned, 1)

                @block.gpsimd
                def _(pool):
                    pool.wait_ge(nchain, NEWTON_STEPS)
                    for h, (c, e) in enumerate(HALVES):
                        for k in range(1, KD, 2):
                            n = h * KD + k
                            if n >= 4:
                                pool.wait_ge(y_ready, n - 3)
                            pool.tensor_tensor(term[:, k % 4, c:e], fT[:, k, c:e], rstd[:, c:e], ALU.mult).then_inc(scaled, 1)

                def take(eng, copy, b):
                    m = P if b < NB else NS
                    eng.wait_ge(y_turned, b + 1)
                    if b >= 4:
                        eng.wait_ge(y_out[b % 4], 16 * (b // 4))
                    if b:
                        eng.wait_ge(y_taken, b)
                    copy(ytok[0:m, b % 4], tp[b % 2][0:m]).then_inc(y_taken, 1)

                @block.scalar
                def _(act):
                    act.wait_ge(mean_ready, 1)
                    act.activation(rstd[:], mean[:], ACT.Sqrt).then_inc(root_ready, 1)
                    for b in (0, 1, 2, 3, 5, 7):
                        take(act, lambda o, i: act.activation(o, i, ACT.Copy), b)

                @block.vector
                def _(dve):
                    chain = Chain(dve, nchain)
                    finish_norm(dve, chain, acc, summed, 1, mean, mean_ready, rstd, root_ready, ntmp)
                    dve.wait_ge(x1_loaded, 16)
                    for h, (c, e) in enumerate(HALVES):
                        for k in range(KD):
                            t = term[:, k % 4]
                            if k % 2:
                                dve.wait_ge(scaled, h * KD // 2 + k // 2 + 1)
                            else:
                                chain.then_wait(dve.tensor_tensor(t[:, c:e], fT[:, k, c:e], rstd[:, c:e], ALU.mult))
                            add_term(dve, chain, x1[:, k], t, gt2[:, k], c, e).then_inc(y_ready, 1)
                    for b in (4, 6, 8):
                        take(dve, dve.tensor_copy, b)

                @block.sync
                def _(sp):
                    for b in range(NB + 1):
                        sp.wait_ge(y_taken, b + 1)
                        dst = y_prompt[0, b * P:(b + 1) * P, :] if b < NB else y_sample[:, 0, :]
                        sp.dma_start(dst, ytok[0:(P if b < NB else NS), b % 4]).then_inc(y_out[b % 4], 16)
                    for r in range(4):
                        sp.wait_ge(y_out[r], 16 * (3 if r == 0 else 2))


_INS = ["x_prompt", "x_sample", "cache_cmp_kv", "cache_sel_kv", "state_win_kv", "state_pool", "page_table",
        "c_prompt", "c_sample", "w_ada", "b_ada", "g_pre_mix", "g_post_mix", "g_pre_mlp", "g_post_mlp", "w_in",
        "w_cmp", "pos_cmp", "w_pool", "pool_scale", "w_up_nsa", "w_up_pool", "w_o", "w_ff1", "w_ff2"]
_OUTS = [((1, TP, D), "float32"), ((NS, 1, D), "float32"),
         ((1, 1, TP, 2, KVH, HD), "float32"), ((1, 1, TP, 2, KVH, HD), "float32"),
         ((1, 1, WINDOW, 2, KVH, HD), "float32"), ((1, 1, HIST, PW), "float32"),
         ((1, NS, 1, 2, KVH, HD), "float32"), ((1, NS, 1, 2, KVH, HD), "float32"),
         ((1, NS, PAST, 2, KVH, HD), "float32"), ((1, NS, HIST, PW), "float32")]


def kernel(**inputs):
    import numpy as _np
    import concourse.bacc as _bacc
    from concourse import mybir as _mybir
    from concourse.bass_utils import run_bass_kernel_spmd as _run

    nc = _bacc.Bacc("TRN2", target_bir_lowering=False, num_devices=1)
    arrays, args = {}, []
    for name in _INS:
        a = _np.ascontiguousarray(inputs[name])
        arrays[f"in_{name}_dram"] = a
        args.append(nc.dram_tensor(f"in_{name}_dram", a.shape, _mybir.dt.from_np(a.dtype), kind="ExternalInput").ap())
    for i, (shape, dtype) in enumerate(_OUTS):
        dt = _mybir.dt.from_np(_np.dtype(dtype))
        args.append(nc.dram_tensor(f"out_{i}_dram", shape, dt, kind="ExternalOutput").ap())
    hybrid_step(nc, *args)
    r = _run(nc, [arrays], core_ids=[0])
    return tuple(r.results[0][f"out_{i}_dram"] for i in range(len(_OUTS)))
```
